# Optimizing a Trainium2 kernel written in Bass

```python
import math
import jax, jax.numpy as jnp
from jax import lax
import numpy as np

D_MODEL = 1024
BATCH = 1
SEQ = 1024
DEPTH = 1

CHUNK = 64
HEAD_DIM = 64
PLE_DIM = 256
EPS = 1e-6

A_HEADS = 8
A_KV_HEADS = 2
A_GROUP = A_HEADS // A_KV_HEADS
A_WINDOW = 128
A_BAND_CHUNKS = A_WINDOW // CHUNK
A_WIDTH = A_HEADS * HEAD_DIM
A_QKV = (A_HEADS + 2 * A_KV_HEADS) * HEAD_DIM

B_HEADS = 16
B_HEAD_DIM = 64
B_WIDTH = B_HEADS * B_HEAD_DIM
B_GROUPS = 2
B_STATE = 128
B_CONV = 4
B_XBC = B_WIDTH + 2 * B_GROUPS * B_STATE
B_IN = B_WIDTH + B_XBC + B_HEADS

C_HEADS = 8
C_WIDTH = C_HEADS * HEAD_DIM
C_LEFT_CHUNKS = 8
C_BAND_CHUNKS = C_LEFT_CHUNKS + 1
C_REL_FUTURE = CHUNK - 1
C_REL_PAST = 256
C_REL_SIZE = C_REL_FUTURE + C_REL_PAST + 1
C_QKV = 3 * C_WIDTH

MIX_WIDTH = A_WIDTH + B_WIDTH + C_WIDTH
IN_WIDTH = A_QKV + B_IN + C_QKV

PEER_HEADS = 8
PEER_KEYS = 128
PEER_EXPERTS = PEER_KEYS * PEER_KEYS
PEER_KEY_DIM = 256
PEER_TOPK = 16
PEER_TOKEN_BLOCK = 128

kernel_name = "hybrid_stream_swa_ssd_chunkrel_peer"

def rmsnorm(x, g):
    xf = x.astype(jnp.float32)
    y = xf * lax.rsqrt(jnp.mean(xf * xf, axis=-1, keepdims=True) + EPS)
    return (y * g.astype(jnp.float32)).astype(x.dtype)

def alibi_slopes(n):
    return np.array([2.0 ** (-8.0 * (h + 1) / n) for h in range(n)], dtype=np.float32)

def band_gather(x, n_band):
    nc = x.shape[1]
    pad = [(0, 0), (n_band - 1, 0)] + [(0, 0)] * (x.ndim - 2)
    xp = jnp.pad(x, pad)
    return jnp.concatenate([xp[:, j:j + nc] for j in range(n_band)], axis=2)

def band_valid(nc, n_band):
    key_chunk = jnp.arange(nc)[:, None] - (n_band - 1) + jnp.arange(n_band * CHUNK)[None, :] // CHUNK
    return key_chunk >= 0

def band_distance(n_band):
    i = jnp.arange(CHUNK)[:, None]
    j = jnp.arange(n_band * CHUNK)[None, :]
    return i + (n_band - 1) * CHUNK - j

def chunk_band_attention(q, k, v, n_band, bias, sinks):
    nc = q.shape[1]
    kb = band_gather(k, n_band)
    vb = band_gather(v, n_band)
    scores = jnp.einsum("bcqkrd,bcskd->bckrqs", q, kb).astype(jnp.float32) * (HEAD_DIM ** -0.5) + bias
    valid = band_valid(nc, n_band)[None, :, None, None, None, :]
    scores = jnp.where(valid, scores, -jnp.inf)
    if sinks is None:
        probs = jax.nn.softmax(scores, axis=-1)
    else:
        sink = sinks.astype(jnp.float32)[None, None, :, :, None, None]
        m = jnp.maximum(jnp.max(scores, axis=-1, keepdims=True), sink)
        e = jnp.exp(scores - m)
        probs = e / (jnp.sum(e, axis=-1, keepdims=True) + jnp.exp(sink - m))
    return jnp.einsum("bckrqs,bcskd->bcqkrd", probs.astype(v.dtype), vb)

def mixer_a(qkv, q_gain, k_gain, sinks, out_gain):
    b, s, _ = qkv.shape
    nc = s // CHUNK
    q, k, v = jnp.split(qkv, [A_WIDTH, A_WIDTH + A_KV_HEADS * HEAD_DIM], axis=-1)
    q = rmsnorm(q.reshape(b, nc, CHUNK, A_KV_HEADS, A_GROUP, HEAD_DIM), q_gain)
    k = rmsnorm(k.reshape(b, nc, CHUNK, A_KV_HEADS, HEAD_DIM), k_gain)
    v = v.reshape(b, nc, CHUNK, A_KV_HEADS, HEAD_DIM)
    slopes = jnp.asarray(alibi_slopes(A_HEADS)).reshape(A_KV_HEADS, A_GROUP)
    dist = jnp.abs(band_distance(A_BAND_CHUNKS)).astype(jnp.float32)
    bias = -slopes[:, :, None, None] * dist[None, None]
    out = chunk_band_attention(q, k, v, A_BAND_CHUNKS, bias, sinks.reshape(A_KV_HEADS, A_GROUP))
    return rmsnorm(out.reshape(b, s, A_WIDTH), out_gain)

def causal_depthwise_conv(x, w, bias):
    c = x.shape[-1]
    y = lax.conv_general_dilated(x, w[:, None, :], window_strides=(1,), padding=[(B_CONV - 1, 0)],
                                 dimension_numbers=("NWC", "WIO", "NWC"), feature_group_count=c)
    return y + bias

def mixer_b(zxbcdt, conv_w, conv_b, dt_bias, a_log, d_skip, out_gain):
    b, s, _ = zxbcdt.shape
    nc = s // CHUNK
    z, xbc, dt = jnp.split(zxbcdt, [B_WIDTH, B_WIDTH + B_XBC], axis=-1)
    xbc = jax.nn.silu(causal_depthwise_conv(xbc, conv_w, conv_b))
    xs, bm, cm = jnp.split(xbc, [B_WIDTH, B_WIDTH + B_GROUPS * B_STATE], axis=-1)
    rep = B_HEADS // B_GROUPS
    x = xs.reshape(b, nc, CHUNK, B_HEADS, B_HEAD_DIM).astype(jnp.float32)
    bm = jnp.repeat(bm.reshape(b, nc, CHUNK, B_GROUPS, B_STATE), rep, axis=3).astype(jnp.float32)
    cm = jnp.repeat(cm.reshape(b, nc, CHUNK, B_GROUPS, B_STATE), rep, axis=3).astype(jnp.float32)
    dt = jax.nn.softplus(dt.astype(jnp.float32) + dt_bias.astype(jnp.float32)).reshape(b, nc, CHUNK, B_HEADS)
    a = -jnp.exp(a_log.astype(jnp.float32))
    da_cs = jnp.cumsum(dt * a, axis=2)
    xdt = x * dt[..., None]
    seg = da_cs[:, :, :, None, :] - da_cs[:, :, None, :, :]
    causal = jnp.tril(jnp.ones((CHUNK, CHUNK), dtype=bool))[None, None, :, :, None]
    decay = jnp.exp(jnp.where(causal, seg, -jnp.inf))
    cb = jnp.einsum("bclhn,bcshn->bclsh", cm, bm) * decay
    y_diag = jnp.einsum("bclsh,bcshp->bclhp", cb, xdt)
    decay_to_end = jnp.exp(da_cs[:, :, -1:, :] - da_cs)
    chunk_states = jnp.einsum("bclhn,bclhp->bchpn", bm * decay_to_end[..., None], xdt)
    chunk_decay = jnp.exp(da_cs[:, :, -1, :])

    def step(state, inp):
        st, dec = inp
        return dec[..., None, None] * state + st, state

    h0 = jnp.zeros((b, B_HEADS, B_HEAD_DIM, B_STATE), jnp.float32)
    _, prev = lax.scan(step, h0, (jnp.moveaxis(chunk_states, 1, 0), jnp.moveaxis(chunk_decay, 1, 0)))
    prev = jnp.moveaxis(prev, 0, 1)
    y_off = jnp.einsum("bclhn,bchpn->bclhp", cm * jnp.exp(da_cs)[..., None], prev)
    y = y_diag + y_off + x * d_skip.astype(jnp.float32)[:, None]
    y = y.reshape(b, s, B_WIDTH) * jax.nn.silu(z.astype(jnp.float32))
    return rmsnorm(y, out_gain).astype(zxbcdt.dtype)

def mixer_c(qkv, q_gain, k_gain, rel_bias, out_gain):
    b, s, _ = qkv.shape
    nc = s // CHUNK
    q, k, v = jnp.split(qkv, 3, axis=-1)
    q = rmsnorm(q.reshape(b, nc, CHUNK, C_HEADS, 1, HEAD_DIM), q_gain)
    k = rmsnorm(k.reshape(b, nc, CHUNK, C_HEADS, HEAD_DIM), k_gain)
    v = v.reshape(b, nc, CHUNK, C_HEADS, HEAD_DIM)
    rel = jnp.clip(band_distance(C_BAND_CHUNKS), -C_REL_FUTURE, C_REL_PAST) + C_REL_FUTURE
    bias = rel_bias.astype(jnp.float32)[:, rel][:, None]
    out = chunk_band_attention(q, k, v, C_BAND_CHUNKS, bias, None)
    return rmsnorm(out.reshape(b, s, C_WIDTH), out_gain)

def peer_ffn(u, w_query, sub_keys, expert_u, expert_v):
    b, s, d = u.shape
    q = (u @ w_query).reshape(b, s, PEER_HEADS, 2, PEER_KEY_DIM // 2)
    sc = jnp.einsum("bshtd,htkd->bshtk", q, sub_keys).astype(jnp.float32)
    top_s, top_i = lax.top_k(sc, PEER_TOPK)
    cand_s = top_s[..., 0, :, None] + top_s[..., 1, None, :]
    cand_i = top_i[..., 0, :, None] * PEER_KEYS + top_i[..., 1, None, :]
    cand_s = cand_s.reshape(b, s, PEER_HEADS, PEER_TOPK * PEER_TOPK)
    cand_i = cand_i.reshape(b, s, PEER_HEADS, PEER_TOPK * PEER_TOPK)
    best_s, best_pos = lax.top_k(cand_s, PEER_TOPK)
    best_i = jnp.take_along_axis(cand_i, best_pos, axis=-1)
    gates = jax.nn.softmax(best_s, axis=-1)
    n_blocks = (b * s) // PEER_TOKEN_BLOCK
    sel = PEER_HEADS * PEER_TOPK
    tokens = u.reshape(n_blocks, PEER_TOKEN_BLOCK, d)
    idx = best_i.reshape(n_blocks, PEER_TOKEN_BLOCK, sel)
    g = gates.reshape(n_blocks, PEER_TOKEN_BLOCK, sel).astype(u.dtype)

    def block(args):
        xt, it, gt = args
        ue = jnp.take(expert_u, it, axis=0)
        ve = jnp.take(expert_v, it, axis=0)
        act = jax.nn.gelu(jnp.einsum("td,ted->te", xt, ue), approximate=False) * gt
        return jnp.einsum("te,ted->td", act, ve)

    out = lax.map(block, (tokens, idx, g))
    return out.reshape(b, s, d)

def setup_inputs(seed: int = 0) -> dict:
    key = jax.random.key(seed)
    ks = jax.random.split(key, 32)
    f32 = jnp.float32

    def nrm(k, shape, scale):
        return jax.random.normal(k, shape, f32) * scale

    def gain(k, shape):
        return 1.0 + 0.05 * jax.random.normal(k, shape, f32)

    dt0 = jnp.exp(jax.random.uniform(ks[9], (DEPTH, B_HEADS), f32, minval=math.log(1e-3), maxval=math.log(1e-1)))
    return {
        "x": nrm(ks[0], (BATCH, SEQ, D_MODEL), 1.0),
        "p": nrm(ks[1], (DEPTH, BATCH, SEQ, PLE_DIM), 1.0),
        "mix_norm": gain(ks[2], (DEPTH, D_MODEL)),
        "w_in": nrm(ks[3], (DEPTH, D_MODEL, IN_WIDTH), D_MODEL ** -0.5),
        "a_q_norm": gain(ks[4], (DEPTH, HEAD_DIM)),
        "a_k_norm": gain(ks[5], (DEPTH, HEAD_DIM)),
        "a_sinks": nrm(ks[6], (DEPTH, A_HEADS), 0.5),
        "a_out_norm": gain(ks[7], (DEPTH, A_WIDTH)),
        "b_conv_w": nrm(ks[8], (DEPTH, B_CONV, B_XBC), B_CONV ** -0.5),
        "b_conv_b": nrm(ks[10], (DEPTH, B_XBC), 0.02),
        "b_dt_bias": dt0 + jnp.log(-jnp.expm1(-dt0)),
        "b_a_log": jnp.log(jax.random.uniform(ks[11], (DEPTH, B_HEADS), f32, minval=1.0, maxval=16.0)),
        "b_d": gain(ks[12], (DEPTH, B_HEADS)),
        "b_out_norm": gain(ks[13], (DEPTH, B_WIDTH)),
        "c_q_norm": gain(ks[14], (DEPTH, HEAD_DIM)),
        "c_k_norm": gain(ks[15], (DEPTH, HEAD_DIM)),
        "c_rel_bias": nrm(ks[16], (DEPTH, C_HEADS, C_REL_SIZE), 0.1),
        "c_out_norm": gain(ks[17], (DEPTH, C_WIDTH)),
        "w_out": nrm(ks[18], (DEPTH, MIX_WIDTH, D_MODEL), MIX_WIDTH ** -0.5),
        "ffn_norm": gain(ks[19], (DEPTH, D_MODEL)),
        "peer_w_query": nrm(ks[20], (DEPTH, D_MODEL, PEER_HEADS * PEER_KEY_DIM), D_MODEL ** -0.5),
        "peer_sub_keys": nrm(ks[21], (DEPTH, PEER_HEADS, 2, PEER_KEYS, PEER_KEY_DIM // 2), (PEER_KEY_DIM // 2) ** -0.5),
        "peer_u": nrm(ks[22], (DEPTH, PEER_EXPERTS, D_MODEL), D_MODEL ** -0.5),
        "peer_v": nrm(ks[23], (DEPTH, PEER_EXPERTS, D_MODEL), 0.5),
        "ple_norm": gain(ks[24], (DEPTH, D_MODEL)),
        "ple_w_gate": nrm(ks[25], (DEPTH, D_MODEL, D_MODEL), D_MODEL ** -0.5),
        "ple_w_proj": nrm(ks[26], (DEPTH, PLE_DIM, D_MODEL), PLE_DIM ** -0.5),
    }

def reference(x, p, mix_norm, w_in, a_q_norm, a_k_norm, a_sinks, a_out_norm,
              b_conv_w, b_conv_b, b_dt_bias, b_a_log, b_d, b_out_norm,
              c_q_norm, c_k_norm, c_rel_bias, c_out_norm, w_out,
              ffn_norm, peer_w_query, peer_sub_keys, peer_u, peer_v,
              ple_norm, ple_w_gate, ple_w_proj):
    h = x
    for i in range(DEPTH):
        u = rmsnorm(h, mix_norm[i])
        proj = u @ w_in[i]
        qkv_a, in_b, qkv_c = jnp.split(proj, [A_QKV, A_QKV + B_IN], axis=-1)
        y_a = mixer_a(qkv_a, a_q_norm[i], a_k_norm[i], a_sinks[i], a_out_norm[i])
        y_b = mixer_b(in_b, b_conv_w[i], b_conv_b[i], b_dt_bias[i], b_a_log[i], b_d[i], b_out_norm[i])
        y_c = mixer_c(qkv_c, c_q_norm[i], c_k_norm[i], c_rel_bias[i], c_out_norm[i])
        h = h + jnp.concatenate([y_a, y_b, y_c], axis=-1) @ w_out[i]
        h = h + peer_ffn(rmsnorm(h, ffn_norm[i]), peer_w_query[i], peer_sub_keys[i], peer_u[i], peer_v[i])
        gate = jax.nn.sigmoid(rmsnorm(h, ple_norm[i]) @ ple_w_gate[i])
        h = h + gate * (p[i] @ ple_w_proj[i])
    return h


_drawn_inputs = setup_inputs


def setup_inputs(seed=0):
    import zlib

    import numpy as np

    out = dict(_drawn_inputs(seed))
    spreads = {}
    factors = {'ple_norm': 8.0}
    for name, (base, spread) in spreads.items():
        noise = np.random.default_rng([zlib.crc32(name.encode()), seed]).standard_normal(out[name].shape)
        drawn = base * np.exp(spread * noise) if base else spread * noise
        out[name] = __import__('jax').numpy.asarray(drawn.astype(out[name].dtype))
    for name, factor in factors.items():
        out[name] = (out[name] * factor).astype(out[name].dtype)
    return out
```

```python
from contextlib import ExitStack

import numpy as np
import concourse.bass as bass
from concourse import mybir

F32 = mybir.dt.float32
U32 = mybir.dt.uint32
ALU = mybir.AluOpType
ACT = mybir.ActivationFunctionType
AX = mybir.AxisListType

P = 128
SEQ, D = 1024, 1024
TILES = SEQ // P
DCH = D // P
CHUNK, HD = 64, 64
EPS = 1e-6
NEG = -1e30
A_HEADS, A_KV = 8, 2
A_WIDTH, A_QKV = 512, 768
B_WIDTH, B_HEADS, B_GROUPS, B_STATE, B_CONV = 1024, 16, 2, 128, 4
B_XBC = B_WIDTH + 2 * B_GROUPS * B_STATE
B_IN = B_WIDTH + B_XBC + B_HEADS
C_HEADS, C_WIDTH = 8, 512
C_PASS = 4
REL_FUTURE, REL_PAST = 63, 256
REL_SIZE = REL_FUTURE + REL_PAST + 1
PLE = 256
PH, PK, PKD, TOPK = 8, 128, 256, 16
SEL = PH * TOPK


class Chain:

    def __init__(self, eng, sem, base=0):
        self.eng, self.sem, self.base, self.n = eng, sem, base, 0

    def link(self, ins):
        self.n += 1
        ins.then_inc(self.sem, 1)
        self.eng.wait_ge(self.sem, self.base + self.n)


class Core:

    def __init__(self, nc, ctx):
        self.nc = nc
        self.h = None
        self.ident = ctx.enter_context(nc.sbuf_tensor("ident", [P, P], F32))
        self.eps = ctx.enter_context(nc.sbuf_tensor("eps", [P, 1], F32))
        self.ps = ctx.enter_context(nc.psum_tensor("ps", [P, 8, 512], F32))


class Phase:

    def __init__(self, nc, ctx, tag):
        self.nc, self.ctx, self.tag, self.used = nc, ctx, tag, []

    def sb(self, name, shape, dt=F32):
        return self.ctx.enter_context(self.nc.sbuf_tensor(f"{self.tag}_{name}", shape, dt))

    def sem(self, name):
        self.used.append(self.ctx.enter_context(self.nc.semaphore(f"{self.tag}_{name}")))
        return self.used[-1]

    def open_block(self):
        self.ctx.callback(self.clear)
        return self.ctx.enter_context(self.nc.Block())

    def clear(self):
        numbers = sorted(s.num for s in self.used)
        starts = [n for n in numbers if n - 1 not in numbers]
        ends = [n + 1 for n in numbers if n + 1 not in numbers]
        for start, end in zip(starts, ends):
            self.nc.sync.sem_clear(range(start, end))
        self.nc.all_engine_barrier()

    def sems(self, names):
        return [self.sem(n) for n in names.split()]


def normalise_input(nc, core, uT, x, gain):
    with ExitStack() as ctx:
        ph = Phase(nc, ctx, "in")
        xn = ph.sb("xn", [P, 2, D])
        gT = ph.sb("gT", [P, DCH])
        rstd = ph.sb("rstd", [P, TILES])
        loaded, consts, squares, rooted, rstd_ready, xn_full, t_full, t_free = ph.sems(
            "loaded consts squares rooted rstd_ready xn_full t_full t_free")
        block = ph.open_block()
        h, ps, ident = core.h, core.ps, core.ident

        @block.sync
        def _(sp):
            for t in range(TILES):
                sp.dma_start(h[:, t, :], x[t * P:(t + 1) * P, :]).then_inc(loaded, 16)
            sp.dma_start(gT[:], gain.rearrange("(c p) -> p c", p=P), allow_slow_non_contiguous=True).then_inc(loaded, 16)
            sp.wait_ge(loaded, 16 * (TILES + 1))

        @block.gpsimd
        def _(pool):
            nc.gpsimd.memset(ident[:], 0.0).then_inc(consts, 1)
            nc.gpsimd.memset(core.eps[:], EPS).then_inc(consts, 1)
            pool.wait_ge(consts, 2)
            nc.gpsimd.affine_select(out=ident[:], in_=ident[:], compare_op=ALU.not_equal, fill=1.0, base=0,
                                    pattern=[[-1, P]], channel_multiplier=1).then_inc(consts, 1)

        @block.scalar
        def _(act):
            act.wait_ge(loaded, 16 * (TILES + 1))
            for t in range(TILES):
                nc.scalar.activation(uT[:, t, :], h[:, t, :], ACT.Square, accum_out=rstd[:, t:t + 1]).then_inc(squares, 1)
            act.wait_ge(squares, TILES)
            act.wait_ge(consts, 3)
            nc.scalar.activation(rstd[:], rstd[:], ACT.Sqrt, bias=core.eps[:, 0:1], scale=1.0 / D).then_inc(rooted, 1)

        @block.vector
        def _(dve):
            dve.sem_inc(t_free, 2)
            dve.wait_ge(rooted, 1)
            nc.vector.reciprocal(rstd[:], rstd[:]).then_inc(rstd_ready, 1)
            dve.wait_ge(rstd_ready, 1)
            dve.wait_ge(loaded, 16 * (TILES + 1))
            with dve.Fori(0, TILES // 2) as i:
                for b in range(2):
                    nc.vector.tensor_scalar(xn[:, b, :], h[:, bass.ds(i * 2 + b, 1), :].rearrange("p o d -> p (o d)"),
                                            rstd[:, bass.ds(i * 2 + b, 1)], None, ALU.mult).then_inc(xn_full, 1)
                for b in range(2):
                    dve.wait_ge(t_full, i * 2 + (b + 1))
                    nc.vector.tensor_tensor(
                        uT[:, :, bass.ds((i * 2 + b) * P, P)],
                        ps[:, 2 * b:2 * b + 2, :].rearrange("p k (c n) -> p (k c) n", n=P),
                        gT[:].unsqueeze(2).broadcast_to([P, DCH, P]), ALU.mult).then_inc(t_free, 1)

        @block.tensor
        def _(pe):
            pe.wait_ge(consts, 3)
            with pe.Fori(0, TILES // 2) as i:
                for b in range(2):
                    pe.wait_ge(xn_full, i * 2 + (b + 1))
                    pe.wait_ge(t_free, i * 2 + (b + 1))
                    transpose_row(nc, core, ps[:, 2 * b:2 * b + 2, :], xn[:, b, :], DCH).then_inc(t_full, 1)


def transpose_row(nc, core, out, src, n):
    flat = out.rearrange("p k (c n) -> p (k c) n", n=P)
    for c in range(n):
        last = nc.tensor.transpose(flat[:, c, :], src[:, c * P:(c + 1) * P], core.ident[:])
    return last


def attention(nc, core, uT, y, ycol, tag, weights, nq, nkv, ktiles, gains, sinks, rel_bias):
    wq, wk, wv = nq * HD, nkv * HD, nkv * HD
    nqk, width, keys = nq + nkv, wq + wk + wv, ktiles * P
    pad = (ktiles - 1) * P
    s_banks = (keys + 511) // 512
    t_banks = (nq * P + 511) // 512
    units = nq * ktiles // 4
    per_unit = -(-nq // units)
    bank_q, bank_k = 0, t_banks
    bank_s = [bank_k + 1, bank_k + 1 + s_banks]
    bank_p = bank_k + 1 + 2 * s_banks
    assert bank_p + 2 <= 8
    n_neg = 2 if sinks is not None else 1

    def last_head(u):
        return (4 * u + 3) // ktiles

    def pipeline(eng, begin, step):
        begin()
        with eng.Fori(0, (TILES - 2) // 2) as i:
            for b in range(2):
                step(i * 2 + b, b)
        step(TILES - 2, 0, normalise=False)
        step(TILES - 1, 1, normalise=False, scores=False)

    window = keys - P
    with ExitStack() as ctx:
        ph = Phase(nc, ctx, tag)
        w = ph.sb("w", [P, DCH, width])
        qk = ph.sb("qk", [P, TILES, nqk * HD])
        v = ph.sb("v", [P, ktiles - 1 + TILES, wv])
        sq = ph.sb("sq", [P, 2, nqk * HD])
        rstd = ph.sb("rstd", [P, TILES * nqk])
        gain = ph.sb("gain", [HD, 2])
        bias = ph.sb("bias", [P, nq, keys])
        kT = ph.sb("kT", [HD + 1, nkv, pad + SEQ])
        qT = ph.sb("qT", [HD + 1, nq * P])
        qkn = ph.sb("qkn", [P, nqk * HD])
        logits = ph.sb("logits", [P, 2, nq, keys])
        rowmax = ph.sb("rowmax", [P, nq])
        negmax = ph.sb("negmax", [P, nq])
        rowsum = ph.sb("rowsum", [P, nq])
        sink = ph.sb("sink", [P, nq])
        sinkexp = ph.sb("sinkexp", [P, nq])
        inv = ph.sb("inv", [P, nq])
        pT = ph.sb("pT", [P, 2, 4, P])
        (w_in_, small_in, row_in, skew_out, bias_in, consts, made, bias_ready,
         proj_full, proj_free, sq_full, sq_free, v_full, rooted, rstd_ready,
         qkn_full, turned, qT_full, kT_full, s_full, s_free, neg_ready, p_full, sink_full,
         pt_full, pt_copied, pt_used, o_full, o_free, link, held) = ph.sems(
            "w_in small_in row_in skew_out bias_in consts made bias_ready "
            "proj_full proj_free sq_full sq_free v_full rooted rstd_ready "
            "qkn_full turned qT_full kT_full s_full s_free neg_ready p_full sink_full "
            "pt_full pt_copied pt_used o_full o_free link held")
        ps = core.ps
        n_small = 2 + (1 if sinks is not None else 0)
        if rel_bias is not None:
            pitch = keys + P
            head_row = ph.sb("relrow", [nq, REL_SIZE])
            ext = ph.sb("ext", [nq, pitch])
            skew = nc.dram_tensor(f"{tag}_skew", (nq, P * pitch), F32, kind="Internal").ap()
        block = ph.open_block()

        @block.sync
        def _(sp):
            at = 0
            for cols, n in zip(weights, (wq, wk, wv)):
                sp.dma_start(w[:, :, at:at + n], cols.rearrange("(c p) n -> p c n", p=P)).then_inc(w_in_, 16)
                at += n
            for j in range(2):
                sp.dma_start(gain[:, j:j + 1], gains[j].rearrange("(p o) -> p o", o=1)).then_inc(small_in, 16)
            if sinks is not None:
                sp.dma_start(sink[:], sinks.partition_broadcast(P)).then_inc(small_in, 16)
            if rel_bias is not None:
                sp.dma_start(head_row[:], rel_bias).then_inc(row_in, 16)
                sp.wait_ge(made, 2)
                for i in range(nq):
                    sp.dma_start(skew[i:i + 1, :].rearrange("o (q m) -> o q m", q=P),
                                 ext[i:i + 1, :].unsqueeze(1).broadcast_to([1, P, pitch])).then_inc(skew_out, 16)
                sp.wait_ge(skew_out, 16 * nq)
                for i in range(nq):
                    rows = skew[i, P - 1:P - 1 + P * (pitch - 1)].rearrange("(q m) -> q m", q=P)
                    sp.dma_start(bias[:, i, :], rows[:, 0:keys]).then_inc(bias_in, 16)
                sp.wait_ge(bias_in, 16 * nq)

        @block.gpsimd
        def _(pool):
            fill = Chain(pool, consts)
            fill.link(nc.gpsimd.memset(kT[0:HD, :, 0:pad], 0.0))
            fill.link(nc.gpsimd.memset(v[:, 0:ktiles - 1, :], 0.0))
            fill.link(nc.gpsimd.memset(kT[HD:HD + 1, :, 0:pad], NEG))
            fill.link(nc.gpsimd.memset(kT[HD:HD + 1, :, pad:], 0.0))
            fill.link(nc.gpsimd.memset(qT[HD:HD + 1, :], 1.0))
            if rel_bias is None:
                pool.iota(bias[:, 0, :], pattern=[[-1, keys]], base=window, channel_multiplier=1,
                          allow_small_or_imprecise_dtypes=True).then_inc(made, 1)

        @block.scalar
        def _(act):
            for t in range(TILES):
                act.wait_ge(proj_full, t + 1)
                src = ps[:, 2 * (t % 4):2 * (t % 4) + 2, :].rearrange("p k n -> p (k n)")
                nc.scalar.activation(qk[:, t, :], src[:, 0:nqk * HD], ACT.Copy).then_inc(proj_free, 1)
                act.wait_ge(sq_free, t + 1)
                nc.scalar.activation(sq[:, t % 2, :], src[:, 0:nqk * HD], ACT.Square).then_inc(sq_full, 1)
            act.wait_ge(sq_free, TILES + 2)
            nc.scalar.activation(rstd[:], rstd[:], ACT.Sqrt, bias=core.eps[:, 0:1], scale=1.0 / HD).then_inc(rooted, 1)
            act.wait_ge(small_in, 16 * n_small)
            act.wait_ge(consts, 5)
            def copy_turned(t):
                act.wait_ge(turned, t + 1)
                nc.scalar.activation(qT[0:HD, :], ps[0:HD, bank_q:bank_q + t_banks, :].rearrange("p k n -> p (k n)")[:, 0:nq * P],
                                     ACT.Copy, scale=gain[:, 0:1]).then_inc(qT_full, 1)
                nc.scalar.activation(kT[0:HD, :, bass.ds(t * P + pad, P)],
                                     ps[0:HD, bank_k, 0:nkv * P].rearrange("p (k n) -> p k n", n=P),
                                     ACT.Copy, scale=gain[:, 1:2]).then_inc(kT_full, 1)

            def exponentials(par, heads):
                for i in heads:
                    nc.scalar.activation(logits[:, par, i, :], logits[:, par, i, :], ACT.Exp, bias=negmax[:, i:i + 1],
                                         accum_out=rowsum[:, i:i + 1]).then_inc(p_full, 1)

            def step(t, par, normalise=True, scores=True):
                act.wait_ge(neg_ready, t * n_neg + n_neg)
                early = last_head(1) + 1
                exponentials(par, range(early))
                if scores:
                    copy_turned(t + 1)
                exponentials(par, range(early, nq))
                if sinks is not None:
                    nc.scalar.activation(sinkexp[:], sinkexp[:], ACT.Exp).then_inc(sink_full, 1)
                for u in range(units):
                    n = (par * units + u) % 2
                    act.wait_ge(pt_full, t * units + (u + 1))
                    act.wait_ge(pt_used, t * units + (u + 1))
                    nc.scalar.activation(pT[:, n].rearrange("p k n -> p (k n)"), ps[:, bank_p + n, :], ACT.Copy).then_inc(pt_copied, 1)

            act.sem_inc(pt_copied, 2)
            pipeline(act, lambda: copy_turned(0), step)

        @block.vector
        def _(dve):
            dve.sem_inc(sq_free, 2)
            dve.sem_inc(s_free, 2)
            dve.sem_inc(o_free, 2)
            for t in range(TILES):
                dve.wait_ge(sq_full, t + 1)
                nc.vector.tensor_copy(v[:, ktiles - 1 + t, :],
                                      ps[:, 2 * (t % 4):2 * (t % 4) + 2, :].rearrange("p k n -> p (k n)")[:, nqk * HD:width]).then_inc(v_full, 1)
                nc.vector.tensor_reduce(rstd[:, t * nqk:(t + 1) * nqk], sq[:, t % 2, :].rearrange("p (h d) -> p h d", d=HD),
                                        axis=AX.X, op=ALU.add).then_inc(sq_free, 1)
            dve.wait_ge(rooted, 1)
            nc.vector.reciprocal(rstd[:], rstd[:]).then_inc(rstd_ready, 1)
            dve.wait_ge(rstd_ready, 1)
            once = Chain(dve, bias_ready)
            if rel_bias is None:
                dve.wait_ge(made, 1)
                once.link(nc.vector.tensor_scalar(bias[:, 1, :], bias[:, 0, :], -1.0, None, ALU.mult))
                once.link(nc.vector.tensor_tensor(bias[:, 0, :], bias[:, 0, :], bias[:, 1, :], ALU.max))
                for i in reversed(range(nq)):
                    slope = float(np.float32(2.0 ** (-8.0 * (i + 1) / nq)))
                    once.link(nc.vector.tensor_scalar(bias[:, i, :], bias[:, 0, :], -slope / HD ** -0.5, None, ALU.mult))
            else:
                dve.wait_ge(row_in, 16)
                far = window + P - 1 - REL_PAST
                ext_rev = ext[:, far:far + REL_SIZE]
                nc.vector.tensor_copy(ext_rev, head_row[:, ::-1]).then_inc(made, 1)
                dve.wait_ge(made, 1)
                once.link(nc.vector.tensor_scalar(ext[:, 0:far], head_row[:, REL_SIZE - 1:REL_SIZE].broadcast_to([nq, far]), 1.0, None, ALU.mult))
                nc.vector.tensor_scalar(ext[:, far + REL_SIZE:], head_row[:, 0:1].broadcast_to([nq, pitch - far - REL_SIZE]),
                                        1.0, None, ALU.mult).then_inc(made, 1)
                dve.wait_ge(bias_in, 16 * nq)
                once.link(nc.vector.tensor_scalar(bias[:].rearrange("p h k -> p (h k)"), bias[:].rearrange("p h k -> p (h k)"),
                                                  HD ** 0.5, None, ALU.mult))
            early, late = bias[0:CHUNK], bias[CHUNK:P]
            once.link(nc.vector.memset(early[:, :, keys - CHUNK:keys], NEG))
            if rel_bias is None:
                once.link(nc.vector.memset(early[:, :, 0:CHUNK], NEG))
                once.link(nc.vector.memset(late[:, :, 0:2 * CHUNK], NEG))
            else:
                once.link(nc.vector.memset(late[:, :, 0:CHUNK], NEG))
            dve.wait_ge(small_in, 16 * n_small)

            def normalise_qk(t):
                nc.vector.tensor_tensor(qkn[:].rearrange("p (h d) -> p h d", d=HD),
                                        qk[:, bass.ds(t, 1), :].rearrange("p o (h d) -> p (o h) d", d=HD),
                                        rstd[:, bass.ds(t * nqk, nqk)].unsqueeze(2).broadcast_to([P, nqk, HD]),
                                        ALU.mult).then_inc(qkn_full, 1)

            def read_scores(t, par):
                for i in range(nq):
                    dve.wait_ge(s_full, t * nq + (i + 1))
                    dve.sem_inc(held, 1)
                    b = bank_s[i % 2]
                    nc.vector.tensor_tensor_reduce(
                        out=logits[:, par, i, :], in0=ps[:, b:b + s_banks, :].rearrange("p k n -> p (k n)")[:, 0:keys],
                        in1=bias[:, i, :], scale=HD ** -0.5, scalar=sink[:, i:i + 1] if sinks is not None else NEG,
                        op0=ALU.add, op1=ALU.max, accum_out=rowmax[:, i:i + 1]).then_inc(s_free, 1)
                dve.wait_ge(s_free, t * nq + (nq + 2))
                nc.vector.tensor_scalar(negmax[:], rowmax[:], -1.0, None, ALU.mult).then_inc(neg_ready, 1)
                if sinks is not None:
                    dve.wait_ge(neg_ready, t * 2 + 1)
                    nc.vector.tensor_tensor(sinkexp[:], sink[:], negmax[:], ALU.add).then_inc(neg_ready, 1)

            def begin():
                normalise_qk(0)
                dve.wait_ge(turned, 1)
                normalise_qk(1)
                read_scores(0, 0)

            def step(t, par, normalise=True, scores=True):
                if normalise:
                    dve.wait_ge(turned, t + 2)
                    normalise_qk(t + 2)
                dve.wait_ge(p_full, t * nq + nq)
                dve.wait_ge(o_free, t + 2)
                chain = Chain(dve, link, t * n_neg)
                if sinks is not None:
                    dve.wait_ge(sink_full, t + 1)
                    chain.link(nc.vector.tensor_tensor(inv[:], rowsum[:], sinkexp[:], ALU.add))
                    chain.link(nc.vector.reciprocal(inv[:], inv[:]))
                else:
                    chain.link(nc.vector.reciprocal(inv[:], rowsum[:]))
                if scores:
                    read_scores(t + 1, 1 - par)
                dve.wait_ge(o_full, t + 1)
                nc.vector.tensor_tensor(
                    y[:, bass.ds(t, 1), ycol:ycol + wq].rearrange("p o (h d) -> p (o h) d", d=HD),
                    ps[:, bank_k, 0:wq].rearrange("p (h d) -> p h d", d=HD),
                    inv[:].unsqueeze(2).broadcast_to([P, nq, HD]), ALU.mult).then_inc(o_free, 1)

            pipeline(dve, begin, step)

        @block.tensor
        def _(pe):
            pe.wait_ge(w_in_, 48)
            for t in range(TILES):
                if t >= 4:
                    pe.wait_ge(sq_full, t - 3)
                    pe.wait_ge(proj_free, t - 3)
                    pe.wait_ge(v_full, t - 3)
                b = 2 * (t % 4)
                for lo in range(0, width, 512):
                    hi = min(lo + 512, width)
                    for c in range(DCH):
                        last = nc.tensor.matmul(ps[:, b + lo // 512, 0:hi - lo], uT[:, c, t * P:(t + 1) * P],
                                                w[:, c, lo:hi], start=(c == 0), stop=(c == DCH - 1))
                last.then_inc(proj_full, 1)
            pe.wait_ge(sq_full, TILES)
            pe.wait_ge(proj_free, TILES)
            pe.wait_ge(v_full, TILES)
            pe.wait_ge(consts, 5)

            def turn(t):
                pe.wait_ge(qkn_full, t + 1)
                pe.sem_inc(held, 1)
                for i in range(nqk):
                    if i == nq:
                        pe.wait_ge(o_free, t + 1)
                        pe.sem_inc(held, 1)
                    b, col = (bank_q + i * P // 512, i * P % 512) if i < nq else (bank_k, (i - nq) * P)
                    last = nc.tensor.transpose(ps[0:HD, b, col:col + P], qkn[:, i * HD:(i + 1) * HD], core.ident[:])
                last.then_inc(turned, 1)

            def score_heads(t, heads):
                for i in heads:
                    if i == 0:
                        pe.wait_ge(qT_full, t + 1)
                        pe.wait_ge(kT_full, t + 1)
                    pe.wait_ge(s_free, t * nq + (i + 1))
                    for lo in range(0, keys, 512):
                        n = min(512, keys - lo)
                        last = nc.tensor.matmul(ps[:, bank_s[i % 2] + lo // 512, 0:n], qT[:, i * P:(i + 1) * P],
                                                kT[:, i * nkv // nq, bass.ds(t * P + lo, n)], start=True, stop=True)
                    last.then_inc(s_full, 1)

            def turn_unit(t, par, u):
                pe.wait_ge(p_full, t * nq + (last_head(u) + 1))
                pe.wait_ge(pt_copied, t * units + (u + 1))
                for j in range(4):
                    i, k = divmod(4 * u + j, ktiles)
                    last = nc.tensor.transpose(ps[:, bank_p + (par * units + u) % 2, j * P:(j + 1) * P],
                                               logits[:, par, i, k * P:(k + 1) * P], core.ident[:])
                last.then_inc(pt_full, 1)

            def multiply_unit(t, par, u):
                pe.wait_ge(pt_copied, t * units + (u + 3))
                for j in range(4):
                    i, k = divmod(4 * u + j, ktiles)
                    kv = i * nkv // nq
                    last = nc.tensor.matmul(ps[:, bank_k, i * HD:(i + 1) * HD], pT[:, (par * units + u) % 2, j, :],
                                            v[:, bass.ds(t + k, 1), kv * HD:(kv + 1) * HD].rearrange("p o d -> p (o d)"),
                                            start=(k == 0), stop=(k == ktiles - 1))
                last.then_inc(pt_used, 1)
                if u == units - 1:
                    pe.wait_ge(pt_used, t * units + (units + 2))
                    pe.sem_inc(o_full, 1)

            def begin():
                turn(0)
                score_heads(0, range(nq))

            def step(t, par, normalise=True, scores=True):
                if scores:
                    turn(t + 1)
                turn_unit(t, par, 0)
                turn_unit(t, par, 1)
                if not scores:
                    pe.wait_ge(o_free, t + 2)
                for u in range(units):
                    if scores:
                        score_heads(t + 1, range(u * per_unit, min(nq, (u + 1) * per_unit)))
                    multiply_unit(t, par, u)
                    if u + 2 < units:
                        turn_unit(t, par, u + 2)

            pe.sem_inc(pt_used, 2)
            pipeline(pe, begin, step)


def project_out(nc, core, tag, y, nch, gain, w_rows):
    with ExitStack() as ctx:
        ph = Phase(nc, ctx, tag)
        w = ph.sb("w", [P, nch, D])
        yn = ph.sb("yn", [P, 2, nch * P])
        yT = ph.sb("yT", [P, 2, nch * P])
        gT = ph.sb("gT", [P, nch])
        rstd = ph.sb("rstd", [P, TILES])
        w_in_, small_in, squares, rooted, rstd_ready, yn_full, t_full, yT_full, out_full, out_free = ph.sems(
            "w_in small_in squares rooted rstd_ready yn_full t_full yT_full out_full out_free")
        block = ph.open_block()
        h, ps = core.h, core.ps

        @block.sync
        def _(sp):
            sp.dma_start(w[:], w_rows.rearrange("(c p) n -> p c n", p=P)).then_inc(w_in_, 16)
            sp.dma_start(gT[:], gain.rearrange("(c p) -> p c", p=P), allow_slow_non_contiguous=True).then_inc(small_in, 16)

        @block.scalar
        def _(act):
            for t in range(TILES):
                if t:
                    act.wait_ge(squares, t)
                nc.scalar.activation(yn[:, 0, :], y[:, t, :], ACT.Square, accum_out=rstd[:, t:t + 1]).then_inc(squares, 1)
            act.wait_ge(squares, TILES)
            nc.scalar.activation(rstd[:], rstd[:], ACT.Sqrt, bias=core.eps[:, 0:1], scale=1.0 / (nch * P)).then_inc(rooted, 1)

        @block.vector
        def _(dve):
            dve.sem_inc(out_free, 2)
            dve.wait_ge(rooted, 1)
            nc.vector.reciprocal(rstd[:], rstd[:]).then_inc(rstd_ready, 1)
            dve.wait_ge(rstd_ready, 1)
            dve.wait_ge(small_in, 16)
            with dve.Fori(0, TILES // 2) as i:
                for b in range(2):
                    nc.vector.tensor_scalar(yn[:, b, :], y[:, bass.ds(i * 2 + b, 1), :].rearrange("p o d -> p (o d)"),
                                            rstd[:, bass.ds(i * 2 + b, 1)], None, ALU.mult).then_inc(yn_full, 1)
                for b in range(2):
                    dve.wait_ge(t_full, i * 2 + (b + 1))
                    nc.vector.tensor_tensor(
                        yT[:, b, :].rearrange("p (c n) -> p c n", n=P),
                        ps[:, 2 * b:2 * b + 2, :].rearrange("p k (c n) -> p (k c) n", n=P)[:, 0:nch, :],
                        gT[:].unsqueeze(2).broadcast_to([P, nch, P]), ALU.mult).then_inc(yT_full, 1)
                for b in range(2):
                    dve.wait_ge(out_full, i * 2 + (b + 1))
                    row = h[:, bass.ds(i * 2 + b, 1), :].rearrange("p o d -> p (o d)")
                    nc.vector.tensor_tensor(row, ps[:, 4 + 2 * b:6 + 2 * b, :].rearrange("p k n -> p (k n)"), row,
                                            ALU.add).then_inc(out_free, 1)

        @block.tensor
        def _(pe):
            pe.wait_ge(w_in_, 16)
            with pe.Fori(0, TILES // 2) as i:
                for b in range(2):
                    pe.wait_ge(yn_full, i * 2 + (b + 1))
                    for c in range(nch):
                        last = nc.tensor.transpose(ps[:, 2 * b + c // 4, c % 4 * P:(c % 4 + 1) * P],
                                                   yn[:, b, c * P:(c + 1) * P], core.ident[:])
                    last.then_inc(t_full, 1)
                for b in range(2):
                    pe.wait_ge(yT_full, i * 2 + (b + 1))
                    pe.wait_ge(out_free, i * 2 + (b + 1))
                    for half in range(2):
                        for c in range(nch):
                            last = nc.tensor.matmul(ps[:, 4 + 2 * b + half, :], yT[:, b, c * P:(c + 1) * P],
                                                    w[:, c, half * 512:(half + 1) * 512], start=(c == 0), stop=(c == nch - 1))
                    last.then_inc(out_full, 1)


def mixer_a(nc, core, uT, y, io):
    w = io["w_in"][0]
    kcol, vcol = A_WIDTH, A_WIDTH + A_KV * HD
    attention(nc, core, uT, y, 0, "a", [w[:, 0:kcol], w[:, kcol:vcol], w[:, vcol:A_QKV]], A_HEADS, A_KV, 2,
              [io["a_q_norm"][0], io["a_k_norm"][0]], io["a_sinks"][0], None)
    project_out(nc, core, "aout", y, A_WIDTH // P, io["a_out_norm"][0], io["w_out"][0, 0:A_WIDTH, :])


def mixer_c(nc, core, uT, y, io):
    w = io["w_in"][0]
    for part in range(C_HEADS // C_PASS):
        n = C_PASS * HD
        at = A_QKV + B_IN + part * n
        attention(nc, core, uT, y, part * n, f"c{part}", [w[:, at + j * C_WIDTH:at + j * C_WIDTH + n] for j in range(3)],
                  C_PASS, C_PASS, 5, [io["c_q_norm"][0], io["c_k_norm"][0]], None,
                  io["c_rel_bias"][0, part * C_PASS:(part + 1) * C_PASS, :])
    project_out(nc, core, "cout", y, C_WIDTH // P, io["c_out_norm"][0], io["w_out"][0, A_WIDTH + B_WIDTH:, :])


def mixer_b_project(nc, core, uT, z, xbc, dt, io):
    zcol = A_QKV
    xcol = zcol + B_WIDTH
    dcol = xcol + B_XBC
    XCH = B_XBC // P
    w_in = io["w_in"][0]
    slabs = [zcol, zcol + 512, xcol, xcol + 512, xcol + 1024]
    with ExitStack() as ctx:
        ph = Phase(nc, ctx, "bp")
        w = ph.sb("w", [P, 2, DCH, 512])
        wdt = ph.sb("wdt", [P, DCH, B_HEADS])
        taps = ph.sb("taps", [P, XCH, B_CONV])
        cbias = ph.sb("cbias", [P, XCH])
        acc = ph.sb("acc", [P, 2, SEQ])
        slab_in = [ph.sem(f"slab{j}_in") for j in range(len(slabs))]
        small_in, history, unit_full, unit_copied, conv_full, silu_full, link = ph.sems(
            "small_in history unit_full unit_copied conv_full silu_full link")
        block = ph.open_block()
        ps = core.ps
        n_z = 2 * TILES
        n_units = n_z + 2 * XCH

        @block.sync
        def _(sp):
            for j, col in enumerate(slabs):
                if j >= 2:
                    sp.wait_ge(unit_full, 8 * (j - 1))
                sp.dma_start(w[:, j % 2], w_in[:, col:col + 512].rearrange("(c p) n -> p c n", p=P)).then_inc(slab_in[j], 16)
                if j == 0:
                    sp.dma_start(wdt[:], w_in[:, dcol:dcol + B_HEADS].rearrange("(c p) n -> p c n", p=P)).then_inc(small_in, 16)
                    sp.dma_start(cbias[:], io["b_conv_b"][0].rearrange("(c p) -> p c", p=P),
                                 allow_slow_non_contiguous=True).then_inc(small_in, 16)
                    for k in range(B_CONV):
                        sp.dma_start(taps[:, :, k], io["b_conv_w"][0, k].rearrange("(c p) -> p c", p=P),
                                     allow_slow_non_contiguous=True).then_inc(small_in, 16)

        @block.gpsimd
        def _(pool):
            nc.gpsimd.memset(xbc[:, :, 0:B_CONV - 1], 0.0).then_inc(history, 1)

        @block.scalar
        def _(act):
            for u in range(n_z):
                act.wait_ge(unit_full, u + 1)
                s, t = divmod(u, TILES)
                nc.scalar.activation(z[:, t, s * 512:(s + 1) * 512], ps[:, u % 7, :], ACT.Silu).then_inc(unit_copied, 1)
            for j in range(XCH + 1):
                if j < XCH:
                    for half in range(2):
                        u = n_z + 2 * j + half
                        act.wait_ge(unit_full, u + 1)
                        nc.scalar.activation(xbc[:, j, 3 + half * 512:3 + (half + 1) * 512], ps[:, u % 7, :],
                                             ACT.Copy).then_inc(unit_copied, 1)
                if j:
                    act.wait_ge(conv_full, j)
                    nc.scalar.activation(xbc[:, j - 1, 3:], acc[:, (j - 1) % 2, :], ACT.Silu).then_inc(silu_full, 1)

        @block.vector
        def _(dve):
            dve.wait_ge(small_in, 16 * (2 + B_CONV))
            dve.wait_ge(history, 1)
            chain = Chain(dve, link)
            for j in range(XCH):
                dve.wait_ge(unit_copied, n_z + 2 * j + 2)
                if j >= 2:
                    dve.wait_ge(silu_full, j - 1)
                a = acc[:, j % 2, :]
                chain.link(nc.vector.tensor_scalar(a, xbc[:, j, 3:], taps[:, j, 3:4], cbias[:, j:j + 1], ALU.mult, ALU.add))
                for k in range(B_CONV - 1):
                    ins = nc.vector.scalar_tensor_tensor(a, xbc[:, j, k:k + SEQ], taps[:, j, k:k + 1], a, ALU.mult, ALU.add)
                    if k < B_CONV - 2:
                        chain.link(ins)
                ins.then_inc(conv_full, 1)
            dve.wait_ge(unit_full, n_units + 1)
            nc.vector.tensor_copy(dt[:].rearrange("p t h -> p (t h)"), ps[:, 7, 0:TILES * B_HEADS])

        @block.tensor
        def _(pe):
            u = 0
            for j in range(len(slabs)):
                pe.wait_ge(slab_in[j], 16)
                for part in range(8):
                    if u >= 7:
                        pe.wait_ge(unit_copied, u - 6)
                    for c in range(DCH):
                        if j < 2:
                            lhsT, rhs = uT[:, c, part * P:(part + 1) * P], w[:, j % 2, c, :]
                        else:
                            lhsT = w[:, j % 2, c, part // 2 * P:(part // 2 + 1) * P]
                            rhs = uT[:, c, part % 2 * 512:(part % 2 + 1) * 512]
                        last = nc.tensor.matmul(ps[:, u % 7, :], lhsT, rhs, start=(c == 0), stop=(c == DCH - 1))
                    last.then_inc(unit_full, 1)
                    u += 1
            pe.wait_ge(small_in, 16 * (2 + B_CONV))
            for t in range(TILES):
                for c in range(DCH):
                    last = nc.tensor.matmul(ps[:, 7, t * B_HEADS:(t + 1) * B_HEADS], uT[:, c, t * P:(t + 1) * P], wdt[:, c, :],
                                            start=(c == 0), stop=(c == DCH - 1))
            last.then_inc(unit_full, 1)


def mixer_b_scan(nc, core, uT, z, xbc, dt, io):
    XH = B_WIDTH // P
    HB = TILES * B_HEADS
    GH = B_HEADS // B_GROUPS
    with ExitStack() as ctx:
        ph = Phase(nc, ctx, "bs")
        tri = ph.sb("tri", [P, P])
        ones = ph.sb("ones", [P, P])
        rows = ph.sb("rows", [P, 3, B_HEADS])
        soft = ph.sb("soft", [P, 3, HB])
        dtA = ph.sb("dtA", [P, HB])
        cs = ph.sb("cs", [P, HB])
        csT = ph.sb("csT", [HB, P])
        from_start = ph.sb("from_start", [P, HB])
        to_end = ph.sb("to_end", [P, HB])
        whole = ph.sb("whole", [P, HB])
        xs = ph.sb("xs", [P, 2, XH + 2 * B_GROUPS, P])
        bcs = uT[:, 0:4, :].rearrange("p (b k) n -> p b (k n)", b=2)
        seg = uT[:, 4:6, :].rearrange("p k (h l) -> p (k h) l", l=P)
        xdt, xend = uT[:, 6, :], uT[:, 7, :]
        yx = ph.sb("yx", [P, B_WIDTH])
        yo = ph.sb("yo", [P, B_WIDTH])
        bnat = ph.sb("bnat", [P, B_GROUPS * P])
        state = ph.sb("state", [P, B_WIDTH])
        spill = nc.dram_tensor("b_cs_rows", (HB, P), F32, kind="Internal").ap()
        (small_in, consts, pre, exped, sums, csT_full, spilled, tables, xs_full, bcs0_in, bcs1_in, seg_full, masked, decay,
         turned, b_full, cb_used, xdt_full, yx_full, xend_full, off_full, diag_full, state_add, state_full,
         yo_full, ysum_full, y_full, gated, m_full) = ph.sems(
            "small_in consts pre exped sums csT_full spilled tables xs_full bcs0_in bcs1_in seg_full masked decay "
            "turned b_full cb_used xdt_full yx_full xend_full off_full diag_full state_add state_full "
            "yo_full ysum_full y_full gated m_full")
        block = ph.open_block()
        ps = core.ps
        x_ps = ps[:, 0:2, :].rearrange("p k n -> p (k n)")
        b_ps, cb_ps = ps[:, 2, 0:B_GROUPS * P], ps[:, 2, B_GROUPS * P:2 * B_GROUPS * P]
        diag_ps = ps[:, 3:5, :].rearrange("p k n -> p (k n)")
        off_ps = ps[:, 5:7, :].rearrange("p k n -> p (k n)")
        heads = lambda ap: ap.rearrange("p (h d) -> p h d", d=HD)
        per_head = lambda ap: ap.unsqueeze(2).broadcast_to([P, B_HEADS, HD])

        @block.sync
        def _(sp):
            for j, name in enumerate(["b_dt_bias", "b_a_log", "b_d"]):
                sp.dma_start(rows[:, j, :], io[name][0].partition_broadcast(P)).then_inc(small_in, 16)
            sp.wait_ge(csT_full, 1)
            sp.dma_start(spill, csT[:]).then_inc(spilled, 16)
            sp.wait_ge(spilled, 16)
            with sp.Fori(0, TILES // 2) as i:
                for b, arrived in enumerate([bcs0_in, bcs1_in]):
                    sp.wait_ge(seg_full, i * 2 + (b + 1))
                    src = spill[bass.ds((i * 2 + b) * B_HEADS, B_HEADS), :].rearrange("h l -> (h l)")
                    sp.dma_start(bcs[:, b, :], src.partition_broadcast(P)).then_inc(arrived, 16)

        @block.gpsimd
        def _(pool):
            fill = Chain(pool, consts)
            fill.link(nc.gpsimd.memset(tri[:], 1.0))
            fill.link(nc.gpsimd.affine_select(out=tri[:], in_=tri[:], compare_op=ALU.is_ge, fill=0.0, base=0,
                                              pattern=[[1, P]], channel_multiplier=-1))
            fill.link(nc.gpsimd.memset(ones[:], 1.0))
            fill.link(nc.gpsimd.memset(state[:], 0.0))
            pool.wait_ge(tables, 3)
            with pool.Fori(0, TILES // 2) as i:
                for b in range(2):
                    n = i * 2 + (b + 1)
                    nc.gpsimd.tensor_copy(xs[:, b], xbc[:, :, bass.ds((i * 2 + b) * P + 3, P)]).then_inc(xs_full, 1)
                    pool.wait_ge(seg_full, n + 2)
                    pool.sem_inc(consts, 1)
                    nc.gpsimd.affine_select(out=seg[:], in_=seg[:], compare_op=ALU.is_ge, fill=NEG, base=0,
                                            pattern=[[0, B_HEADS], [1, P]], channel_multiplier=-1).then_inc(masked, 1)
                    pool.wait_ge(xdt_full, n)
                    pool.wait_ge(state_full, n)
                    nc.gpsimd.tensor_tensor(heads(xend), heads(xdt), per_head(to_end[:, bass.ds((i * 2 + b) * B_HEADS, B_HEADS)]),
                                            ALU.mult).then_inc(xend_full, 1)
                    pool.wait_ge(y_full, n)
                    row = z[:, bass.ds(i * 2 + b, 1), :].rearrange("p o d -> p (o d)")
                    nc.gpsimd.tensor_tensor(row, yx[:], row, ALU.mult).then_inc(gated, 1)

        @block.scalar
        def _(act):
            act.wait_ge(pre, 3)
            nc.scalar.activation(soft[:, 1, :], soft[:, 1, :], ACT.Exp, scale=-1.0).then_inc(exped, 1)
            nc.scalar.activation(rows[:, 1, :], rows[:, 1, :], ACT.Exp).then_inc(exped, 1)
            act.wait_ge(exped, 2)
            nc.scalar.activation(soft[:, 1, :], soft[:, 1, :], ACT.Ln, bias=1.0).then_inc(exped, 1)
            act.wait_ge(sums, 1)
            nc.scalar.activation(cs[:], ps[:, 0, 0:HB], ACT.Copy).then_inc(exped, 1)
            nc.scalar.activation(csT[:], ps[:, 1, 0:P], ACT.Copy).then_inc(csT_full, 1)
            nc.scalar.activation(from_start[:], ps[:, 0, 0:HB], ACT.Exp).then_inc(tables, 1)
            nc.scalar.activation(whole[:], ps[:, 2, 0:HB], ACT.Exp).then_inc(tables, 1)
            act.wait_ge(pre, 6)
            nc.scalar.activation(to_end[:], to_end[:], ACT.Exp).then_inc(tables, 1)
            with act.Fori(0, TILES) as t:
                act.wait_ge(masked, t + 1)
                nc.scalar.activation(seg[:], seg[:], ACT.Exp).then_inc(decay, 1)
                act.wait_ge(turned, t + 1)
                nc.scalar.activation(bnat[:], b_ps, ACT.Copy).then_inc(b_full, 1)

        @block.vector
        def _(dve):
            dve.sem_inc(seg_full, 2)
            dve.sem_inc(state_full, 1)
            dve.sem_inc(cb_used, 1)
            dve.sem_inc(yx_full, 1)
            dve.wait_ge(small_in, 48)
            first = Chain(dve, pre)
            raw = dt[:].rearrange("p t h -> p (t h)")
            first.link(nc.vector.tensor_tensor(soft[:, 0, :].rearrange("p (t h) -> p t h", h=B_HEADS), dt[:],
                                               rows[:, 0:1, :].broadcast_to([P, TILES, B_HEADS]), ALU.add))
            first.link(nc.vector.tensor_scalar(soft[:, 2, :], soft[:, 0, :], 0.0, None, ALU.max))
            first.link(nc.vector.scalar_tensor_tensor(soft[:, 1, :], soft[:, 2, :], 2.0, soft[:, 0, :], ALU.mult, ALU.subtract))
            dve.wait_ge(exped, 3)
            first.link(nc.vector.tensor_tensor(raw, soft[:, 1, :], soft[:, 2, :], ALU.add))
            first.link(nc.vector.scalar_tensor_tensor(dtA[:].rearrange("p (t h) -> p t h", h=B_HEADS), dt[:], -1.0,
                                                      rows[:, 1:2, :].broadcast_to([P, TILES, B_HEADS]), ALU.mult, ALU.mult))
            dve.wait_ge(sums, 1)
            dve.wait_ge(exped, 4)
            dve.wait_ge(tables, 2)
            first.link(nc.vector.tensor_tensor(to_end[:], ps[:, 2, 0:HB], cs[:], ALU.subtract))
            dve.wait_ge(tables, 3)
            with dve.Fori(0, TILES // 2) as i:
                for b, arrived in enumerate([bcs0_in, bcs1_in]):
                    n = i * 2 + (b + 1)
                    of_tile = bass.ds((i * 2 + b) * B_HEADS, B_HEADS)
                    dve.wait_ge(arrived, i * 16 + 16)
                    nc.vector.tensor_tensor(seg[:], bcs[:, b, :].rearrange("p (h l) -> p h l", l=P),
                                            cs[:, of_tile].unsqueeze(2).broadcast_to([P, B_HEADS, P]),
                                            ALU.subtract).then_inc(seg_full, 1)
                    dve.wait_ge(turned, n)
                    nc.vector.tensor_tensor(heads(xdt), heads(x_ps), per_head(dt[:, bass.ds(i * 2 + b, 1), :].rearrange("p o h -> p (o h)")),
                                            ALU.mult).then_inc(xdt_full, 1)
                    nc.vector.tensor_tensor(heads(yx[:]), heads(x_ps), per_head(rows[:, 2, :]), ALU.mult).then_inc(yx_full, 1)
                    dve.wait_ge(decay, n)
                    dve.wait_ge(b_full, n)
                    by_group = seg[:].rearrange("p (g h) l -> p g h l", g=B_GROUPS)
                    nc.vector.tensor_tensor(by_group, by_group,
                                            cb_ps.rearrange("p (g l) -> p g l", l=P).unsqueeze(2).broadcast_to([P, B_GROUPS, GH, P]),
                                            ALU.mult).then_inc(m_full, 1)
                    dve.wait_ge(off_full, n)
                    nc.vector.tensor_tensor(heads(yo[:]), heads(off_ps), per_head(from_start[:, of_tile]), ALU.mult).then_inc(yo_full, 1)
                    nc.vector.tensor_tensor(heads(state[:]), heads(state[:]), per_head(whole[:, of_tile]), ALU.mult).then_inc(yo_full, 1)
                    dve.wait_ge(yo_full, n * 2)
                    nc.vector.tensor_tensor(yx[:], yx[:], yo[:], ALU.add).then_inc(ysum_full, 1)
                    dve.wait_ge(state_add, n)
                    nc.vector.tensor_tensor(state[:], x_ps, state[:], ALU.add).then_inc(state_full, 1)
                    dve.wait_ge(diag_full, n)
                    dve.wait_ge(ysum_full, n)
                    nc.vector.tensor_tensor(yx[:], diag_ps, yx[:], ALU.add).then_inc(y_full, 1)
                    dve.wait_ge(gated, n)

        @block.tensor
        def _(pe):
            pe.wait_ge(consts, 4)
            pe.wait_ge(pre, 5)
            nc.tensor.matmul(ps[:, 0, 0:HB], tri[:], dtA[:], start=True, stop=True)
            nc.tensor.matmul(ps[0:HB, 1, 0:P], dtA[:], tri[:], start=True, stop=True)
            nc.tensor.matmul(ps[:, 2, 0:HB], ones[:], dtA[:], start=True, stop=True).then_inc(sums, 1)
            pe.wait_ge(tables, 3)
            pe.wait_ge(csT_full, 1)
            with pe.Fori(0, TILES // 2) as i:
                for b in range(2):
                    n = i * 2 + (b + 1)
                    pe.wait_ge(xs_full, n)
                    pe.wait_ge(state_full, n)
                    for c in range(XH + B_GROUPS):
                        out = x_ps[:, c * P:(c + 1) * P] if c < XH else b_ps[:, (c - XH) * P:(c - XH + 1) * P]
                        nc.tensor.transpose(out, xs[:, b, c, :], core.ident[:])
                    for g in range(B_GROUPS):
                        last = nc.tensor.matmul(cb_ps[:, g * P:(g + 1) * P], xs[:, b, XH + g, :], xs[:, b, XH + B_GROUPS + g, :],
                                                start=True, stop=True)
                    last.then_inc(turned, 1)
                    for g in range(B_GROUPS):
                        last = nc.tensor.matmul(off_ps[:, g * 512:(g + 1) * 512], xs[:, b, XH + B_GROUPS + g, :],
                                                state[:, g * 512:(g + 1) * 512], start=True, stop=True)
                    last.then_inc(off_full, 1)
                    pe.wait_ge(xend_full, n)
                    pe.wait_ge(yx_full, n + 1)
                    pe.wait_ge(b_full, n)
                    for g in range(B_GROUPS):
                        last = nc.tensor.matmul(x_ps[:, g * 512:(g + 1) * 512], bnat[:, g * P:(g + 1) * P],
                                                xend[:, g * 512:(g + 1) * 512], start=True, stop=True)
                    last.then_inc(state_add, 1)
                    pe.wait_ge(m_full, n)
                    for hd in range(B_HEADS):
                        last = nc.tensor.matmul(diag_ps[:, hd * HD:(hd + 1) * HD], seg[:, hd, :], xdt[:, hd * HD:(hd + 1) * HD],
                                                start=True, stop=True)
                    last.then_inc(diag_full, 1)


def mixer_b(nc, core, uT, io):
    with ExitStack() as ctx:
        z = ctx.enter_context(nc.sbuf_tensor("b_z", [P, TILES, B_WIDTH], F32))
        dt = ctx.enter_context(nc.sbuf_tensor("b_dt", [P, TILES, B_HEADS], F32))
        with ExitStack() as inner:
            xbc = inner.enter_context(nc.sbuf_tensor("b_xbc", [P, B_XBC // P, SEQ + B_CONV - 1], F32))
            mixer_b_project(nc, core, uT, z, xbc, dt, io)
            mixer_b_scan(nc, core, uT, z, xbc, dt, io)
        project_out(nc, core, "bout", z, B_WIDTH // P, io["b_out_norm"][0], io["w_out"][0, A_WIDTH:A_WIDTH + B_WIDTH, :])


def peer_and_gate(nc, core, hd, out, io):
    AHEAD = 5
    RING = 4
    KK = PH * TOPK
    with ExitStack() as ctx:
        ph = Phase(nc, ctx, "peer")
        wq = ph.sb("wq", [P, DCH, PH * PKD])
        wg = ph.sb("wg", [P, DCH, D])
        wp = ph.sb("wp", [P, PLE // P, D])
        skT = ph.sb("skT", [P, 2 * PH, PK])
        gain_row = ph.sb("gain_row", [P, D])
        gT = ph.sb("gT", [P, DCH])
        u_ring = ph.sb("u_ring", [P, RING, D])
        v_ring = ph.sb("v_ring", [P, RING, D])
        h_next = ph.sb("h_next", [P, D])
        h_sum = ph.sb("h_sum", [P, D])
        h_out = ph.sb("h_out", [P, D])
        un = ph.sb("un", [P, D])
        norm = ph.sb("norm", [P, D])
        uT = ph.sb("uT", [P, DCH, P])
        fT = ph.sb("fT", [P, DCH, P])
        gate = ph.sb("gate", [P, 512])
        ptok = ph.sb("ptok", [P, PLE])
        pT = ph.sb("pT", [P, PLE // P, P])
        q = ph.sb("q", [P, PKD])
        qT = ph.sb("qT", [P, PKD])
        top = ph.sb("top", [P, 2, TOPK])
        top_i = ph.sb("top_i", [P, 2, TOPK], U32)
        top_f = ph.sb("top_f", [P, 2, TOPK])
        rest = ph.sb("rest", [P, 2, PK])
        cand = ph.sb("cand", [P, TOPK, TOPK])
        cand2 = ph.sb("cand2", [P, TOPK * TOPK])
        best = ph.sb("best", [P, TOPK])
        best_i = ph.sb("best_i", [P, TOPK], U32)
        pair_i = ph.sb("pair_i", [P, 2, TOPK], U32)
        pair_f = ph.sb("pair_f", [P, 2 * TOPK])
        hot = ph.sb("hot", [P, 2 * TOPK, TOPK])
        halves = ph.sb("halves", [P, 2, TOPK])
        row_f = ph.sb("row_f", [P, TOPK])
        steps16 = ph.sb("steps16", [P, TOPK])
        idx_all = ph.sb("idx_all", [P, KK], U32)
        gates_all = ph.sb("gates_all", [P, KK])
        idx_u = ph.sb("idx_u", [P, 2, TOPK], U32)
        idx_v = ph.sb("idx_v", [P, 2, TOPK], U32)
        negbest = ph.sb("negbest", [P, 1])
        gexp = ph.sb("gexp", [P, TOPK])
        gsum = ph.sb("gsum", [P, 1])
        dots = ph.sb("dots", [P, 2, TOPK])
        weights = ph.sb("weights", [P, 2, TOPK])
        diag = ph.sb("diag", [P, RING, P])
        stat = ph.sb("stat", [P, 2])
        (held, small_in, sub_in, sub_turned, sub_copied, wq_in, wg_in, h_in, p_in,
         pre_sq, pre_root, pre_link, norm_full, pre_turned, uT_full,
         q_full, q_copied, qT_full, qT_copied, score_full, topk_link, idx_full, best_full, gexp_full, gates_full, gate_link, un_taken,
         u_free, v_free, iu_full, iv_full, gelu_full, weights_full, diag_full, sum_read,
         fin_sum, fin_sq, fin_root, fin_link, fin_norm, fin_turned, fin_copied, p_turned, p_copied,
         gate_full, gate_copied, ple_full, fin_mul, fin_done, stored, iota_done) = ph.sems(
            "held small_in sub_in sub_turned sub_copied wq_in wg_in h_in p_in "
            "pre_sq pre_root pre_link norm_full pre_turned uT_full "
            "q_full q_copied qT_full qT_copied score_full topk_link idx_full best_full gexp_full gates_full gate_link un_taken "
            "u_free v_free iu_full iv_full gelu_full weights_full diag_full sum_read "
            "fin_sum fin_sq fin_root fin_link fin_norm fin_turned fin_copied p_turned p_copied "
            "gate_full gate_copied ple_full fin_mul fin_done stored iota_done")
        u_in = [ph.sem(f"u{j}_in") for j in range(RING)]
        v_in = [ph.sem(f"v{j}_in") for j in range(RING)]
        ps = core.ps
        sum_ps = [ps[:, 2 * b:2 * b + 2, :].rearrange("p k n -> p (k n)") for b in range(2)]
        q_ps, qT_ps, score_ps, misc_ps = (ps[:, b, :] for b in range(4, 8))
        TK = 24
        block = ph.open_block()

        def schedule(eng, begin, group, finish_tail):
            def tile(t, first, last):
                g = t * PH
                group(g, t, 0, v=not first, add=not first, topk=True)
                group(g + 1, t, 1, v=True, add=not first, topk=True, finish=not first)
                group(g + 2, t, 2, v=True, topk=True, prepare=not last, final_topk=last)
                with eng.Fori(0, 2) as k:
                    for b in range(2):
                        group(g + k * 2 + (3 + b), t, k * 2 + (3 + b), v=True, topk=not last, odd=1 - b)
                group(g + 7, t, 7, v=True, topk=not last)
            begin()
            tile(0, True, False)
            with eng.Fori(1, TILES - 1) as t:
                tile(t, False, False)
            tile(TILES - 1, False, True)
            finish_tail(TILES * PH)

        @block.sync
        def _(sp):
            def load_tile(t):
                sp.dma_start(h_next[:], hd[bass.ds(t * P, P), :]).then_inc(h_in, 16)

            sp.dma_start(h_next[:], hd[0:P, :]).then_inc(h_in, 16)
            sp.dma_start(gain_row[:], io["ffn_norm"][0].partition_broadcast(P)).then_inc(small_in, 16)
            sp.dma_start(gT[:], io["ple_norm"][0].rearrange("(c p) -> p c", p=P), allow_slow_non_contiguous=True).then_inc(small_in, 16)
            sp.dma_start(wg[:, 0:2, :].rearrange("p c (a d) -> p (c a) d", d=P),
                         io["peer_sub_keys"][0].rearrange("h s k d -> k (h s) d")).then_inc(sub_in, 16)
            sp.dma_start(wq[:], io["peer_w_query"][0].rearrange("(c p) n -> p c n", p=P)).then_inc(wq_in, 16)
            sp.wait_ge(sub_copied, 4)
            sp.dma_start(wg[:], io["ple_w_gate"][0].rearrange("(c p) n -> p c n", p=P)).then_inc(wg_in, 16)
            sp.dma_start(wp[:], io["ple_w_proj"][0].rearrange("(c p) n -> p c n", p=P)).then_inc(wg_in, 16)

            def prepare(t):
                sp.wait_ge(sum_read, t * PH + 3)
                sp.sem_inc(held, 1)
                sp.dma_start(h_next[:], hd[bass.ds((t + 1) * P, P), :]).then_inc(h_in, 16)

            def finish(t):
                sp.wait_ge(p_copied, t + 1)
                sp.sem_inc(held, 1)
                sp.dma_start(ptok[:], io["p"][0, 0, bass.ds(t * P, P), :]).then_inc(p_in, 16)
                sp.wait_ge(fin_done, t * 2 + 2)
                sp.sem_inc(held, 1)
                sp.dma_start(out[bass.ds(t * P, P), :], h_out[:]).then_inc(stored, 16)

            prepare(0)
            with sp.Fori(1, TILES - 1) as t:
                finish(t - 1)
                prepare(t)
            finish(TILES - 2)
            finish(TILES - 1)
            sp.wait_ge(stored, 16 * TILES)

        @block.gpsimd
        def _(pool):
            def begin():
                pool.iota(steps16[:], pattern=[[1, TOPK]], base=0, channel_multiplier=0,
                          allow_small_or_imprecise_dtypes=True).then_inc(iota_done, 1)

            def gather(ring, s, table, idx, arrived):
                nc.gpsimd.indirect_dma_start(ring[:, s % RING, :], None, table,
                                             bass.IndirectOffsetOnAxis(ap=idx[:, s:s + 1], axis=0)).then_inc(arrived[s % RING], 16)

            def values(g, s, odd):
                if s == 0:
                    pool.wait_ge(iv_full, g + 1)
                pool.wait_ge(v_free, g * TOPK + (s + 1))
                pool.sem_inc(held, 1)
                gather(v_ring, s, io["peer_v"][0], idx_v[:, odd, :], v_in)

            def group(g, t, h, v=False, add=True, topk=False, finish=False, prepare=False, odd=None, final_topk=False):
                odd = h % 2 if odd is None else odd
                pool.wait_ge(iu_full, g + 1)
                for s in range(TOPK):
                    pool.wait_ge(u_free, g * TOPK + (s + 1))
                    pool.sem_inc(held, 1)
                    gather(u_ring, s, io["peer_u"][0], idx_u[:, odd, :], u_in)
                    if v:
                        values(g - 1, s, 1 - odd)

            def tail(g):
                for s in range(TOPK):
                    values(g - 1, s, 1)

            schedule(pool, begin, group, tail)

        @block.scalar
        def _(act):
            def square_and_root(src, at, squared, rooted, n):
                nc.scalar.activation(norm[:], src, ACT.Square, accum_out=stat[:, at:at + 1]).then_inc(squared, 1)
                act.wait_ge(squared, n + 1)
                nc.scalar.activation(stat[:, at:at + 1], stat[:, at:at + 1], ACT.Sqrt, bias=core.eps[:, 0:1],
                                     scale=1.0 / D).then_inc(rooted, 1)

            def prepare_root(t, begins=False):
                act.wait_ge(h_in, t * 16 + 16)
                if not begins:
                    act.wait_ge(fin_copied, (t - 1) * 2)
                square_and_root(h_next[:], 0, pre_sq, pre_root, t)

            def prepare_copy(t):
                for half in range(2):
                    act.wait_ge(pre_turned, t * 2 + (half + 1))
                    nc.scalar.activation(uT[:, half * 4:half * 4 + 4, :], misc_ps.rearrange("p (c n) -> p c n", n=P),
                                         ACT.Copy).then_inc(uT_full, 1)

            def q_copy(k):
                act.wait_ge(q_full, k + 1)
                nc.scalar.activation(q[:], q_ps[:, 0:PKD], ACT.Copy).then_inc(q_copied, 1)

            def qT_copy(k):
                act.wait_ge(qT_full, k + 1)
                nc.scalar.activation(qT[:], qT_ps[:, 0:PKD], ACT.Copy).then_inc(qT_copied, 1)

            def gate_exp(k):
                act.wait_ge(best_full, k + 1)
                act.wait_ge(gates_full, k)
                nc.scalar.activation(gexp[:], best[:], ACT.Exp, bias=negbest[:, 0:1], accum_out=gsum[:, 0:1]).then_inc(gexp_full, 1)

            def begin():
                act.sem_inc(p_copied, 1)
                for j in range(4):
                    act.wait_ge(sub_turned, j + 1)
                    nc.scalar.activation(skT[:, 4 * j:4 * j + 4, :], ps[:, j, :].rearrange("p (a k) -> p a k", k=PK),
                                         ACT.Copy).then_inc(sub_copied, 1)
                prepare_root(0, begins=True)
                prepare_copy(0)
                for k in range(AHEAD):
                    q_copy(k)
                    qT_copy(k)
                    gate_exp(k)

            def diagonal(g, s, odd):
                if s == 0:
                    act.wait_ge(weights_full, g + 1)
                act.wait_ge(v_free, g * TOPK + (s + 1))
                nc.scalar.activation(diag[:, s % RING, :], core.ident[:], ACT.Copy,
                                     scale=weights[:, odd, s:s + 1]).then_inc(diag_full, 1)

            def p_copy(t):
                act.wait_ge(p_turned, t + 1)
                nc.scalar.activation(pT[:], misc_ps[:, 0:PLE].rearrange("p (c n) -> p c n", n=P), ACT.Copy).then_inc(p_copied, 1)

            def finish_root(t):
                act.wait_ge(fin_sum, t + 1)
                square_and_root(h_out[:], 1, fin_sq, fin_root, t)

            def gate_half(t, half):
                act.wait_ge(gate_full, t * 2 + (half + 1))
                act.wait_ge(fin_done, t * 2 + half) if half else None
                nc.scalar.activation(gate[:], misc_ps, ACT.Sigmoid).then_inc(gate_copied, 1)

            def group(g, t, h, v=False, add=True, topk=False, finish=False, prepare=False, odd=None, final_topk=False):
                odd = h % 2 if odd is None else odd
                for s in range(TOPK):
                    if v:
                        diagonal(g - 1, s, 1 - odd)
                    if topk and s == 3:
                        q_copy(g + AHEAD)
                    if topk and s == 5:
                        qT_copy(g + AHEAD)
                    if finish and s == 2:
                        p_copy(t - 1)
                        finish_root(t - 1)
                    if finish and s in (9, 12):
                        gate_half(t - 1, s // 12)
                    if prepare and s == 6:
                        prepare_root(t + 1)
                    if prepare and s == 13:
                        prepare_copy(t + 1)
                if topk:
                    gate_exp(g + AHEAD)
                act.wait_ge(u_free, g * TOPK + (TOPK + RING))
                nc.scalar.activation(dots[:, odd, :], dots[:, odd, :], ACT.Gelu).then_inc(gelu_full, 1)

            def tail(g):
                for s in range(TOPK):
                    diagonal(g - 1, s, 1)
                p_copy(TILES - 1)
                finish_root(TILES - 1)
                for half in range(2):
                    gate_half(TILES - 1, half)

            schedule(act, begin, group, tail)

        @block.vector
        def _(dve):
            def retrieval(k, slot):
                chain = Chain(dve, topk_link, k * TK)

                def link(ins):
                    chain.link(ins)
                    dve.sem_inc(held, 1)

                def sixteen_best(vals, idx, src, scratch):
                    link(nc.vector.max(vals[:, 0:8], src))
                    link(nc.vector.max_index(idx[:, 0:8], vals[:, 0:8], src))
                    link(nc.vector.match_replace(scratch, vals[:, 0:8], src, -3e38))
                    link(nc.vector.max(vals[:, 8:16], scratch))
                    link(nc.vector.max_index(idx[:, 8:16], vals[:, 8:16], scratch))

                def keys(side):
                    def step():
                        if side == 0:
                            dve.wait_ge(score_full, k + 1)
                            dve.sem_inc(held, 1)
                        sixteen_best(top[:, side, :], top_i[:, side, :], score_ps[:, side * PK:(side + 1) * PK], rest[:, side, :])
                    return step

                def pairs():
                    chain.link(nc.vector.tensor_copy(top_f[:], top_i[:]))
                    chain.link(nc.vector.tensor_tensor(cand[:], top[:, 0, :].unsqueeze(2).broadcast_to([P, TOPK, TOPK]),
                                                       top[:, 1:2, :].broadcast_to([P, TOPK, TOPK]), ALU.add))

                def best_pairs():
                    dve.wait_ge(gexp_full, k)
                    dve.sem_inc(held, 1)
                    sixteen_best(best[:], best_i[:], cand[:].rearrange("p a b -> p (a b)"), cand2[:])

                def unpair():
                    chain.link(nc.vector.tensor_scalar(pair_i[:, 0, :], best_i[:], 4, None, ALU.logical_shift_right))
                    chain.link(nc.vector.tensor_scalar(pair_i[:, 1, :], best_i[:], 15, None, ALU.bitwise_and))
                    chain.link(nc.vector.tensor_copy(pair_f[:], pair_i[:].rearrange("p a b -> p (a b)")))
                    chain.link(nc.vector.tensor_tensor(hot[:], pair_f[:].unsqueeze(2).broadcast_to([P, 2 * TOPK, TOPK]),
                                                       steps16[:].unsqueeze(1).broadcast_to([P, 2 * TOPK, TOPK]), ALU.is_equal))
                    by_side = hot[:].rearrange("p (a s) b -> p a s b", a=2)
                    chain.link(nc.vector.tensor_tensor(by_side, by_side, top_f[:].unsqueeze(2).broadcast_to([P, 2, TOPK, TOPK]), ALU.mult))
                    chain.link(nc.vector.tensor_reduce(halves[:], by_side, axis=AX.X, op=ALU.add))

                def rows():
                    chain.link(nc.vector.scalar_tensor_tensor(row_f[:], halves[:, 0, :], float(PK), halves[:, 1, :], ALU.mult, ALU.add))
                    nc.vector.tensor_copy(idx_all[:, bass.ds(slot * TOPK, TOPK)], row_f[:]).then_inc(idx_full, 1)
                    assert chain.n == TK, chain.n
                    nc.vector.tensor_scalar(negbest[:], best[:, 0:1], -1.0, None, ALU.mult).then_inc(best_full, 1)

                return keys(0), keys(1), pairs, best_pairs, unpair, rows

            def gates(k, slot):
                dve.wait_ge(gexp_full, k + 1)
                nc.vector.reciprocal(gsum[:], gsum[:]).then_inc(gate_link, 1)
                dve.wait_ge(gate_link, k + 1)
                nc.vector.tensor_scalar(gates_all[:, bass.ds(slot * TOPK, TOPK)], gexp[:], gsum[:, 0:1], None,
                                        ALU.mult).then_inc(gates_full, 1)

            def rstd_of(at, rooted, link, n):
                dve.wait_ge(rooted, n + 1)
                nc.vector.reciprocal(stat[:, at:at + 1], stat[:, at:at + 1]).then_inc(link, 1)
                dve.wait_ge(link, n + 1)

            def prepare(t):
                rstd_of(0, pre_root, pre_link, t)
                nc.vector.scalar_tensor_tensor(norm[:], h_next[:], stat[:, 0:1], gain_row[:], ALU.mult, ALU.mult).then_inc(norm_full, 1)

            def copy_rows(dst, b, slot, full):
                nc.vector.tensor_copy(dst[:, b, :], idx_all[:, bass.ds(slot * TOPK, TOPK)]).then_inc(full, 1)

            def begin():
                dve.sem_inc(u_free, RING)
                dve.sem_inc(sum_read, 2)
                dve.wait_ge(small_in, 32)
                dve.wait_ge(iota_done, 1)
                prepare(0)
                for k in range(AHEAD):
                    for step in retrieval(k, k):
                        step()
                    if k < AHEAD - 1:
                        gates(k, k + 1)
                dve.wait_ge(idx_full, 1)
                copy_rows(idx_u, 0, 0, iu_full)

            def weigh(g, slot, odd):
                dve.wait_ge(gelu_full, g + 1)
                dve.wait_ge(gates_full, g + 1)
                nc.vector.tensor_tensor(weights[:, odd, :], dots[:, odd, :], gates_all[:, bass.ds(slot * TOPK, TOPK)],
                                        ALU.mult).then_inc(weights_full, 1)

            def add_sum(g, h, odd):
                dve.wait_ge(v_free, g * TOPK + (TOPK + RING))
                dve.wait_ge(sum_read, g + 2)
                src, dst = (h_next, h_sum) if h == 2 else (h_sum, h_out) if h == 1 else (h_sum, h_sum)
                return nc.vector.tensor_tensor(dst[:], sum_ps[odd], src[:], ALU.add)

            def finish_sum(t, g, odd):
                dve.wait_ge(stored, t * 16)
                add_sum(g, 1, odd).then_inc(fin_sum, 1)
                dve.wait_ge(fin_sum, t + 1)
                dve.sem_inc(sum_read, 1)

            def finish_norm(t):
                rstd_of(1, fin_root, fin_link, t)
                nc.vector.tensor_scalar(norm[:], h_out[:], stat[:, 1:2], None, ALU.mult).then_inc(fin_norm, 1)

            def finish_copy(t, half):
                dve.wait_ge(fin_turned, t * 2 + (half + 1))
                nc.vector.tensor_tensor(fT[:, half * 4:half * 4 + 4, :], misc_ps.rearrange("p (c n) -> p c n", n=P),
                                        gT[:, half * 4:half * 4 + 4].unsqueeze(2).broadcast_to([P, 4, P]), ALU.mult).then_inc(fin_copied, 1)

            def finish_half(t, half):
                dve.wait_ge(ple_full, t * 2 + (half + 1))
                nc.vector.tensor_tensor(gate[:], misc_ps, gate[:], ALU.mult).then_inc(fin_mul, 1)
                dve.wait_ge(fin_mul, t * 2 + (half + 1))
                part = h_out[:, half * 512:(half + 1) * 512]
                nc.vector.tensor_tensor(part, part, gate[:], ALU.add).then_inc(fin_done, 1)

            def group(g, t, h, v=False, add=True, topk=False, finish=False, prepare=False, odd=None, final_topk=False):
                runtime = odd is not None
                odd = h % 2 if odd is None else odd
                if topk:
                    ks = retrieval(g + AHEAD, (h + AHEAD) % PH if not runtime else h - 3)
                if not runtime and h == 0:
                    dve.wait_ge(u_free, g * TOPK + RING)
                    nc.vector.scalar_tensor_tensor(un[:], h_next[:], stat[:, 0:1], gain_row[:], ALU.mult, ALU.mult).then_inc(un_taken, 1)
                    dve.wait_ge(un_taken, t + 1)
                for s in range(TOPK):
                    dve.wait_ge(u_in[s % RING], g * 64 + 16 * (s // RING + 1))
                    row = u_ring[:, s % RING, :]
                    nc.vector.tensor_tensor_reduce(out=row, in0=row, in1=un[:], scale=1.0, scalar=0.0, op0=ALU.mult, op1=ALU.add,
                                                   accum_out=dots[:, odd, s:s + 1]).then_inc(u_free, 1)
                    if s == 0 and v:
                        weigh(g - 1, h, 1 - odd)
                    if s == 1 and add:
                        if finish:
                            finish_sum(t - 1, g - 2, odd)
                        else:
                            add_sum(g - 2, h if not runtime else 3, odd).then_inc(sum_read, 1)
                    if s == 3:
                        copy_rows(idx_v, odd, h, iv_full)
                    if s == 4 and (topk or runtime or h < 7):
                        dve.wait_ge(idx_full, g + 2)
                        copy_rows(idx_u, 1 - odd, (h + 1) % PH if not runtime else h + 1, iu_full)
                    if topk and 7 <= s <= 12:
                        ks[s - 7]()
                    if topk and s == 5:
                        gates(g + AHEAD - 1, h - 3 if runtime else (h + AHEAD) % PH)
                    if final_topk and s == 15:
                        gates(g + AHEAD, (h + AHEAD + 1) % PH)
                    if finish and s == 4:
                        finish_norm(t - 1)
                    if finish and s in (6, 7):
                        finish_copy(t - 1, s - 6)
                    if finish and s in (11, 14):
                        finish_half(t - 1, s // 14)
                    if prepare and s == 10:
                        prepare_dve(t + 1)

            def tail(g):
                weigh(g - 1, 0, 1)
                add_sum(g - 2, 0, 0).then_inc(sum_read, 1)
                finish_sum(TILES - 1, g - 1, 1)
                finish_norm(TILES - 1)
                for half in range(2):
                    finish_copy(TILES - 1, half)
                for half in range(2):
                    finish_half(TILES - 1, half)

            prepare_dve = prepare
            schedule(dve, begin, group, tail)

        @block.tensor
        def _(pe):
            def prepare(t, begins=False):
                if not begins:
                    pe.wait_ge(fin_mul, (t - 1) * 2)
                for half in range(2):
                    pe.wait_ge(norm_full, t + 1)
                    if half:
                        pe.wait_ge(uT_full, t * 2 + 1)
                    for c in range(4):
                        last = nc.tensor.transpose(misc_ps[:, c * P:(c + 1) * P], norm[:, (half * 4 + c) * P:(half * 4 + c + 1) * P],
                                                   core.ident[:])
                    last.then_inc(pre_turned, 1)

            def query(k, slot, t):
                pe.wait_ge(uT_full, t * 2 + 2)
                pe.wait_ge(q_copied, k)
                for c in range(DCH):
                    last = nc.tensor.matmul(q_ps[:, 0:PKD], uT[:, c, :], wq[:, c, bass.ds(slot * PKD, PKD)],
                                            start=(c == 0), stop=(c == DCH - 1))
                last.then_inc(q_full, 1)

            def turn_query(k):
                pe.wait_ge(q_copied, k + 1)
                for side in range(2):
                    last = nc.tensor.transpose(qT_ps[:, side * P:(side + 1) * P], q[:, side * P:(side + 1) * P], core.ident[:])
                last.then_inc(qT_full, 1)

            def scores(k, slot):
                pe.wait_ge(qT_copied, k + 1)
                pe.wait_ge(idx_full, k)
                for side in range(2):
                    last = nc.tensor.matmul(score_ps[:, side * PK:(side + 1) * PK], qT[:, side * P:(side + 1) * P],
                                            skT[:, bass.ds(slot * 2 + side, 1), :].rearrange("p o k -> p (o k)"), start=True, stop=True)
                last.then_inc(score_full, 1)

            def begin():
                pe.sem_inc(v_free, RING)
                pe.wait_ge(sub_in, 16)
                for j in range(4):
                    for a in range(4):
                        last = nc.tensor.transpose(ps[:, j, a * P:(a + 1) * P],
                                                   wg[:, 0:2, :].rearrange("p c (a d) -> p (c a) d", d=P)[:, 4 * j + a, :], core.ident[:])
                    last.then_inc(sub_turned, 1)
                prepare(0, begins=True)
                pe.wait_ge(wq_in, 16)
                pe.wait_ge(sub_copied, 4)
                for k in range(AHEAD):
                    query(k, k, 0)
                    turn_query(k)
                    scores(k, k)

            def values(g, s, odd):
                if s == 0:
                    pe.wait_ge(sum_read, g + 1)
                pe.wait_ge(diag_full, g * TOPK + (s + 1))
                pe.wait_ge(v_in[s % RING], g * 64 + 16 * (s // RING + 1))
                for half in range(2):
                    last = nc.tensor.matmul(sum_ps[odd][:, half * 512:(half + 1) * 512], diag[:, s % RING, :],
                                            v_ring[:, s % RING, half * 512:(half + 1) * 512], start=(s == 0), stop=(s == TOPK - 1))
                last.then_inc(v_free, 1)

            def turn_p(t):
                pe.wait_ge(p_in, t * 16 + 16)
                pe.wait_ge(fin_mul, t * 2)
                for c in range(PLE // P):
                    last = nc.tensor.transpose(misc_ps[:, c * P:(c + 1) * P], ptok[:, c * P:(c + 1) * P], core.ident[:])
                last.then_inc(p_turned, 1)

            def finish_turn(t, half):
                pe.wait_ge(fin_norm, t + 1)
                if half:
                    pe.wait_ge(fin_copied, t * 2 + 1)
                else:
                    pe.wait_ge(p_copied, t + 2)
                for c in range(4):
                    last = nc.tensor.transpose(misc_ps[:, c * P:(c + 1) * P], norm[:, (half * 4 + c) * P:(half * 4 + c + 1) * P],
                                               core.ident[:])
                last.then_inc(fin_turned, 1)

            def gate_half(t, half):
                pe.wait_ge(wg_in, 32)
                pe.wait_ge(fin_copied, t * 2 + 2)
                if half:
                    pe.wait_ge(fin_mul, t * 2 + 1)
                for c in range(DCH):
                    last = nc.tensor.matmul(misc_ps, fT[:, c, :], wg[:, c, half * 512:(half + 1) * 512], start=(c == 0), stop=(c == DCH - 1))
                last.then_inc(gate_full, 1)

            def ple_half(t, half):
                pe.wait_ge(gate_copied, t * 2 + (half + 1))
                for c in range(PLE // P):
                    last = nc.tensor.matmul(misc_ps, pT[:, c, :], wp[:, c, half * 512:(half + 1) * 512], start=(c == 0), stop=(c == PLE // P - 1))
                last.then_inc(ple_full, 1)

            prepare_pe = prepare

            def group(g, t, h, v=False, add=True, topk=False, finish=False, prepare=False, odd=None, final_topk=False):
                runtime = odd is not None
                odd = h % 2 if odd is None else odd
                slot = (h + AHEAD) % PH if not runtime else h - 3
                late = runtime or h + AHEAD >= PH
                for s in range(TOPK):
                    if v:
                        values(g - 1, s, 1 - odd)
                    if topk and s == 1:
                        query(g + AHEAD, slot, t + 1 if late else t)
                    if topk and s == 3:
                        turn_query(g + AHEAD)
                    if topk and s == 5:
                        scores(g + AHEAD, slot)
                    if finish and s == 0:
                        turn_p(t - 1)
                    if finish and s in (5, 6):
                        finish_turn(t - 1, s - 5)
                    if finish and s in (8, 11):
                        gate_half(t - 1, s // 11)
                    if finish and s in (9, 12):
                        ple_half(t - 1, s // 12)
                    if prepare and s == 12:
                        prepare_pe(t + 1)

            def tail(g):
                for s in range(TOPK):
                    values(g - 1, s, 1)
                turn_p(TILES - 1)
                for half in range(2):
                    finish_turn(TILES - 1, half)
                for half in range(2):
                    gate_half(TILES - 1, half)
                    ple_half(TILES - 1, half)

            schedule(pe, begin, group, tail)


def store_stream(nc, core, hd):
    with ExitStack() as ctx:
        ph = Phase(nc, ctx, "store")
        done = ph.sem("done")
        block = ph.open_block()

        @block.sync
        def _(sp):
            for t in range(TILES):
                sp.dma_start(hd[t * P:(t + 1) * P, :], core.h[:, t, :]).then_inc(done, 16)
            sp.wait_ge(done, 16 * TILES)


def build(nc, io, out):
    hd = nc.dram_tensor("stream", (SEQ, D), F32, kind="Internal").ap()
    with ExitStack() as ctx:
        core = Core(nc, ctx)
        with ExitStack() as mixers:
            core.h = mixers.enter_context(nc.sbuf_tensor("h", [P, TILES, D], F32))
            uT = mixers.enter_context(nc.sbuf_tensor("uT", [P, DCH, SEQ], F32))
            normalise_input(nc, core, uT, io["x"][0], io["mix_norm"][0])
            with ExitStack() as pair:
                y = pair.enter_context(nc.sbuf_tensor("y", [P, TILES, A_WIDTH], F32))
                mixer_a(nc, core, uT, y, io)
                mixer_c(nc, core, uT, y, io)
            mixer_b(nc, core, uT, io)
            store_stream(nc, core, hd)
        peer_and_gate(nc, core, hd, out[0], io)


_INS = ["x", "p", "mix_norm", "w_in", "a_q_norm", "a_k_norm", "a_sinks", "a_out_norm", "b_conv_w", "b_conv_b", "b_dt_bias",
        "b_a_log", "b_d", "b_out_norm", "c_q_norm", "c_k_norm", "c_rel_bias", "c_out_norm", "w_out", "ffn_norm",
        "peer_w_query", "peer_sub_keys", "peer_u", "peer_v", "ple_norm", "ple_w_gate", "ple_w_proj"]


def kernel(**inputs):
    import concourse.bacc as bacc
    from concourse.bass_utils import run_bass_kernel_spmd

    nc = bacc.Bacc("TRN2", target_bir_lowering=False, num_devices=1)
    arrays = {name: np.ascontiguousarray(inputs[name]) for name in _INS}
    io = {name: nc.dram_tensor(name, a.shape, mybir.dt.from_np(a.dtype), kind="ExternalInput").ap() for name, a in arrays.items()}
    out = nc.dram_tensor("out", (1, SEQ, D), F32, kind="ExternalOutput").ap()
    build(nc, io, out)
    r = run_bass_kernel_spmd(nc, [arrays], core_ids=[0])
    return r.results[0]["out"]
```

```python
from contextlib import ExitStack

import numpy as np
import concourse.bass as bass
from concourse import mybir

F32 = mybir.dt.float32
U32 = mybir.dt.uint32
ALU = mybir.AluOpType
ACT = mybir.ActivationFunctionType
AX = mybir.AxisListType

P = 128
SEQ, D = 1024, 1024
TILES = SEQ // P
DCH = D // P
CHUNK, HD = 64, 64
EPS = 1e-6
NEG = -1e30
A_HEADS, A_KV = 8, 2
A_WIDTH, A_QKV = 512, 768
B_WIDTH, B_HEADS, B_GROUPS, B_STATE, B_CONV = 1024, 16, 2, 128, 4
B_XBC = B_WIDTH + 2 * B_GROUPS * B_STATE
B_IN = B_WIDTH + B_XBC + B_HEADS
C_HEADS, C_WIDTH = 8, 512
C_PASS = 4
REL_FUTURE, REL_PAST = 63, 256
REL_SIZE = REL_FUTURE + REL_PAST + 1
PLE = 256
PH, PK, PKD, TOPK = 8, 128, 256, 16
SEL = PH * TOPK


class Chain:

    def __init__(self, eng, sem, base=0):
        self.eng, self.sem, self.base, self.n = eng, sem, base, 0

    def link(self, ins):
        self.n += 1
        ins.then_inc(self.sem, 1)
        self.eng.wait_ge(self.sem, self.base + self.n)


class Core:

    def __init__(self, nc, ctx):
        self.nc = nc
        self.h = None
        self.ident = ctx.enter_context(nc.sbuf_tensor("ident", [P, P], F32))
        self.eps = ctx.enter_context(nc.sbuf_tensor("eps", [P, 1], F32))
        self.ps = ctx.enter_context(nc.psum_tensor("ps", [P, 8, 512], F32))


class Phase:

    def __init__(self, nc, ctx, tag):
        self.nc, self.ctx, self.tag, self.used = nc, ctx, tag, []

    def sb(self, name, shape, dt=F32):
        return self.ctx.enter_context(self.nc.sbuf_tensor(f"{self.tag}_{name}", shape, dt))

    def sem(self, name):
        self.used.append(self.ctx.enter_context(self.nc.semaphore(f"{self.tag}_{name}")))
        return self.used[-1]

    def open_block(self):
        self.ctx.callback(self.clear)
        return self.ctx.enter_context(self.nc.Block())

    def clear(self):
        numbers = sorted(s.num for s in self.used)
        starts = [n for n in numbers if n - 1 not in numbers]
        ends = [n + 1 for n in numbers if n + 1 not in numbers]
        for start, end in zip(starts, ends):
            self.nc.sync.sem_clear(range(start, end))
        self.nc.all_engine_barrier()

    def sems(self, names):
        return [self.sem(n) for n in names.split()]


def normalise_input(nc, core, uT, x, gain):
    with ExitStack() as ctx:
        ph = Phase(nc, ctx, "in")
        xn = ph.sb("xn", [P, 2, D])
        gT = ph.sb("gT", [P, DCH])
        rstd = ph.sb("rstd", [P, TILES])
        scratch = ph.sb("scratch", [P, D])
        loaded = [ph.sem(f"x{t}_in") for t in range(TILES)]
        small_in, consts, squares, rooted, rstd_ready, xn_full, t_full, t_free = ph.sems(
            "small_in consts squares rooted rstd_ready xn_full t_full t_free")
        block = ph.open_block()
        h, ps, ident = core.h, core.ps, core.ident

        @block.sync
        def _(sp):
            for t in range(TILES):
                sp.dma_start(h[:, t, :], x[t * P:(t + 1) * P, :]).then_inc(loaded[t], 16)
                if t == 0:
                    sp.dma_start(gT[:], gain.rearrange("(c p) -> p c", p=P), allow_slow_non_contiguous=True).then_inc(small_in, 16)

        @block.gpsimd
        def _(pool):
            nc.gpsimd.memset(ident[:], 0.0).then_inc(consts, 1)
            nc.gpsimd.memset(core.eps[:], EPS).then_inc(consts, 1)
            pool.wait_ge(consts, 2)
            nc.gpsimd.affine_select(out=ident[:], in_=ident[:], compare_op=ALU.not_equal, fill=1.0, base=0,
                                    pattern=[[-1, P]], channel_multiplier=1).then_inc(consts, 1)

        @block.scalar
        def _(act):
            act.wait_ge(consts, 3)
            for t in range(TILES):
                act.wait_ge(loaded[t], 16)
                nc.scalar.activation(scratch[:], h[:, t, :], ACT.Square, accum_out=rstd[:, t:t + 1]).then_inc(squares, 1)
                act.wait_ge(squares, t + 1)
                nc.scalar.activation(rstd[:, t:t + 1], rstd[:, t:t + 1], ACT.Sqrt, bias=core.eps[:, 0:1],
                                     scale=1.0 / D).then_inc(rooted, 1)

        @block.vector
        def _(dve):
            def normalise(t):
                dve.wait_ge(rooted, t + 1)
                dve.wait_ge(loaded[t], 16)
                nc.vector.reciprocal(rstd[:, t:t + 1], rstd[:, t:t + 1]).then_inc(rstd_ready, 1)
                dve.wait_ge(rstd_ready, t + 1)
                if t >= 2:
                    dve.wait_ge(t_full, t - 1)
                nc.vector.tensor_scalar(xn[:, t % 2, :], h[:, t, :], rstd[:, t:t + 1], None, ALU.mult).then_inc(xn_full, 1)

            dve.wait_ge(small_in, 16)
            normalise(0)
            for t in range(TILES):
                if t + 1 < TILES:
                    normalise(t + 1)
                b = t % 2
                dve.wait_ge(t_full, t + 1)
                nc.vector.tensor_tensor(uT[:, :, t * P:(t + 1) * P],
                                        ps[:, 2 * b:2 * b + 2, :].rearrange("p k (c n) -> p (k c) n", n=P),
                                        gT[:].unsqueeze(2).broadcast_to([P, DCH, P]), ALU.mult).then_inc(t_free, 1)

        @block.tensor
        def _(pe):
            pe.wait_ge(consts, 3)
            for t in range(TILES):
                pe.wait_ge(xn_full, t + 1)
                if t >= 2:
                    pe.wait_ge(t_free, t - 1)
                transpose_row(nc, core, ps[:, 2 * (t % 2):2 * (t % 2) + 2, :], xn[:, t % 2, :], DCH).then_inc(t_full, 1)


def pipeline(eng, begin, step):
    begin()
    with eng.Fori(0, (TILES - 2) // 2) as i:
        for b in range(2):
            step(i * 2 + b, b, True, True)
    step(TILES - 2, 0, False, True)
    step(TILES - 1, 1, False, False)


def transpose_row(nc, core, out, src, n):
    flat = out.rearrange("p k (c n) -> p (k c) n", n=P)
    for c in range(n):
        last = nc.tensor.transpose(flat[:, c, :], src[:, c * P:(c + 1) * P], core.ident[:])
    return last


def attention(nc, core, uT, y, ycol, tag, weights, nq, nkv, ktiles, gains, sinks, rel_bias):
    wq, wk, wv = nq * HD, nkv * HD, nkv * HD
    nqk, width, keys = nq + nkv, wq + wk + wv, ktiles * P
    pad = (ktiles - 1) * P
    s_banks = (keys + 511) // 512
    t_banks = (nq * P + 511) // 512
    units = nq * ktiles // 4
    per_unit = -(-nq // units)
    bank_q, bank_k = 0, t_banks
    bank_s = [bank_k + 1, bank_k + 1 + s_banks]
    bank_p = bank_k + 1 + 2 * s_banks
    assert bank_p + 2 <= 8
    n_neg = 2 if sinks is not None else 1

    window = keys - P

    def last_head(u):
        return (4 * u + 3) // ktiles

    with ExitStack() as ctx:
        ph = Phase(nc, ctx, tag)
        w = ph.sb("w", [P, DCH, width])
        qk = ph.sb("qk", [P, TILES, nqk * HD])
        v = ph.sb("v", [P, ktiles - 1 + TILES, wv])
        sq = ph.sb("sq", [P, 2, nqk * HD])
        rstd = ph.sb("rstd", [P, TILES * nqk])
        gain = ph.sb("gain", [HD, 2])
        bias = ph.sb("bias", [P, nq, keys])
        kT = ph.sb("kT", [HD + 1, nkv, pad + SEQ])
        qT = ph.sb("qT", [HD + 1, nq * P])
        qkn = ph.sb("qkn", [P, nqk * HD])
        logits = ph.sb("logits", [P, 2, nq, keys])
        rowmax = ph.sb("rowmax", [P, nq])
        negmax = ph.sb("negmax", [P, nq])
        rowsum = ph.sb("rowsum", [P, nq])
        sink = ph.sb("sink", [P, nq])
        sinkexp = ph.sb("sinkexp", [P, nq])
        inv = ph.sb("inv", [P, nq])
        pT = ph.sb("pT", [P, 2, 4, P])
        w_in_ = [ph.sem(f"w{c}_in") for c in range(0, DCH, 2)]
        (small_in, row_in, skew_out, bias_in, consts, made, bias_ready,
         proj_full, proj_free, sq_full, sq_free, v_full, rooted, rstd_ready,
         qkn_full, turned, qT_full, kT_full, s_full, s_free, neg_ready, p_full, sink_full,
         pt_full, pt_copied, pt_used, o_full, o_free, link, held) = ph.sems(
            "small_in row_in skew_out bias_in consts made bias_ready "
            "proj_full proj_free sq_full sq_free v_full rooted rstd_ready "
            "qkn_full turned qT_full kT_full s_full s_free neg_ready p_full sink_full "
            "pt_full pt_copied pt_used o_full o_free link held")
        ps = core.ps
        n_small = 2 + (1 if sinks is not None else 0)
        if rel_bias is not None:
            pitch = keys + P
            head_row = ph.sb("relrow", [nq, REL_SIZE])
            ext = ph.sb("ext", [nq, pitch])
            skew = nc.dram_tensor(f"{tag}_skew", (nq, P * pitch), F32, kind="Internal").ap()
        block = ph.open_block()

        @block.sync
        def _(sp):
            if rel_bias is not None:
                sp.dma_start(head_row[:], rel_bias).then_inc(row_in, 16)
            for c in range(0, DCH, 2):
                at = 0
                for cols, n in zip(weights, (wq, wk, wv)):
                    sp.dma_start(w[:, c:c + 2, at:at + n],
                                 cols[c * P:(c + 2) * P].rearrange("(c p) n -> p c n", p=P)).then_inc(w_in_[c // 2], 16)
                    at += n
            for j in range(2):
                sp.dma_start(gain[:, j:j + 1], gains[j].rearrange("(p o) -> p o", o=1)).then_inc(small_in, 16)
            if sinks is not None:
                sp.dma_start(sink[:], sinks.partition_broadcast(P)).then_inc(small_in, 16)
            if rel_bias is not None:
                sp.wait_ge(made, 2)
                for i in range(nq):
                    sp.dma_start(skew[i:i + 1, :].rearrange("o (q m) -> o q m", q=P),
                                 ext[i:i + 1, :].unsqueeze(1).broadcast_to([1, P, pitch])).then_inc(skew_out, 16)
                sp.wait_ge(skew_out, 16 * nq)
                for i in range(nq):
                    rows = skew[i, P - 1:P - 1 + P * (pitch - 1)].rearrange("(q m) -> q m", q=P)
                    sp.dma_start(bias[:, i, :], rows[:, 0:keys]).then_inc(bias_in, 16)
                sp.wait_ge(bias_in, 16 * nq)

        @block.gpsimd
        def _(pool):
            fill = Chain(pool, consts)
            fill.link(nc.gpsimd.memset(kT[0:HD, :, 0:pad], 0.0))
            fill.link(nc.gpsimd.memset(v[:, 0:ktiles - 1, :], 0.0))
            fill.link(nc.gpsimd.memset(kT[HD:HD + 1, :, 0:pad], NEG))
            fill.link(nc.gpsimd.memset(kT[HD:HD + 1, :, pad:], 0.0))
            fill.link(nc.gpsimd.memset(qT[HD:HD + 1, :], 1.0))
            if rel_bias is None:
                pool.iota(bias[:, 0, :], pattern=[[-1, keys]], base=window, channel_multiplier=1,
                          allow_small_or_imprecise_dtypes=True).then_inc(made, 1)

        @block.scalar
        def _(act):
            def root(t):
                act.wait_ge(sq_free, t + 3)
                part = rstd[:, t * nqk:(t + 1) * nqk]
                nc.scalar.activation(part, part, ACT.Sqrt, bias=core.eps[:, 0:1], scale=1.0 / HD).then_inc(rooted, 1)

            for t in range(TILES):
                act.wait_ge(proj_full, t + 1)
                src = ps[:, 2 * (t % 4):2 * (t % 4) + 2, :].rearrange("p k n -> p (k n)")
                nc.scalar.activation(qk[:, t, :], src[:, 0:nqk * HD], ACT.Copy).then_inc(proj_free, 1)
                act.wait_ge(sq_free, t + 1)
                nc.scalar.activation(sq[:, t % 2, :], src[:, 0:nqk * HD], ACT.Square).then_inc(sq_full, 1)
                if t:
                    root(t - 1)
            root(TILES - 1)
            act.wait_ge(small_in, 16 * n_small)
            act.wait_ge(consts, 5)
            def copy_turned(t):
                act.wait_ge(turned, t + 1)
                nc.scalar.activation(qT[0:HD, :], ps[0:HD, bank_q:bank_q + t_banks, :].rearrange("p k n -> p (k n)")[:, 0:nq * P],
                                     ACT.Copy, scale=gain[:, 0:1]).then_inc(qT_full, 1)
                nc.scalar.activation(kT[0:HD, :, bass.ds(t * P + pad, P)],
                                     ps[0:HD, bank_k, 0:nkv * P].rearrange("p (k n) -> p k n", n=P),
                                     ACT.Copy, scale=gain[:, 1:2]).then_inc(kT_full, 1)

            def exponentials(par, heads):
                for i in heads:
                    nc.scalar.activation(logits[:, par, i, :], logits[:, par, i, :], ACT.Exp, bias=negmax[:, i:i + 1],
                                         accum_out=rowsum[:, i:i + 1]).then_inc(p_full, 1)

            def step(t, par, normalise, scores):
                act.wait_ge(neg_ready, t * n_neg + n_neg)
                early = last_head(1) + 1
                exponentials(par, range(early))
                if scores:
                    copy_turned(t + 1)
                exponentials(par, range(early, nq))
                if sinks is not None:
                    nc.scalar.activation(sinkexp[:], sinkexp[:], ACT.Exp).then_inc(sink_full, 1)
                for u in range(units):
                    n = (par * units + u) % 2
                    act.wait_ge(pt_full, t * units + (u + 1))
                    act.wait_ge(pt_used, t * units + (u + 1))
                    nc.scalar.activation(pT[:, n].rearrange("p k n -> p (k n)"), ps[:, bank_p + n, :], ACT.Copy).then_inc(pt_copied, 1)

            act.sem_inc(pt_copied, 2)
            pipeline(act, lambda: copy_turned(0), step)

        @block.vector
        def _(dve):
            dve.sem_inc(sq_free, 2)
            dve.sem_inc(s_free, 2)
            dve.sem_inc(o_free, 2)
            once = Chain(dve, bias_ready)

            def extend_rows():
                dve.wait_ge(row_in, 16)
                far = window + P - 1 - REL_PAST
                ext_rev = ext[:, far:far + REL_SIZE]
                nc.vector.tensor_copy(ext_rev, head_row[:, ::-1]).then_inc(made, 1)
                dve.wait_ge(made, 1)
                once.link(nc.vector.tensor_scalar(ext[:, 0:far], head_row[:, REL_SIZE - 1:REL_SIZE].broadcast_to([nq, far]), 1.0, None, ALU.mult))
                nc.vector.tensor_scalar(ext[:, far + REL_SIZE:], head_row[:, 0:1].broadcast_to([nq, pitch - far - REL_SIZE]),
                                        1.0, None, ALU.mult).then_inc(made, 1)

            def make_bias():
                if rel_bias is None:
                    dve.wait_ge(made, 1)
                    once.link(nc.vector.tensor_scalar(bias[:, 1, :], bias[:, 0, :], -1.0, None, ALU.mult))
                    once.link(nc.vector.tensor_tensor(bias[:, 0, :], bias[:, 0, :], bias[:, 1, :], ALU.max))
                    for i in reversed(range(nq)):
                        slope = float(np.float32(2.0 ** (-8.0 * (i + 1) / nq)))
                        once.link(nc.vector.tensor_scalar(bias[:, i, :], bias[:, 0, :], -slope / HD ** -0.5, None, ALU.mult))
                else:
                    dve.wait_ge(bias_in, 16 * nq)
                    flat = bias[:].rearrange("p h k -> p (h k)")
                    once.link(nc.vector.tensor_scalar(flat, flat, HD ** 0.5, None, ALU.mult))
                early, late = bias[0:CHUNK], bias[CHUNK:P]
                once.link(nc.vector.memset(early[:, :, keys - CHUNK:keys], NEG))
                if rel_bias is None:
                    once.link(nc.vector.memset(early[:, :, 0:CHUNK], NEG))
                    once.link(nc.vector.memset(late[:, :, 0:2 * CHUNK], NEG))
                else:
                    once.link(nc.vector.memset(late[:, :, 0:CHUNK], NEG))

            def invert(t):
                dve.wait_ge(rooted, t + 1)
                part = rstd[:, t * nqk:(t + 1) * nqk]
                nc.vector.reciprocal(part, part).then_inc(rstd_ready, 1)

            def normalise_qk(t):
                nc.vector.tensor_tensor(qkn[:].rearrange("p (h d) -> p h d", d=HD),
                                        qk[:, bass.ds(t, 1), :].rearrange("p o (h d) -> p (o h) d", d=HD),
                                        rstd[:, bass.ds(t * nqk, nqk)].unsqueeze(2).broadcast_to([P, nqk, HD]),
                                        ALU.mult).then_inc(qkn_full, 1)

            def read_scores(t, par):
                for i in range(nq):
                    dve.wait_ge(s_full, t * nq + (i + 1))
                    dve.sem_inc(held, 1)
                    b = bank_s[i % 2]
                    nc.vector.tensor_tensor_reduce(
                        out=logits[:, par, i, :], in0=ps[:, b:b + s_banks, :].rearrange("p k n -> p (k n)")[:, 0:keys],
                        in1=bias[:, i, :], scale=HD ** -0.5, scalar=sink[:, i:i + 1] if sinks is not None else NEG,
                        op0=ALU.add, op1=ALU.max, accum_out=rowmax[:, i:i + 1]).then_inc(s_free, 1)
                dve.wait_ge(s_free, t * nq + (nq + 2))
                nc.vector.tensor_scalar(negmax[:], rowmax[:], -1.0, None, ALU.mult).then_inc(neg_ready, 1)
                if sinks is not None:
                    dve.wait_ge(neg_ready, t * 2 + 1)
                    nc.vector.tensor_tensor(sinkexp[:], sink[:], negmax[:], ALU.add).then_inc(neg_ready, 1)

            def begin():
                if rel_bias is not None:
                    extend_rows()
                for t in range(TILES):
                    dve.wait_ge(sq_full, t + 1)
                    nc.vector.tensor_copy(v[:, ktiles - 1 + t, :],
                                          ps[:, 2 * (t % 4):2 * (t % 4) + 2, :].rearrange("p k n -> p (k n)")[:, nqk * HD:width]).then_inc(v_full, 1)
                    nc.vector.tensor_reduce(rstd[:, t * nqk:(t + 1) * nqk], sq[:, t % 2, :].rearrange("p (h d) -> p h d", d=HD),
                                            axis=AX.X, op=ALU.add).then_inc(sq_free, 1)
                    if t:
                        invert(t - 1)
                    if t == 1:
                        dve.wait_ge(rstd_ready, 1)
                        normalise_qk(0)
                    if t == 4:
                        make_bias()
                invert(TILES - 1)
                dve.wait_ge(small_in, 16 * n_small)
                dve.wait_ge(rstd_ready, TILES)
                dve.wait_ge(turned, 1)
                normalise_qk(1)
                read_scores(0, 0)

            def step(t, par, normalise, scores):
                if normalise:
                    dve.wait_ge(turned, t + 2)
                    normalise_qk(t + 2)
                dve.wait_ge(p_full, t * nq + nq)
                dve.wait_ge(o_free, t + 2)
                chain = Chain(dve, link, t * n_neg)
                if sinks is not None:
                    dve.wait_ge(sink_full, t + 1)
                    chain.link(nc.vector.tensor_tensor(inv[:], rowsum[:], sinkexp[:], ALU.add))
                    chain.link(nc.vector.reciprocal(inv[:], inv[:]))
                else:
                    chain.link(nc.vector.reciprocal(inv[:], rowsum[:]))
                if scores:
                    read_scores(t + 1, 1 - par)
                dve.wait_ge(o_full, t + 1)
                nc.vector.tensor_tensor(
                    y[:, bass.ds(t, 1), ycol:ycol + wq].rearrange("p o (h d) -> p (o h) d", d=HD),
                    ps[:, bank_k, 0:wq].rearrange("p (h d) -> p h d", d=HD),
                    inv[:].unsqueeze(2).broadcast_to([P, nq, HD]), ALU.mult).then_inc(o_free, 1)

            pipeline(dve, begin, step)

        @block.tensor
        def _(pe):
            for t in range(TILES):
                if t >= 4:
                    pe.wait_ge(sq_full, t - 3)
                    pe.wait_ge(proj_free, t - 3)
                    pe.wait_ge(v_full, t - 3)
                b = 2 * (t % 4)
                for lo in range(0, width, 512):
                    hi = min(lo + 512, width)
                    for c in range(DCH):
                        if t == 0 and lo == 0 and c % 2 == 0:
                            pe.wait_ge(w_in_[c // 2], 48)
                        last = nc.tensor.matmul(ps[:, b + lo // 512, 0:hi - lo], uT[:, c, t * P:(t + 1) * P],
                                                w[:, c, lo:hi], start=(c == 0), stop=(c == DCH - 1))
                last.then_inc(proj_full, 1)
            pe.wait_ge(sq_full, TILES)
            pe.wait_ge(proj_free, TILES)
            pe.wait_ge(v_full, TILES)
            pe.wait_ge(consts, 5)

            def turn(t):
                pe.wait_ge(qkn_full, t + 1)
                pe.sem_inc(held, 1)
                for i in range(nqk):
                    if i == nq:
                        pe.wait_ge(o_free, t + 1)
                        pe.sem_inc(held, 1)
                    b, col = (bank_q + i * P // 512, i * P % 512) if i < nq else (bank_k, (i - nq) * P)
                    last = nc.tensor.transpose(ps[0:HD, b, col:col + P], qkn[:, i * HD:(i + 1) * HD], core.ident[:])
                last.then_inc(turned, 1)

            def score_heads(t, heads):
                for i in heads:
                    if i == 0:
                        pe.wait_ge(qT_full, t + 1)
                        pe.wait_ge(kT_full, t + 1)
                    pe.wait_ge(s_free, t * nq + (i + 1))
                    for lo in range(0, keys, 512):
                        n = min(512, keys - lo)
                        last = nc.tensor.matmul(ps[:, bank_s[i % 2] + lo // 512, 0:n], qT[:, i * P:(i + 1) * P],
                                                kT[:, i * nkv // nq, bass.ds(t * P + lo, n)], start=True, stop=True)
                    last.then_inc(s_full, 1)

            def turn_unit(t, par, u):
                pe.wait_ge(p_full, t * nq + (last_head(u) + 1))
                pe.wait_ge(pt_copied, t * units + (u + 1))
                for j in range(4):
                    i, k = divmod(4 * u + j, ktiles)
                    last = nc.tensor.transpose(ps[:, bank_p + (par * units + u) % 2, j * P:(j + 1) * P],
                                               logits[:, par, i, k * P:(k + 1) * P], core.ident[:])
                last.then_inc(pt_full, 1)

            def multiply_unit(t, par, u):
                pe.wait_ge(pt_copied, t * units + (u + 3))
                for j in range(4):
                    i, k = divmod(4 * u + j, ktiles)
                    kv = i * nkv // nq
                    last = nc.tensor.matmul(ps[:, bank_k, i * HD:(i + 1) * HD], pT[:, (par * units + u) % 2, j, :],
                                            v[:, bass.ds(t + k, 1), kv * HD:(kv + 1) * HD].rearrange("p o d -> p (o d)"),
                                            start=(k == 0), stop=(k == ktiles - 1))
                last.then_inc(pt_used, 1)
                if u == units - 1:
                    pe.wait_ge(pt_used, t * units + (units + 2))
                    pe.sem_inc(o_full, 1)

            def begin():
                turn(0)
                score_heads(0, range(nq))

            def step(t, par, normalise, scores):
                if scores:
                    turn(t + 1)
                turn_unit(t, par, 0)
                turn_unit(t, par, 1)
                if not scores:
                    pe.wait_ge(o_free, t + 2)
                for u in range(units):
                    if scores:
                        score_heads(t + 1, range(u * per_unit, min(nq, (u + 1) * per_unit)))
                    multiply_unit(t, par, u)
                    if u + 2 < units:
                        turn_unit(t, par, u + 2)

            pe.sem_inc(pt_used, 2)
            pipeline(pe, begin, step)


def project_out(nc, core, tag, y, nch, gain, w_rows):
    with ExitStack() as ctx:
        ph = Phase(nc, ctx, tag)
        w = ph.sb("w", [P, nch, D])
        scratch = ph.sb("scratch", [P, nch * P])
        yn = ph.sb("yn", [P, 2, nch * P])
        yT = ph.sb("yT", [P, 2, nch * P])
        gT = ph.sb("gT", [P, nch])
        rstd = ph.sb("rstd", [P, TILES])
        w_in_ = [ph.sem(f"w{c}_in") for c in range(0, nch, 2)]
        held, small_in, squares, rooted, rstd_ready, yn_full, t_full, yT_full, out_full, out_free = ph.sems(
            "held small_in squares rooted rstd_ready yn_full t_full yT_full out_full out_free")
        block = ph.open_block()
        h, ps = core.h, core.ps

        @block.sync
        def _(sp):
            sp.dma_start(gT[:], gain.rearrange("(c p) -> p c", p=P), allow_slow_non_contiguous=True).then_inc(small_in, 16)
            for c in range(0, nch, 2):
                sp.dma_start(w[:, c:c + 2, :], w_rows[c * P:(c + 2) * P].rearrange("(c p) n -> p c n", p=P)).then_inc(w_in_[c // 2], 16)

        @block.scalar
        def _(act):
            with act.Fori(0, TILES // 2) as i:
                for b in range(2):
                    root = rstd[:, bass.ds(i * 2 + b, 1)]
                    nc.scalar.activation(scratch[:], y[:, bass.ds(i * 2 + b, 1), :].rearrange("p o d -> p (o d)"), ACT.Square,
                                         accum_out=root).then_inc(squares, 1)
                    act.wait_ge(squares, i * 2 + (b + 1))
                    act.sem_inc(held, 1)
                    nc.scalar.activation(root, root, ACT.Sqrt, bias=core.eps[:, 0:1], scale=1.0 / (nch * P)).then_inc(rooted, 1)

        @block.vector
        def _(dve):
            def normalise(t, b):
                dve.wait_ge(rooted, t + 1)
                nc.vector.reciprocal(rstd[:, bass.ds(t, 1)], rstd[:, bass.ds(t, 1)]).then_inc(rstd_ready, 1)
                dve.wait_ge(rstd_ready, t + 1)
                nc.vector.tensor_scalar(yn[:, b, :], y[:, bass.ds(t, 1), :].rearrange("p o d -> p (o d)"),
                                        rstd[:, bass.ds(t, 1)], None, ALU.mult).then_inc(yn_full, 1)

            def scale(t, b):
                dve.wait_ge(t_full, t + 1)
                nc.vector.tensor_tensor(
                    yT[:, b, :].rearrange("p (c n) -> p c n", n=P),
                    ps[:, 2 * b:2 * b + 2, :].rearrange("p k (c n) -> p (k c) n", n=P)[:, 0:nch, :],
                    gT[:].unsqueeze(2).broadcast_to([P, nch, P]), ALU.mult).then_inc(yT_full, 1)

            def add(t, b):
                dve.wait_ge(out_full, t + 1)
                row = h[:, bass.ds(t, 1), :].rearrange("p o d -> p (o d)")
                nc.vector.tensor_tensor(row, ps[:, 4 + 2 * b:6 + 2 * b, :].rearrange("p k n -> p (k n)"), row,
                                        ALU.add).then_inc(out_free, 1)

            dve.sem_inc(out_free, 2)
            dve.wait_ge(small_in, 16)
            normalise(0, 0)
            normalise(1, 1)
            scale(0, 0)
            with dve.Fori(0, TILES // 2 - 1) as i:
                for b in range(2):
                    scale(i * 2 + (b + 1), 1 - b)
                    normalise(i * 2 + (b + 2), b)
                    add(i * 2 + b, b)
            scale(TILES - 1, 1)
            add(TILES - 2, 0)
            add(TILES - 1, 1)

        @block.tensor
        def _(pe):
            def turn(t, b):
                pe.wait_ge(yn_full, t + 1)
                for c in range(nch):
                    last = nc.tensor.transpose(ps[:, 2 * b + c // 4, c % 4 * P:(c % 4 + 1) * P],
                                               yn[:, b, c * P:(c + 1) * P], core.ident[:])
                last.then_inc(t_full, 1)

            def multiply(t, b, weights_in=False):
                pe.wait_ge(yT_full, t + 1)
                pe.wait_ge(out_free, t + 1)
                for half in range(2):
                    for c in range(nch):
                        if weights_in and half == 0 and c % 2 == 0:
                            pe.wait_ge(w_in_[c // 2], 16)
                        last = nc.tensor.matmul(ps[:, 4 + 2 * b + half, :], yT[:, b, c * P:(c + 1) * P],
                                                w[:, c, half * 512:(half + 1) * 512], start=(c == 0), stop=(c == nch - 1))
                last.then_inc(out_full, 1)

            turn(0, 0)
            turn(1, 1)
            multiply(0, 0, weights_in=True)
            with pe.Fori(0, TILES // 2 - 1) as i:
                for b in range(2):
                    turn(i * 2 + (b + 2), b)
                    multiply(i * 2 + (b + 1), 1 - b)
            multiply(TILES - 1, 1)


def mixer_a(nc, core, uT, y, io):
    w = io["w_in"][0]
    kcol, vcol = A_WIDTH, A_WIDTH + A_KV * HD
    attention(nc, core, uT, y, 0, "a", [w[:, 0:kcol], w[:, kcol:vcol], w[:, vcol:A_QKV]], A_HEADS, A_KV, 2,
              [io["a_q_norm"][0], io["a_k_norm"][0]], io["a_sinks"][0], None)
    project_out(nc, core, "aout", y, A_WIDTH // P, io["a_out_norm"][0], io["w_out"][0, 0:A_WIDTH, :])


def mixer_c(nc, core, uT, y, io):
    w = io["w_in"][0]
    for part in range(C_HEADS // C_PASS):
        n = C_PASS * HD
        at = A_QKV + B_IN + part * n
        attention(nc, core, uT, y, part * n, f"c{part}", [w[:, at + j * C_WIDTH:at + j * C_WIDTH + n] for j in range(3)],
                  C_PASS, C_PASS, 5, [io["c_q_norm"][0], io["c_k_norm"][0]], None,
                  io["c_rel_bias"][0, part * C_PASS:(part + 1) * C_PASS, :])
    project_out(nc, core, "cout", y, C_WIDTH // P, io["c_out_norm"][0], io["w_out"][0, A_WIDTH + B_WIDTH:, :])


class ScanTables:

    def __init__(self, nc, ctx):
        sb = lambda name, shape: ctx.enter_context(nc.sbuf_tensor(f"b_{name}", shape, F32))
        HB = TILES * B_HEADS
        self.rows = sb("rows", [P, 3, B_HEADS])
        self.dt = sb("dt", [P, HB])
        self.cs = sb("cs", [P, HB])
        self.from_start = sb("from_start", [P, HB])
        self.to_end = sb("to_end", [P, HB])
        self.whole = sb("whole", [P, HB])
        self.tri = sb("tri", [P, P])
        self.cs_rows = nc.dram_tensor("b_cs_rows", (HB, P), F32, kind="Internal").ap()


def mixer_b_project(nc, core, uT, z, xbc, tab, io):
    HB = TILES * B_HEADS
    zcol = A_QKV
    xcol = zcol + B_WIDTH
    dcol = xcol + B_XBC
    XCH = B_XBC // P
    w_in = io["w_in"][0]
    slabs = [zcol, zcol + 512, xcol, xcol + 512, xcol + 1024]
    with ExitStack() as ctx:
        ph = Phase(nc, ctx, "bp")
        w = ph.sb("w", [P, 2, DCH, 512])
        wdt = ph.sb("wdt", [P, DCH, B_HEADS])
        taps = ph.sb("taps", [P, XCH, B_CONV])
        cbias = ph.sb("cbias", [P, XCH])
        acc = ph.sb("acc", [P, 2, SEQ])
        ones = ph.sb("ones", [P, P])
        soft = ph.sb("soft", [P, 3, HB])
        dtA = ph.sb("dtA", [P, HB])
        csT = ph.sb("csT", [HB, P])
        first_in = [ph.sem(f"first{c}_in") for c in range(0, DCH, 2)]
        slab_in = [ph.sem(f"slab{j}_in") for j in range(len(slabs))]
        (small_in, rows_in, history, unit_full, unit_copied, conv_full, silu_full, link,
         consts, dt_full, pre, exped, sums, csT_full, spilled, tables) = ph.sems(
            "small_in rows_in history unit_full unit_copied conv_full silu_full link "
            "consts dt_full pre exped sums csT_full spilled tables")
        block = ph.open_block()
        ps = core.ps
        dt_ps, cs_ps, csT_ps, total_ps = (ps[:, 7, j * P:(j + 1) * P] for j in range(4))
        n_z = 2 * TILES
        n_units = n_z + 2 * XCH

        @block.sync
        def _(sp):
            for j, col in enumerate(slabs):
                if j >= 2:
                    sp.wait_ge(unit_full, 8 * (j - 1))
                if j:
                    sp.dma_start(w[:, j % 2], w_in[:, col:col + 512].rearrange("(c p) n -> p c n", p=P)).then_inc(slab_in[j], 16)
                else:
                    for c in range(0, DCH, 2):
                        sp.dma_start(w[:, 0, c:c + 2], w_in[c * P:(c + 2) * P, col:col + 512].rearrange(
                            "(c p) n -> p c n", p=P)).then_inc(first_in[c // 2], 16)
                    sp.dma_start(wdt[:], w_in[:, dcol:dcol + B_HEADS].rearrange("(c p) n -> p c n", p=P)).then_inc(small_in, 16)
                    sp.dma_start(cbias[:], io["b_conv_b"][0].rearrange("(c p) -> p c", p=P),
                                 allow_slow_non_contiguous=True).then_inc(small_in, 16)
                    for k in range(B_CONV):
                        sp.dma_start(taps[:, :, k], io["b_conv_w"][0, k].rearrange("(c p) -> p c", p=P),
                                     allow_slow_non_contiguous=True).then_inc(small_in, 16)
                    for k, name in enumerate(["b_dt_bias", "b_a_log", "b_d"]):
                        sp.dma_start(tab.rows[:, k, :], io[name][0].partition_broadcast(P)).then_inc(rows_in, 16)
            sp.wait_ge(csT_full, 1)
            sp.dma_start(tab.cs_rows, csT[:]).then_inc(spilled, 16)
            sp.wait_ge(spilled, 16)

        @block.gpsimd
        def _(pool):
            nc.gpsimd.memset(xbc[:, :, 0:B_CONV - 1], 0.0).then_inc(history, 1)
            fill = Chain(pool, consts)
            fill.link(nc.gpsimd.memset(tab.tri[:], 1.0))
            fill.link(nc.gpsimd.affine_select(out=tab.tri[:], in_=tab.tri[:], compare_op=ALU.is_ge, fill=0.0, base=0,
                                              pattern=[[1, P]], channel_multiplier=-1))
            fill.link(nc.gpsimd.memset(ones[:], 1.0))

        @block.scalar
        def _(act):
            for u in range(n_z):
                act.wait_ge(unit_full, u + 1)
                s, t = divmod(u, TILES)
                nc.scalar.activation(z[:, t, s * 512:(s + 1) * 512], ps[:, u % 7, :], ACT.Silu).then_inc(unit_copied, 1)
                if u == TILES + 1:
                    act.wait_ge(pre, 3)
                    nc.scalar.activation(soft[:, 1, :], soft[:, 1, :], ACT.Exp, scale=-1.0).then_inc(exped, 1)
                    nc.scalar.activation(tab.rows[:, 1, :], tab.rows[:, 1, :], ACT.Exp).then_inc(exped, 1)
                    act.wait_ge(exped, 2)
                    nc.scalar.activation(soft[:, 1, :], soft[:, 1, :], ACT.Ln, bias=1.0).then_inc(exped, 1)
            act.wait_ge(sums, 1)
            nc.scalar.activation(tab.cs[:], cs_ps, ACT.Copy).then_inc(exped, 1)
            nc.scalar.activation(csT[:], csT_ps, ACT.Copy).then_inc(csT_full, 1)
            nc.scalar.activation(tab.from_start[:], cs_ps, ACT.Exp).then_inc(tables, 1)
            nc.scalar.activation(tab.whole[:], total_ps, ACT.Exp).then_inc(tables, 1)
            act.wait_ge(pre, 6)
            nc.scalar.activation(tab.to_end[:], tab.to_end[:], ACT.Exp).then_inc(tables, 1)
            for j in range(XCH + 1):
                if j < XCH:
                    for half in range(2):
                        u = n_z + 2 * j + half
                        act.wait_ge(unit_full, u + 1)
                        nc.scalar.activation(xbc[:, j, 3 + half * 512:3 + (half + 1) * 512], ps[:, u % 7, :],
                                             ACT.Copy).then_inc(unit_copied, 1)
                if j:
                    act.wait_ge(conv_full, j)
                    nc.scalar.activation(xbc[:, j - 1, 3:], acc[:, (j - 1) % 2, :], ACT.Silu).then_inc(silu_full, 1)

        @block.vector
        def _(dve):
            dve.wait_ge(rows_in, 48)
            dve.wait_ge(dt_full, 1)
            first = Chain(dve, pre)
            by_tile = lambda ap: ap.rearrange("p (t h) -> p t h", h=B_HEADS)
            first.link(nc.vector.tensor_tensor(by_tile(soft[:, 0, :]), by_tile(dt_ps),
                                               tab.rows[:, 0:1, :].broadcast_to([P, TILES, B_HEADS]), ALU.add))
            first.link(nc.vector.tensor_scalar(soft[:, 2, :], soft[:, 0, :], 0.0, None, ALU.max))
            first.link(nc.vector.scalar_tensor_tensor(soft[:, 1, :], soft[:, 2, :], 2.0, soft[:, 0, :], ALU.mult, ALU.subtract))
            dve.wait_ge(exped, 3)
            first.link(nc.vector.tensor_tensor(tab.dt[:], soft[:, 1, :], soft[:, 2, :], ALU.add))
            first.link(nc.vector.scalar_tensor_tensor(by_tile(dtA[:]), by_tile(tab.dt[:]), -1.0,
                                                      tab.rows[:, 1:2, :].broadcast_to([P, TILES, B_HEADS]), ALU.mult, ALU.mult))
            dve.wait_ge(sums, 1)
            dve.wait_ge(exped, 4)
            dve.wait_ge(tables, 2)
            first.link(nc.vector.tensor_tensor(tab.to_end[:], total_ps, tab.cs[:], ALU.subtract))
            dve.wait_ge(small_in, 16 * (2 + B_CONV))
            dve.wait_ge(history, 1)
            chain = Chain(dve, link)
            for j in range(XCH):
                dve.wait_ge(unit_copied, n_z + 2 * j + 2)
                if j >= 2:
                    dve.wait_ge(silu_full, j - 1)
                a = acc[:, j % 2, :]
                chain.link(nc.vector.tensor_scalar(a, xbc[:, j, 3:], taps[:, j, 3:4], cbias[:, j:j + 1], ALU.mult, ALU.add))
                for k in range(B_CONV - 1):
                    ins = nc.vector.scalar_tensor_tensor(a, xbc[:, j, k:k + SEQ], taps[:, j, k:k + 1], a, ALU.mult, ALU.add)
                    if k < B_CONV - 2:
                        chain.link(ins)
                ins.then_inc(conv_full, 1)

        @block.tensor
        def _(pe):
            u = 0
            for j in range(len(slabs)):
                if j:
                    pe.wait_ge(slab_in[j], 16)
                for part in range(8):
                    if u >= 7:
                        pe.wait_ge(unit_copied, u - 6)
                    for c in range(DCH):
                        if u == 0 and c % 2 == 0:
                            pe.wait_ge(first_in[c // 2], 16)
                        if j < 2:
                            lhsT, rhs = uT[:, c, part * P:(part + 1) * P], w[:, j % 2, c, :]
                        else:
                            lhsT = w[:, j % 2, c, part // 2 * P:(part // 2 + 1) * P]
                            rhs = uT[:, c, part % 2 * 512:(part % 2 + 1) * 512]
                        last = nc.tensor.matmul(ps[:, u % 7, :], lhsT, rhs, start=(c == 0), stop=(c == DCH - 1))
                    last.then_inc(unit_full, 1)
                    u += 1
                if j == 0:
                    pe.wait_ge(small_in, 16 * (2 + B_CONV))
                    for t in range(TILES):
                        for c in range(DCH):
                            last = nc.tensor.matmul(dt_ps[:, t * B_HEADS:(t + 1) * B_HEADS], uT[:, c, t * P:(t + 1) * P], wdt[:, c, :],
                                                    start=(c == 0), stop=(c == DCH - 1))
                    last.then_inc(dt_full, 1)
                if j == 1:
                    pe.wait_ge(consts, 3)
                    pe.wait_ge(pre, 5)
                    nc.tensor.matmul(cs_ps, tab.tri[:], dtA[:], start=True, stop=True)
                    nc.tensor.matmul(csT_ps, dtA[:], tab.tri[:], start=True, stop=True)
                    nc.tensor.matmul(total_ps, ones[:], dtA[:], start=True, stop=True).then_inc(sums, 1)


def mixer_b_scan(nc, core, uT, z, xbc, tab, io):
    XH = B_WIDTH // P
    GH = B_HEADS // B_GROUPS
    with ExitStack() as ctx:
        ph = Phase(nc, ctx, "bs")
        xs = ph.sb("xs", [P, 2, XH + 2 * B_GROUPS, P])
        bcs = uT[:, 0:4, :].rearrange("p (b k) n -> p b (k n)", b=2)
        seg = uT[:, 4:8, :].rearrange("p (b k) (h l) -> p b (k h) l", b=2, l=P)
        xdt = ph.sb("xdt", [P, 2, B_WIDTH])
        xend = ph.sb("xend", [P, 2, B_WIDTH])
        skip = ph.sb("skip", [P, B_WIDTH])
        yo = ph.sb("yo", [P, B_WIDTH])
        yx = ph.sb("yx", [P, B_WIDTH])
        bnat = ph.sb("bnat", [P, 2, B_GROUPS * P])
        cb = ph.sb("cb", [P, B_GROUPS * P])
        state = ph.sb("state", [P, B_WIDTH])
        (zeroed, xs_full, bcs0_in, bcs1_in, seg_full, decay, turned, b_full, cb_full, xdt_full, x_free, xend_full,
         off_full, yo_full, ysum_full, m_full, diag_full, state_add, faded, state_full, y_full, gated, held) = ph.sems(
            "zeroed xs_full bcs0_in bcs1_in seg_full decay turned b_full cb_full xdt_full x_free xend_full "
            "off_full yo_full ysum_full m_full diag_full state_add faded state_full y_full gated held")
        arrived = [bcs0_in, bcs1_in]
        block = ph.open_block()
        ps = core.ps
        x_ps = ps[:, 0:2, :].rearrange("p k n -> p (k n)")
        diag_ps = ps[:, 3:5, :].rearrange("p k n -> p (k n)")
        off_ps = ps[:, 5:7, :].rearrange("p k n -> p (k n)")
        b_ps = [ps[:, k, 0:B_GROUPS * P] for k in (2, 7)]
        cb_ps = [ps[:, k, B_GROUPS * P:2 * B_GROUPS * P] for k in (2, 7)]
        heads = lambda ap: ap.rearrange("p (h d) -> p h d", d=HD)
        per_head = lambda ap: ap.unsqueeze(2).broadcast_to([P, B_HEADS, HD])
        of_tile = lambda table, t: table[:, bass.ds(t * B_HEADS, B_HEADS)]

        @block.sync
        def _(sp):
            with sp.Fori(0, TILES // 2) as i:
                for b in range(2):
                    sp.wait_ge(seg_full, i * 2 + (b + 1))
                    src = tab.cs_rows[bass.ds((i * 2 + b) * B_HEADS, B_HEADS), :].rearrange("h l -> (h l)")
                    sp.dma_start(bcs[:, b, :], src.partition_broadcast(P)).then_inc(arrived[b], 16)

        @block.gpsimd
        def _(pool):
            def decay_to_end(t, par):
                pool.wait_ge(xdt_full, t + 1)
                nc.gpsimd.tensor_tensor(heads(xend[:, par, :]), heads(xdt[:, par, :]), per_head(of_tile(tab.to_end, t)),
                                        ALU.mult).then_inc(xend_full, 1)

            def begin():
                nc.gpsimd.memset(state[:], 0.0).then_inc(zeroed, 1)
                pool.wait_ge(zeroed, 1)
                pool.sem_inc(state_full, 1)
                decay_to_end(0, 0)

            def step(t, par, ahead, front):
                pool.wait_ge(off_full, t + 1)
                pool.wait_ge(state_full, t + 1)
                nc.gpsimd.tensor_tensor(heads(state[:]), heads(state[:]), per_head(of_tile(tab.whole, t)), ALU.mult).then_inc(faded, 1)
                if front:
                    decay_to_end(t + 1, 1 - par)
                pool.wait_ge(y_full, t + 2)
                row = z[:, bass.ds(t, 1), :].rearrange("p o d -> p (o d)")
                nc.gpsimd.tensor_tensor(row, yx[:], row, ALU.mult).then_inc(gated, 1)

            pipeline(pool, begin, step)

        @block.scalar
        def _(act):
            def copy_tile(t, par):
                nc.scalar.activation(xs[:, par], xbc[:, :, bass.ds(t * P + 3, P)], ACT.Copy).then_inc(xs_full, 1)

            def decays(t, par):
                act.wait_ge(arrived[par], t * 8 + (8 if par else 16))
                act.wait_ge(diag_full, t + 1)
                act.sem_inc(held, 1)
                for hd in range(B_HEADS):
                    last = nc.scalar.activation(seg[:, par, hd, :], bcs[:, par, hd * P:(hd + 1) * P], ACT.Relu,
                                                bias=tab.cs[:, bass.ds(t * B_HEADS + hd, 1)], scale=-1.0)
                last.then_inc(seg_full, 1)
                act.wait_ge(seg_full, t + 3)
                nc.scalar.activation(seg[:, par], seg[:, par], ACT.Exp, scale=-1.0).then_inc(decay, 1)

            def copy_b(t, par):
                act.wait_ge(turned, t + 1)
                act.wait_ge(state_add, t + 1)
                nc.scalar.activation(bnat[:, par, :], b_ps[par], ACT.Copy).then_inc(b_full, 1)

            def begin():
                act.sem_inc(seg_full, 2)
                act.sem_inc(diag_full, 2)
                act.sem_inc(state_add, 2)
                copy_tile(0, 0)
                copy_tile(1, 1)
                decays(0, 0)
                copy_b(0, 0)

            def step(t, par, ahead, front):
                if front:
                    decays(t + 1, 1 - par)
                    copy_b(t + 1, 1 - par)
                if ahead:
                    act.wait_ge(off_full, t + 1)
                    act.sem_inc(held, 1)
                    copy_tile(t + 2, par)

            pipeline(act, begin, step)

        @block.vector
        def _(dve):
            def read_x(t, par):
                dve.wait_ge(turned, t + 1)
                nc.vector.tensor_tensor(heads(xdt[:, par, :]), heads(x_ps), per_head(of_tile(tab.dt, t)), ALU.mult).then_inc(xdt_full, 1)
                nc.vector.tensor_tensor(heads(skip[:]), heads(x_ps), per_head(tab.rows[:, 2, :]), ALU.mult).then_inc(x_free, 1)

            def begin():
                dve.sem_inc(x_free, 1)
                dve.sem_inc(y_full, 1)
                dve.sem_inc(gated, 1)
                read_x(0, 0)

            def step(t, par, ahead, front):
                dve.wait_ge(off_full, t + 1)
                dve.wait_ge(b_full, t + 1)
                nc.vector.tensor_tensor(heads(yo[:]), heads(off_ps), per_head(of_tile(tab.from_start, t)), ALU.mult).then_inc(yo_full, 1)
                nc.vector.tensor_tensor(cb[:].rearrange("p (g l) -> p g l", l=P), cb_ps[par].rearrange("p (g l) -> p g l", l=P),
                                        tab.tri[:].unsqueeze(1).broadcast_to([P, B_GROUPS, P]), ALU.mult).then_inc(cb_full, 1)
                dve.wait_ge(yo_full, t + 1)
                dve.wait_ge(x_free, t + 2)
                nc.vector.tensor_tensor(yo[:], skip[:], yo[:], ALU.add).then_inc(ysum_full, 1)
                dve.wait_ge(decay, t + 1)
                dve.wait_ge(cb_full, t + 1)
                by_group = seg[:, par].rearrange("p (g h) l -> p g h l", g=B_GROUPS)
                nc.vector.tensor_tensor(by_group, by_group,
                                        cb[:].rearrange("p (g l) -> p g l", l=P).unsqueeze(2).broadcast_to([P, B_GROUPS, GH, P]),
                                        ALU.mult).then_inc(m_full, 1)
                if front:
                    dve.wait_ge(ysum_full, t + 1)
                    read_x(t + 1, 1 - par)
                dve.wait_ge(state_add, t + 3)
                dve.wait_ge(faded, t + 1)
                nc.vector.tensor_tensor(state[:], off_ps, state[:], ALU.add).then_inc(state_full, 1)
                dve.wait_ge(diag_full, t + 3)
                dve.wait_ge(ysum_full, t + 1)
                dve.wait_ge(gated, t + 1)
                nc.vector.tensor_tensor(yx[:], diag_ps, yo[:], ALU.add).then_inc(y_full, 1)
                dve.wait_ge(y_full, t + 2)
                dve.wait_ge(m_full, t + 1)

            pipeline(dve, begin, step)

        @block.tensor
        def _(pe):
            def turn(t, par):
                pe.wait_ge(xs_full, t + 1)
                pe.wait_ge(x_free, t + 1)
                for c in range(XH + B_GROUPS):
                    out = x_ps[:, c * P:(c + 1) * P] if c < XH else b_ps[par][:, (c - XH) * P:(c - XH + 1) * P]
                    nc.tensor.transpose(out, xs[:, par, c, :], core.ident[:])
                for g in range(B_GROUPS):
                    last = nc.tensor.matmul(cb_ps[par][:, g * P:(g + 1) * P], xs[:, par, XH + g, :],
                                            xs[:, par, XH + B_GROUPS + g, :], start=True, stop=True)
                last.then_inc(turned, 1)

            def begin():
                turn(0, 0)

            def step(t, par, ahead, front):
                pe.wait_ge(state_full, t + 1)
                for g in range(B_GROUPS):
                    last = nc.tensor.matmul(off_ps[:, g * 512:(g + 1) * 512], xs[:, par, XH + B_GROUPS + g, :],
                                            state[:, g * 512:(g + 1) * 512], start=True, stop=True)
                last.then_inc(off_full, 1)
                if front:
                    turn(t + 1, 1 - par)
                pe.wait_ge(xend_full, t + 1)
                pe.wait_ge(yo_full, t + 1)
                pe.wait_ge(b_full, t + 1)
                for g in range(B_GROUPS):
                    last = nc.tensor.matmul(off_ps[:, g * 512:(g + 1) * 512], bnat[:, par, g * P:(g + 1) * P],
                                            xend[:, par, g * 512:(g + 1) * 512], start=True, stop=True)
                last.then_inc(state_add, 1)
                pe.wait_ge(m_full, t + 1)
                pe.wait_ge(xdt_full, t + 1)
                pe.wait_ge(y_full, t + 1)
                for hd in range(B_HEADS):
                    last = nc.tensor.matmul(diag_ps[:, hd * HD:(hd + 1) * HD], seg[:, par, hd, :], xdt[:, par, hd * HD:(hd + 1) * HD],
                                            start=True, stop=True)
                last.then_inc(diag_full, 1)

            pipeline(pe, begin, step)


def mixer_b(nc, core, uT, io):
    with ExitStack() as ctx:
        z = ctx.enter_context(nc.sbuf_tensor("b_z", [P, TILES, B_WIDTH], F32))
        with ExitStack() as inner:
            tab = ScanTables(nc, inner)
            xbc = inner.enter_context(nc.sbuf_tensor("b_xbc", [P, B_XBC // P, SEQ + B_CONV - 1], F32))
            mixer_b_project(nc, core, uT, z, xbc, tab, io)
            mixer_b_scan(nc, core, uT, z, xbc, tab, io)
        project_out(nc, core, "bout", z, B_WIDTH // P, io["b_out_norm"][0], io["w_out"][0, A_WIDTH:A_WIDTH + B_WIDTH, :])


def peer_and_gate(nc, core, hd, out, io):
    AHEAD = 5
    RING = 4
    KK = PH * TOPK
    with ExitStack() as ctx:
        ph = Phase(nc, ctx, "peer")
        wq = ph.sb("wq", [P, DCH, PH * PKD])
        wg = ph.sb("wg", [P, DCH, D])
        wp = ph.sb("wp", [P, PLE // P, D])
        skT = ph.sb("skT", [P, 2 * PH, PK])
        gain_row = ph.sb("gain_row", [P, D])
        gT = ph.sb("gT", [P, DCH])
        u_ring = ph.sb("u_ring", [P, RING, D])
        v_ring = ph.sb("v_ring", [P, RING, D])
        h_next = ph.sb("h_next", [P, D])
        h_sum = ph.sb("h_sum", [P, D])
        h_out = ph.sb("h_out", [P, D])
        un = ph.sb("un", [P, D])
        norm = ph.sb("norm", [P, D])
        uT = ph.sb("uT", [P, DCH, P])
        fT = ph.sb("fT", [P, DCH, P])
        gate = ph.sb("gate", [P, 512])
        ptok = ph.sb("ptok", [P, PLE])
        pT = ph.sb("pT", [P, PLE // P, P])
        q = ph.sb("q", [P, PKD])
        qT = ph.sb("qT", [P, PKD])
        top = ph.sb("top", [P, 2, TOPK])
        top_i = ph.sb("top_i", [P, 2, TOPK], U32)
        top_f = ph.sb("top_f", [P, 2, TOPK])
        rest = ph.sb("rest", [P, 2, PK])
        cand = ph.sb("cand", [P, TOPK, TOPK])
        cand2 = ph.sb("cand2", [P, TOPK * TOPK])
        best = ph.sb("best", [P, TOPK])
        best_i = ph.sb("best_i", [P, TOPK], U32)
        pair_i = ph.sb("pair_i", [P, 2, TOPK], U32)
        pair_f = ph.sb("pair_f", [P, 2 * TOPK])
        hot = ph.sb("hot", [P, 2 * TOPK, TOPK])
        halves = ph.sb("halves", [P, 2, TOPK])
        row_f = ph.sb("row_f", [P, TOPK])
        steps16 = ph.sb("steps16", [P, TOPK])
        idx_all = ph.sb("idx_all", [P, KK], U32)
        gates_all = ph.sb("gates_all", [P, KK])
        idx_u = ph.sb("idx_u", [P, 2, TOPK], U32)
        idx_v = ph.sb("idx_v", [P, 2, TOPK], U32)
        negbest = ph.sb("negbest", [P, 1])
        gexp = ph.sb("gexp", [P, TOPK])
        gsum = ph.sb("gsum", [P, 1])
        dots = ph.sb("dots", [P, 2, TOPK])
        weights = ph.sb("weights", [P, 2, TOPK])
        diag = ph.sb("diag", [P, RING, P])
        stat = ph.sb("stat", [P, 2])
        (held, small_in, sub_in, sub_turned, sub_copied, wq_in, wg_in, h_in, p_in,
         pre_sq, pre_root, pre_link, norm_full, pre_turned, uT_full,
         q_full, q_copied, qT_full, qT_copied, score_full, topk_link, idx_full, best_full, gexp_full, gates_full, gate_link, un_taken,
         u_free, v_free, iu_full, iv_full, gelu_full, weights_full, diag_full, sum_read,
         fin_sum, fin_sq, fin_root, fin_link, fin_norm, fin_turned, fin_copied, p_turned, p_copied,
         gate_full, gate_copied, ple_full, fin_mul, fin_done, stored, iota_done) = ph.sems(
            "held small_in sub_in sub_turned sub_copied wq_in wg_in h_in p_in "
            "pre_sq pre_root pre_link norm_full pre_turned uT_full "
            "q_full q_copied qT_full qT_copied score_full topk_link idx_full best_full gexp_full gates_full gate_link un_taken "
            "u_free v_free iu_full iv_full gelu_full weights_full diag_full sum_read "
            "fin_sum fin_sq fin_root fin_link fin_norm fin_turned fin_copied p_turned p_copied "
            "gate_full gate_copied ple_full fin_mul fin_done stored iota_done")
        u_in = [ph.sem(f"u{j}_in") for j in range(RING)]
        v_in = [ph.sem(f"v{j}_in") for j in range(RING)]
        ps = core.ps
        sum_ps = [ps[:, 2 * b:2 * b + 2, :].rearrange("p k n -> p (k n)") for b in range(2)]
        q_ps, qT_ps, score_ps, misc_ps = (ps[:, b, :] for b in range(4, 8))
        TK = 24
        block = ph.open_block()

        def schedule(eng, begin, group, finish_tail):
            def tile(t, first, last):
                g = t * PH
                group(g, t, 0, v=not first, add=not first, topk=True)
                group(g + 1, t, 1, v=True, add=not first, topk=True, finish=not first)
                group(g + 2, t, 2, v=True, topk=True, prepare=not last, final_topk=last)
                with eng.Fori(0, 2) as k:
                    for b in range(2):
                        group(g + k * 2 + (3 + b), t, k * 2 + (3 + b), v=True, topk=not last, odd=1 - b)
                group(g + 7, t, 7, v=True, topk=not last)
            begin()
            tile(0, True, False)
            with eng.Fori(1, TILES - 1) as t:
                tile(t, False, False)
            tile(TILES - 1, False, True)
            finish_tail(TILES * PH)

        @block.sync
        def _(sp):
            def load_tile(t):
                sp.dma_start(h_next[:], hd[bass.ds(t * P, P), :]).then_inc(h_in, 16)

            sp.dma_start(h_next[:], hd[0:P, :]).then_inc(h_in, 16)
            sp.dma_start(gain_row[:], io["ffn_norm"][0].partition_broadcast(P)).then_inc(small_in, 16)
            sp.dma_start(gT[:], io["ple_norm"][0].rearrange("(c p) -> p c", p=P), allow_slow_non_contiguous=True).then_inc(small_in, 16)
            sp.dma_start(wg[:, 0:2, :].rearrange("p c (a d) -> p (c a) d", d=P),
                         io["peer_sub_keys"][0].rearrange("h s k d -> k (h s) d")).then_inc(sub_in, 16)
            sp.dma_start(wq[:], io["peer_w_query"][0].rearrange("(c p) n -> p c n", p=P)).then_inc(wq_in, 16)
            sp.wait_ge(sub_copied, 4)
            sp.dma_start(wg[:], io["ple_w_gate"][0].rearrange("(c p) n -> p c n", p=P)).then_inc(wg_in, 16)
            sp.dma_start(wp[:], io["ple_w_proj"][0].rearrange("(c p) n -> p c n", p=P)).then_inc(wg_in, 16)

            def prepare(t):
                sp.wait_ge(sum_read, t * PH + 3)
                sp.sem_inc(held, 1)
                sp.dma_start(h_next[:], hd[bass.ds((t + 1) * P, P), :]).then_inc(h_in, 16)

            def finish(t):
                sp.wait_ge(p_copied, t + 1)
                sp.sem_inc(held, 1)
                sp.dma_start(ptok[:], io["p"][0, 0, bass.ds(t * P, P), :]).then_inc(p_in, 16)
                sp.wait_ge(fin_done, t * 2 + 2)
                sp.sem_inc(held, 1)
                sp.dma_start(out[bass.ds(t * P, P), :], h_out[:]).then_inc(stored, 16)

            prepare(0)
            with sp.Fori(1, TILES - 1) as t:
                finish(t - 1)
                prepare(t)
            finish(TILES - 2)
            finish(TILES - 1)
            sp.wait_ge(stored, 16 * TILES)

        @block.gpsimd
        def _(pool):
            def begin():
                pool.iota(steps16[:], pattern=[[1, TOPK]], base=0, channel_multiplier=0,
                          allow_small_or_imprecise_dtypes=True).then_inc(iota_done, 1)

            def gather(ring, s, table, idx, arrived):
                nc.gpsimd.indirect_dma_start(ring[:, s % RING, :], None, table,
                                             bass.IndirectOffsetOnAxis(ap=idx[:, s:s + 1], axis=0)).then_inc(arrived[s % RING], 16)

            def values(g, s, odd):
                if s == 0:
                    pool.wait_ge(iv_full, g + 1)
                pool.wait_ge(v_free, g * TOPK + (s + 1))
                pool.sem_inc(held, 1)
                gather(v_ring, s, io["peer_v"][0], idx_v[:, odd, :], v_in)

            def group(g, t, h, v=False, add=True, topk=False, finish=False, prepare=False, odd=None, final_topk=False):
                odd = h % 2 if odd is None else odd
                pool.wait_ge(iu_full, g + 1)
                for s in range(TOPK):
                    pool.wait_ge(u_free, g * TOPK + (s + 1))
                    pool.sem_inc(held, 1)
                    gather(u_ring, s, io["peer_u"][0], idx_u[:, odd, :], u_in)
                    if v:
                        values(g - 1, s, 1 - odd)

            def tail(g):
                for s in range(TOPK):
                    values(g - 1, s, 1)

            schedule(pool, begin, group, tail)

        @block.scalar
        def _(act):
            def square_and_root(src, at, squared, rooted, n):
                nc.scalar.activation(norm[:], src, ACT.Square, accum_out=stat[:, at:at + 1]).then_inc(squared, 1)
                act.wait_ge(squared, n + 1)
                nc.scalar.activation(stat[:, at:at + 1], stat[:, at:at + 1], ACT.Sqrt, bias=core.eps[:, 0:1],
                                     scale=1.0 / D).then_inc(rooted, 1)

            def prepare_root(t, begins=False):
                act.wait_ge(h_in, t * 16 + 16)
                if not begins:
                    act.wait_ge(fin_copied, (t - 1) * 2)
                square_and_root(h_next[:], 0, pre_sq, pre_root, t)

            def prepare_copy(t):
                for half in range(2):
                    act.wait_ge(pre_turned, t * 2 + (half + 1))
                    nc.scalar.activation(uT[:, half * 4:half * 4 + 4, :], misc_ps.rearrange("p (c n) -> p c n", n=P),
                                         ACT.Copy).then_inc(uT_full, 1)

            def q_copy(k):
                act.wait_ge(q_full, k + 1)
                nc.scalar.activation(q[:], q_ps[:, 0:PKD], ACT.Copy).then_inc(q_copied, 1)

            def qT_copy(k):
                act.wait_ge(qT_full, k + 1)
                nc.scalar.activation(qT[:], qT_ps[:, 0:PKD], ACT.Copy).then_inc(qT_copied, 1)

            def gate_exp(k):
                act.wait_ge(best_full, k + 1)
                act.wait_ge(gates_full, k)
                nc.scalar.activation(gexp[:], best[:], ACT.Exp, bias=negbest[:, 0:1], accum_out=gsum[:, 0:1]).then_inc(gexp_full, 1)

            def begin():
                act.sem_inc(p_copied, 1)
                for j in range(4):
                    act.wait_ge(sub_turned, j + 1)
                    nc.scalar.activation(skT[:, 4 * j:4 * j + 4, :], ps[:, j, :].rearrange("p (a k) -> p a k", k=PK),
                                         ACT.Copy).then_inc(sub_copied, 1)
                prepare_root(0, begins=True)
                prepare_copy(0)
                for k in range(AHEAD):
                    q_copy(k)
                    qT_copy(k)
                    gate_exp(k)

            def diagonal(g, s, odd):
                if s == 0:
                    act.wait_ge(weights_full, g + 1)
                act.wait_ge(v_free, g * TOPK + (s + 1))
                nc.scalar.activation(diag[:, s % RING, :], core.ident[:], ACT.Copy,
                                     scale=weights[:, odd, s:s + 1]).then_inc(diag_full, 1)

            def p_copy(t):
                act.wait_ge(p_turned, t + 1)
                nc.scalar.activation(pT[:], misc_ps[:, 0:PLE].rearrange("p (c n) -> p c n", n=P), ACT.Copy).then_inc(p_copied, 1)

            def finish_root(t):
                act.wait_ge(fin_sum, t + 1)
                square_and_root(h_out[:], 1, fin_sq, fin_root, t)

            def gate_half(t, half):
                act.wait_ge(gate_full, t * 2 + (half + 1))
                act.wait_ge(fin_done, t * 2 + half) if half else None
                nc.scalar.activation(gate[:], misc_ps, ACT.Sigmoid).then_inc(gate_copied, 1)

            def group(g, t, h, v=False, add=True, topk=False, finish=False, prepare=False, odd=None, final_topk=False):
                odd = h % 2 if odd is None else odd
                for s in range(TOPK):
                    if v:
                        diagonal(g - 1, s, 1 - odd)
                    if topk and s == 3:
                        q_copy(g + AHEAD)
                    if topk and s == 5:
                        qT_copy(g + AHEAD)
                    if finish and s == 2:
                        p_copy(t - 1)
                        finish_root(t - 1)
                    if finish and s in (9, 12):
                        gate_half(t - 1, s // 12)
                    if prepare and s == 6:
                        prepare_root(t + 1)
                    if prepare and s == 13:
                        prepare_copy(t + 1)
                if topk:
                    gate_exp(g + AHEAD)
                act.wait_ge(u_free, g * TOPK + (TOPK + RING))
                nc.scalar.activation(dots[:, odd, :], dots[:, odd, :], ACT.Gelu).then_inc(gelu_full, 1)

            def tail(g):
                for s in range(TOPK):
                    diagonal(g - 1, s, 1)
                p_copy(TILES - 1)
                finish_root(TILES - 1)
                for half in range(2):
                    gate_half(TILES - 1, half)

            schedule(act, begin, group, tail)

        @block.vector
        def _(dve):
            def retrieval(k, slot):
                chain = Chain(dve, topk_link, k * TK)

                def link(ins):
                    chain.link(ins)
                    dve.sem_inc(held, 1)

                def sixteen_best(vals, idx, src, scratch):
                    link(nc.vector.max(vals[:, 0:8], src))
                    link(nc.vector.max_index(idx[:, 0:8], vals[:, 0:8], src))
                    link(nc.vector.match_replace(scratch, vals[:, 0:8], src, -3e38))
                    link(nc.vector.max(vals[:, 8:16], scratch))
                    link(nc.vector.max_index(idx[:, 8:16], vals[:, 8:16], scratch))

                def keys(side):
                    def step():
                        if side == 0:
                            dve.wait_ge(score_full, k + 1)
                            dve.sem_inc(held, 1)
                        sixteen_best(top[:, side, :], top_i[:, side, :], score_ps[:, side * PK:(side + 1) * PK], rest[:, side, :])
                    return step

                def pairs():
                    chain.link(nc.vector.tensor_copy(top_f[:], top_i[:]))
                    chain.link(nc.vector.tensor_tensor(cand[:], top[:, 0, :].unsqueeze(2).broadcast_to([P, TOPK, TOPK]),
                                                       top[:, 1:2, :].broadcast_to([P, TOPK, TOPK]), ALU.add))

                def best_pairs():
                    dve.wait_ge(gexp_full, k)
                    dve.sem_inc(held, 1)
                    sixteen_best(best[:], best_i[:], cand[:].rearrange("p a b -> p (a b)"), cand2[:])

                def unpair():
                    chain.link(nc.vector.tensor_scalar(pair_i[:, 0, :], best_i[:], 4, None, ALU.logical_shift_right))
                    chain.link(nc.vector.tensor_scalar(pair_i[:, 1, :], best_i[:], 15, None, ALU.bitwise_and))
                    chain.link(nc.vector.tensor_copy(pair_f[:], pair_i[:].rearrange("p a b -> p (a b)")))
                    chain.link(nc.vector.tensor_tensor(hot[:], pair_f[:].unsqueeze(2).broadcast_to([P, 2 * TOPK, TOPK]),
                                                       steps16[:].unsqueeze(1).broadcast_to([P, 2 * TOPK, TOPK]), ALU.is_equal))
                    by_side = hot[:].rearrange("p (a s) b -> p a s b", a=2)
                    chain.link(nc.vector.tensor_tensor(by_side, by_side, top_f[:].unsqueeze(2).broadcast_to([P, 2, TOPK, TOPK]), ALU.mult))
                    chain.link(nc.vector.tensor_reduce(halves[:], by_side, axis=AX.X, op=ALU.add))

                def rows():
                    chain.link(nc.vector.scalar_tensor_tensor(row_f[:], halves[:, 0, :], float(PK), halves[:, 1, :], ALU.mult, ALU.add))
                    nc.vector.tensor_copy(idx_all[:, bass.ds(slot * TOPK, TOPK)], row_f[:]).then_inc(idx_full, 1)
                    assert chain.n == TK, chain.n
                    nc.vector.tensor_scalar(negbest[:], best[:, 0:1], -1.0, None, ALU.mult).then_inc(best_full, 1)

                return keys(0), keys(1), pairs, best_pairs, unpair, rows

            def gates(k, slot):
                dve.wait_ge(gexp_full, k + 1)
                nc.vector.reciprocal(gsum[:], gsum[:]).then_inc(gate_link, 1)
                dve.wait_ge(gate_link, k + 1)
                nc.vector.tensor_scalar(gates_all[:, bass.ds(slot * TOPK, TOPK)], gexp[:], gsum[:, 0:1], None,
                                        ALU.mult).then_inc(gates_full, 1)

            def rstd_of(at, rooted, link, n):
                dve.wait_ge(rooted, n + 1)
                nc.vector.reciprocal(stat[:, at:at + 1], stat[:, at:at + 1]).then_inc(link, 1)
                dve.wait_ge(link, n + 1)

            def prepare(t):
                rstd_of(0, pre_root, pre_link, t)
                nc.vector.scalar_tensor_tensor(norm[:], h_next[:], stat[:, 0:1], gain_row[:], ALU.mult, ALU.mult).then_inc(norm_full, 1)

            def copy_rows(dst, b, slot, full):
                nc.vector.tensor_copy(dst[:, b, :], idx_all[:, bass.ds(slot * TOPK, TOPK)]).then_inc(full, 1)

            def begin():
                dve.sem_inc(u_free, RING)
                dve.sem_inc(sum_read, 2)
                dve.wait_ge(small_in, 32)
                dve.wait_ge(iota_done, 1)
                prepare(0)
                for k in range(AHEAD):
                    for step in retrieval(k, k):
                        step()
                    if k < AHEAD - 1:
                        gates(k, k + 1)
                dve.wait_ge(idx_full, 1)
                copy_rows(idx_u, 0, 0, iu_full)

            def weigh(g, slot, odd):
                dve.wait_ge(gelu_full, g + 1)
                dve.wait_ge(gates_full, g + 1)
                nc.vector.tensor_tensor(weights[:, odd, :], dots[:, odd, :], gates_all[:, bass.ds(slot * TOPK, TOPK)],
                                        ALU.mult).then_inc(weights_full, 1)

            def add_sum(g, h, odd):
                dve.wait_ge(v_free, g * TOPK + (TOPK + RING))
                dve.wait_ge(sum_read, g + 2)
                src, dst = (h_next, h_sum) if h == 2 else (h_sum, h_out) if h == 1 else (h_sum, h_sum)
                return nc.vector.tensor_tensor(dst[:], sum_ps[odd], src[:], ALU.add)

            def finish_sum(t, g, odd):
                dve.wait_ge(stored, t * 16)
                add_sum(g, 1, odd).then_inc(fin_sum, 1)
                dve.wait_ge(fin_sum, t + 1)
                dve.sem_inc(sum_read, 1)

            def finish_norm(t):
                rstd_of(1, fin_root, fin_link, t)
                nc.vector.tensor_scalar(norm[:], h_out[:], stat[:, 1:2], None, ALU.mult).then_inc(fin_norm, 1)

            def finish_copy(t, half):
                dve.wait_ge(fin_turned, t * 2 + (half + 1))
                nc.vector.tensor_tensor(fT[:, half * 4:half * 4 + 4, :], misc_ps.rearrange("p (c n) -> p c n", n=P),
                                        gT[:, half * 4:half * 4 + 4].unsqueeze(2).broadcast_to([P, 4, P]), ALU.mult).then_inc(fin_copied, 1)

            def finish_half(t, half):
                dve.wait_ge(ple_full, t * 2 + (half + 1))
                nc.vector.tensor_tensor(gate[:], misc_ps, gate[:], ALU.mult).then_inc(fin_mul, 1)
                dve.wait_ge(fin_mul, t * 2 + (half + 1))
                part = h_out[:, half * 512:(half + 1) * 512]
                nc.vector.tensor_tensor(part, part, gate[:], ALU.add).then_inc(fin_done, 1)

            def group(g, t, h, v=False, add=True, topk=False, finish=False, prepare=False, odd=None, final_topk=False):
                runtime = odd is not None
                odd = h % 2 if odd is None else odd
                if topk:
                    ks = retrieval(g + AHEAD, (h + AHEAD) % PH if not runtime else h - 3)
                if not runtime and h == 0:
                    dve.wait_ge(u_free, g * TOPK + RING)
                    nc.vector.scalar_tensor_tensor(un[:], h_next[:], stat[:, 0:1], gain_row[:], ALU.mult, ALU.mult).then_inc(un_taken, 1)
                    dve.wait_ge(un_taken, t + 1)
                for s in range(TOPK):
                    dve.wait_ge(u_in[s % RING], g * 64 + 16 * (s // RING + 1))
                    row = u_ring[:, s % RING, :]
                    nc.vector.tensor_tensor_reduce(out=row, in0=row, in1=un[:], scale=1.0, scalar=0.0, op0=ALU.mult, op1=ALU.add,
                                                   accum_out=dots[:, odd, s:s + 1]).then_inc(u_free, 1)
                    if s == 0 and v:
                        weigh(g - 1, h, 1 - odd)
                    if s == 1 and add:
                        if finish:
                            finish_sum(t - 1, g - 2, odd)
                        else:
                            add_sum(g - 2, h if not runtime else 3, odd).then_inc(sum_read, 1)
                    if s == 3:
                        copy_rows(idx_v, odd, h, iv_full)
                    if s == 4 and (topk or runtime or h < 7):
                        dve.wait_ge(idx_full, g + 2)
                        copy_rows(idx_u, 1 - odd, (h + 1) % PH if not runtime else h + 1, iu_full)
                    if topk and 7 <= s <= 12:
                        ks[s - 7]()
                    if topk and s == 5:
                        gates(g + AHEAD - 1, h - 3 if runtime else (h + AHEAD) % PH)
                    if final_topk and s == 15:
                        gates(g + AHEAD, (h + AHEAD + 1) % PH)
                    if finish and s == 4:
                        finish_norm(t - 1)
                    if finish and s in (6, 7):
                        finish_copy(t - 1, s - 6)
                    if finish and s in (11, 14):
                        finish_half(t - 1, s // 14)
                    if prepare and s == 10:
                        prepare_dve(t + 1)

            def tail(g):
                weigh(g - 1, 0, 1)
                add_sum(g - 2, 0, 0).then_inc(sum_read, 1)
                finish_sum(TILES - 1, g - 1, 1)
                finish_norm(TILES - 1)
                for half in range(2):
                    finish_copy(TILES - 1, half)
                for half in range(2):
                    finish_half(TILES - 1, half)

            prepare_dve = prepare
            schedule(dve, begin, group, tail)

        @block.tensor
        def _(pe):
            def prepare(t, begins=False):
                if not begins:
                    pe.wait_ge(fin_mul, (t - 1) * 2)
                for half in range(2):
                    pe.wait_ge(norm_full, t + 1)
                    if half:
                        pe.wait_ge(uT_full, t * 2 + 1)
                    for c in range(4):
                        last = nc.tensor.transpose(misc_ps[:, c * P:(c + 1) * P], norm[:, (half * 4 + c) * P:(half * 4 + c + 1) * P],
                                                   core.ident[:])
                    last.then_inc(pre_turned, 1)

            def query(k, slot, t):
                pe.wait_ge(uT_full, t * 2 + 2)
                pe.wait_ge(q_copied, k)
                for c in range(DCH):
                    last = nc.tensor.matmul(q_ps[:, 0:PKD], uT[:, c, :], wq[:, c, bass.ds(slot * PKD, PKD)],
                                            start=(c == 0), stop=(c == DCH - 1))
                last.then_inc(q_full, 1)

            def turn_query(k):
                pe.wait_ge(q_copied, k + 1)
                for side in range(2):
                    last = nc.tensor.transpose(qT_ps[:, side * P:(side + 1) * P], q[:, side * P:(side + 1) * P], core.ident[:])
                last.then_inc(qT_full, 1)

            def scores(k, slot):
                pe.wait_ge(qT_copied, k + 1)
                pe.wait_ge(idx_full, k)
                for side in range(2):
                    last = nc.tensor.matmul(score_ps[:, side * PK:(side + 1) * PK], qT[:, side * P:(side + 1) * P],
                                            skT[:, bass.ds(slot * 2 + side, 1), :].rearrange("p o k -> p (o k)"), start=True, stop=True)
                last.then_inc(score_full, 1)

            def begin():
                pe.sem_inc(v_free, RING)
                pe.wait_ge(sub_in, 16)
                for j in range(4):
                    for a in range(4):
                        last = nc.tensor.transpose(ps[:, j, a * P:(a + 1) * P],
                                                   wg[:, 0:2, :].rearrange("p c (a d) -> p (c a) d", d=P)[:, 4 * j + a, :], core.ident[:])
                    last.then_inc(sub_turned, 1)
                prepare(0, begins=True)
                pe.wait_ge(wq_in, 16)
                pe.wait_ge(sub_copied, 4)
                for k in range(AHEAD):
                    query(k, k, 0)
                    turn_query(k)
                    scores(k, k)

            def values(g, s, odd):
                if s == 0:
                    pe.wait_ge(sum_read, g + 1)
                pe.wait_ge(diag_full, g * TOPK + (s + 1))
                pe.wait_ge(v_in[s % RING], g * 64 + 16 * (s // RING + 1))
                for half in range(2):
                    last = nc.tensor.matmul(sum_ps[odd][:, half * 512:(half + 1) * 512], diag[:, s % RING, :],
                                            v_ring[:, s % RING, half * 512:(half + 1) * 512], start=(s == 0), stop=(s == TOPK - 1))
                last.then_inc(v_free, 1)

            def turn_p(t):
                pe.wait_ge(p_in, t * 16 + 16)
                pe.wait_ge(fin_mul, t * 2)
                for c in range(PLE // P):
                    last = nc.tensor.transpose(misc_ps[:, c * P:(c + 1) * P], ptok[:, c * P:(c + 1) * P], core.ident[:])
                last.then_inc(p_turned, 1)

            def finish_turn(t, half):
                pe.wait_ge(fin_norm, t + 1)
                if half:
                    pe.wait_ge(fin_copied, t * 2 + 1)
                else:
                    pe.wait_ge(p_copied, t + 2)
                for c in range(4):
                    last = nc.tensor.transpose(misc_ps[:, c * P:(c + 1) * P], norm[:, (half * 4 + c) * P:(half * 4 + c + 1) * P],
                                               core.ident[:])
                last.then_inc(fin_turned, 1)

            def gate_half(t, half):
                pe.wait_ge(wg_in, 32)
                pe.wait_ge(fin_copied, t * 2 + 2)
                if half:
                    pe.wait_ge(fin_mul, t * 2 + 1)
                for c in range(DCH):
                    last = nc.tensor.matmul(misc_ps, fT[:, c, :], wg[:, c, half * 512:(half + 1) * 512], start=(c == 0), stop=(c == DCH - 1))
                last.then_inc(gate_full, 1)

            def ple_half(t, half):
                pe.wait_ge(gate_copied, t * 2 + (half + 1))
                for c in range(PLE // P):
                    last = nc.tensor.matmul(misc_ps, pT[:, c, :], wp[:, c, half * 512:(half + 1) * 512], start=(c == 0), stop=(c == PLE // P - 1))
                last.then_inc(ple_full, 1)

            prepare_pe = prepare

            def group(g, t, h, v=False, add=True, topk=False, finish=False, prepare=False, odd=None, final_topk=False):
                runtime = odd is not None
                odd = h % 2 if odd is None else odd
                slot = (h + AHEAD) % PH if not runtime else h - 3
                late = runtime or h + AHEAD >= PH
                for s in range(TOPK):
                    if v:
                        values(g - 1, s, 1 - odd)
                    if topk and s == 1:
                        query(g + AHEAD, slot, t + 1 if late else t)
                    if topk and s == 3:
                        turn_query(g + AHEAD)
                    if topk and s == 5:
                        scores(g + AHEAD, slot)
                    if finish and s == 0:
                        turn_p(t - 1)
                    if finish and s in (5, 6):
                        finish_turn(t - 1, s - 5)
                    if finish and s in (8, 11):
                        gate_half(t - 1, s // 11)
                    if finish and s in (9, 12):
                        ple_half(t - 1, s // 12)
                    if prepare and s == 12:
                        prepare_pe(t + 1)

            def tail(g):
                for s in range(TOPK):
                    values(g - 1, s, 1)
                turn_p(TILES - 1)
                for half in range(2):
                    finish_turn(TILES - 1, half)
                for half in range(2):
                    gate_half(TILES - 1, half)
                    ple_half(TILES - 1, half)

            schedule(pe, begin, group, tail)


def store_stream(nc, core, hd):
    with ExitStack() as ctx:
        ph = Phase(nc, ctx, "store")
        done = ph.sem("done")
        block = ph.open_block()

        @block.sync
        def _(sp):
            for t in range(TILES):
                sp.dma_start(hd[t * P:(t + 1) * P, :], core.h[:, t, :]).then_inc(done, 16)
            sp.wait_ge(done, 16 * TILES)


def build(nc, io, out):
    hd = nc.dram_tensor("stream", (SEQ, D), F32, kind="Internal").ap()
    with ExitStack() as ctx:
        core = Core(nc, ctx)
        with ExitStack() as mixers:
            core.h = mixers.enter_context(nc.sbuf_tensor("h", [P, TILES, D], F32))
            uT = mixers.enter_context(nc.sbuf_tensor("uT", [P, DCH, SEQ], F32))
            normalise_input(nc, core, uT, io["x"][0], io["mix_norm"][0])
            with ExitStack() as pair:
                y = pair.enter_context(nc.sbuf_tensor("y", [P, TILES, A_WIDTH], F32))
                mixer_a(nc, core, uT, y, io)
                mixer_c(nc, core, uT, y, io)
            mixer_b(nc, core, uT, io)
            store_stream(nc, core, hd)
        peer_and_gate(nc, core, hd, out[0], io)


_INS = ["x", "p", "mix_norm", "w_in", "a_q_norm", "a_k_norm", "a_sinks", "a_out_norm", "b_conv_w", "b_conv_b", "b_dt_bias",
        "b_a_log", "b_d", "b_out_norm", "c_q_norm", "c_k_norm", "c_rel_bias", "c_out_norm", "w_out", "ffn_norm",
        "peer_w_query", "peer_sub_keys", "peer_u", "peer_v", "ple_norm", "ple_w_gate", "ple_w_proj"]


def kernel(**inputs):
    import concourse.bacc as bacc
    from concourse.bass_utils import run_bass_kernel_spmd

    nc = bacc.Bacc("TRN2", target_bir_lowering=False, num_devices=1)
    arrays = {name: np.ascontiguousarray(inputs[name]) for name in _INS}
    io = {name: nc.dram_tensor(name, a.shape, mybir.dt.from_np(a.dtype), kind="ExternalInput").ap() for name, a in arrays.items()}
    out = nc.dram_tensor("out", (1, SEQ, D), F32, kind="ExternalOutput").ap()
    build(nc, io, out)
    r = run_bass_kernel_spmd(nc, [arrays], core_ids=[0])
    return r.results[0]["out"]
```

```python
from contextlib import ExitStack

import numpy as np
import concourse.bass as bass
from concourse import mybir

F32 = mybir.dt.float32
U32 = mybir.dt.uint32
ALU = mybir.AluOpType
ACT = mybir.ActivationFunctionType
AX = mybir.AxisListType

P = 128
SEQ, D = 1024, 1024
TILES = SEQ // P
DCH = D // P
CHUNK, HD = 64, 64
EPS = 1e-6
NEG = -1e30
A_HEADS, A_KV = 8, 2
A_WIDTH, A_QKV = 512, 768
B_WIDTH, B_HEADS, B_GROUPS, B_STATE, B_CONV = 1024, 16, 2, 128, 4
B_XBC = B_WIDTH + 2 * B_GROUPS * B_STATE
B_IN = B_WIDTH + B_XBC + B_HEADS
C_HEADS, C_WIDTH = 8, 512
C_PASS = 4
REL_FUTURE, REL_PAST = 63, 256
REL_SIZE = REL_FUTURE + REL_PAST + 1
PLE = 256
PH, PK, PKD, TOPK = 8, 128, 256, 16
SEL = PH * TOPK


class Chain:

    def __init__(self, eng, sem, base=0):
        self.eng, self.sem, self.base, self.n = eng, sem, base, 0

    def link(self, ins):
        self.n += 1
        ins.then_inc(self.sem, 1)
        self.eng.wait_ge(self.sem, self.base + self.n)


class Core:

    def __init__(self, nc, ctx):
        self.nc = nc
        self.h = None
        self.ident = ctx.enter_context(nc.sbuf_tensor("ident", [P, P], F32))
        self.eps = ctx.enter_context(nc.sbuf_tensor("eps", [P, 1], F32))
        self.ps = ctx.enter_context(nc.psum_tensor("ps", [P, 8, 512], F32))
        self.wq = ctx.enter_context(nc.sbuf_tensor("wq", [P, 2, DCH, PH // 2 * PKD], F32))
        self.skT = ctx.enter_context(nc.sbuf_tensor("skT", [P, 2 * PH, PK], F32))
        self.wq0_in = ctx.enter_context(nc.semaphore("wq0_in"))


class Phase:

    def __init__(self, nc, ctx, tag):
        self.nc, self.ctx, self.tag, self.used = nc, ctx, tag, []

    def sb(self, name, shape, dt=F32):
        return self.ctx.enter_context(self.nc.sbuf_tensor(f"{self.tag}_{name}", shape, dt))

    def sem(self, name):
        self.used.append(self.ctx.enter_context(self.nc.semaphore(f"{self.tag}_{name}")))
        return self.used[-1]

    def open_block(self):
        self.ctx.callback(self.clear)
        return self.ctx.enter_context(self.nc.Block())

    def clear(self):
        numbers = sorted(s.num for s in self.used)
        starts = [n for n in numbers if n - 1 not in numbers]
        ends = [n + 1 for n in numbers if n + 1 not in numbers]
        for start, end in zip(starts, ends):
            self.nc.sync.sem_clear(range(start, end))
        self.nc.all_engine_barrier()

    def sems(self, names):
        return [self.sem(n) for n in names.split()]


def normalise_input(nc, core, uT, x, gain, sub_keys):
    with ExitStack() as ctx:
        ph = Phase(nc, ctx, "in")
        xn = ph.sb("xn", [P, 2, D])
        gT = ph.sb("gT", [P, DCH])
        rstd = ph.sb("rstd", [P, TILES])
        scratch = ph.sb("scratch", [P, D])
        sub = ph.sb("sub", [P, 2 * PH, P])
        loaded = [ph.sem(f"x{t}_in") for t in range(TILES)]
        sub_in, sub_turned, small_in, consts, squares, rooted, rstd_ready, xn_full, t_full, t_free = ph.sems(
            "sub_in sub_turned small_in consts squares rooted rstd_ready xn_full t_full t_free")
        block = ph.open_block()
        h, ps, ident = core.h, core.ps, core.ident

        @block.sync
        def _(sp):
            for t in range(TILES):
                sp.dma_start(h[:, t, :], x[t * P:(t + 1) * P, :]).then_inc(loaded[t], 16)
                if t == 0:
                    sp.dma_start(gT[:], gain.rearrange("(c p) -> p c", p=P), allow_slow_non_contiguous=True).then_inc(small_in, 16)
            sp.dma_start(sub[:], sub_keys.rearrange("h s k d -> k (h s) d")).then_inc(sub_in, 16)

        @block.gpsimd
        def _(pool):
            nc.gpsimd.memset(ident[:], 0.0).then_inc(consts, 1)
            nc.gpsimd.memset(core.eps[:], EPS).then_inc(consts, 1)
            pool.wait_ge(consts, 2)
            nc.gpsimd.affine_select(out=ident[:], in_=ident[:], compare_op=ALU.not_equal, fill=1.0, base=0,
                                    pattern=[[-1, P]], channel_multiplier=1).then_inc(consts, 1)

        @block.scalar
        def _(act):
            act.wait_ge(consts, 3)
            for t in range(TILES):
                act.wait_ge(loaded[t], 16)
                nc.scalar.activation(scratch[:], h[:, t, :], ACT.Square, accum_out=rstd[:, t:t + 1]).then_inc(squares, 1)
                act.wait_ge(squares, t + 1)
                nc.scalar.activation(rstd[:, t:t + 1], rstd[:, t:t + 1], ACT.Sqrt, bias=core.eps[:, 0:1],
                                     scale=1.0 / D).then_inc(rooted, 1)
            for j in range(4):
                act.wait_ge(sub_turned, j + 1)
                nc.scalar.activation(core.skT[:, 4 * j:4 * j + 4, :], ps[:, 4 + j, :].rearrange("p (a k) -> p a k", k=PK), ACT.Copy)

        @block.vector
        def _(dve):
            def normalise(t):
                dve.wait_ge(rooted, t + 1)
                dve.wait_ge(loaded[t], 16)
                nc.vector.reciprocal(rstd[:, t:t + 1], rstd[:, t:t + 1]).then_inc(rstd_ready, 1)
                dve.wait_ge(rstd_ready, t + 1)
                if t >= 2:
                    dve.wait_ge(t_full, t - 1)
                nc.vector.tensor_scalar(xn[:, t % 2, :], h[:, t, :], rstd[:, t:t + 1], None, ALU.mult).then_inc(xn_full, 1)

            dve.wait_ge(small_in, 16)
            normalise(0)
            for t in range(TILES):
                if t + 1 < TILES:
                    normalise(t + 1)
                b = t % 2
                dve.wait_ge(t_full, t + 1)
                nc.vector.tensor_tensor(uT[:, :, t * P:(t + 1) * P],
                                        ps[:, 2 * b:2 * b + 2, :].rearrange("p k (c n) -> p (k c) n", n=P),
                                        gT[:].unsqueeze(2).broadcast_to([P, DCH, P]), ALU.mult).then_inc(t_free, 1)

        @block.tensor
        def _(pe):
            pe.wait_ge(consts, 3)
            for t in range(TILES):
                pe.wait_ge(xn_full, t + 1)
                if t >= 2:
                    pe.wait_ge(t_free, t - 1)
                transpose_row(nc, core, ps[:, 2 * (t % 2):2 * (t % 2) + 2, :], xn[:, t % 2, :], DCH).then_inc(t_full, 1)
                if t >= 4:
                    pe.wait_ge(sub_in, 16)
                    for a in range(4):
                        last = nc.tensor.transpose(ps[:, t, a * P:(a + 1) * P], sub[:, 4 * (t - 4) + a, :], core.ident[:])
                    last.then_inc(sub_turned, 1)


def pipeline(eng, begin, step, irregular=0):
    begin()
    for t in range(irregular):
        step(t, t % 2, True, True)
    pairs = (TILES - 2 - irregular) // 2
    if pairs > 1:
        with eng.Fori(0, pairs) as i:
            for b in range(2):
                step(i * 2 + (irregular + b), (irregular + b) % 2, True, True)
    for t in range(irregular + (2 * pairs if pairs > 1 else 0), TILES):
        step(t, t % 2, t + 2 < TILES, t + 1 < TILES)


def transpose_row(nc, core, out, src, n):
    flat = out.rearrange("p k (c n) -> p (k c) n", n=P)
    for c in range(n):
        last = nc.tensor.transpose(flat[:, c, :], src[:, c * P:(c + 1) * P], core.ident[:])
    return last


def attention(nc, core, uT, y, spare, ycol, tag, weights, nq, nkv, ktiles, gains, sinks, rel_bias):
    wq, wk, wv = nq * HD, nkv * HD, nkv * HD
    nqk, width, keys = nq + nkv, wq + wk + wv, ktiles * P
    full = ktiles - 1
    s_banks = (keys + 511) // 512
    t_banks = (nq * P + 511) // 512
    bank_q, bank_k = 0, t_banks
    bank_s = [bank_k + 1, bank_k + 1 + s_banks]
    bank_p = bank_k + 1 + 2 * s_banks
    assert bank_p + 2 <= 8
    n_neg = 2 if sinks is not None else 1

    window = keys - P

    def key_tiles(t):
        return min(t + 1, ktiles) if isinstance(t, int) else ktiles

    def units(t):
        assert nq * key_tiles(t) % 4 == 0
        return nq * key_tiles(t) // 4

    before_full = sum(units(t) for t in range(full))
    since_full = before_full - full * (nq * ktiles // 4)

    def unit_no(t, u):
        if isinstance(t, int):
            return sum(units(e) for e in range(t)) + u
        return t * (nq * ktiles // 4) + (since_full + u)

    def unit_parity(t, par, u):
        return (unit_no(t, u) if isinstance(t, int) else par * (nq * ktiles // 4) + since_full + u) % 2

    def last_head(t, u):
        return (4 * u + 3) // key_tiles(t)

    with ExitStack() as ctx:
        ph = Phase(nc, ctx, tag)
        w = ph.sb("w", [P, DCH, width])
        qk = spare.rearrange("p (t n) -> p t n", t=TILES) if nqk * HD <= 512 else ph.sb("qk", [P, TILES, nqk * HD])
        v = ph.sb("v", [P, TILES, wv])
        sq = ph.sb("sq", [P, 2, nqk * HD])
        rstd = ph.sb("rstd", [P, TILES * nqk])
        gain = ph.sb("gain", [HD, 2])
        bias = ph.sb("bias", [P, nq, keys])
        kT = ph.sb("kT", [HD, nkv, SEQ])
        qT = ph.sb("qT", [HD, nq * P])
        qkn = ph.sb("qkn", [P, nqk * HD])
        logits = ph.sb("logits", [P, 2, nq, keys])
        rowmax = ph.sb("rowmax", [P, nq])
        negmax = ph.sb("negmax", [P, nq])
        rowsum = ph.sb("rowsum", [P, nq])
        sink = ph.sb("sink", [P, nq])
        sinkexp = ph.sb("sinkexp", [P, nq])
        inv = ph.sb("inv", [P, nq])
        pT = ph.sb("pT", [P, 2, 4, P])
        w_in_ = [ph.sem(f"w{c}_in") for c in range(0, DCH, 2)]
        (small_in, row_in, skew_out, bias_in, made, bias_ready,
         proj_full, proj_free, sq_full, sq_free, v_full, rooted, rstd_ready,
         qkn_full, turned, qT_full, kT_full, s_full, s_free, neg_ready, p_full, sink_full,
         pt_full, pt_copied, pt_used, o_full, o_free, link, held) = ph.sems(
            "small_in row_in skew_out bias_in made bias_ready "
            "proj_full proj_free sq_full sq_free v_full rooted rstd_ready "
            "qkn_full turned qT_full kT_full s_full s_free neg_ready p_full sink_full "
            "pt_full pt_copied pt_used o_full o_free link held")
        ps = core.ps
        n_small = 2 + (1 if sinks is not None else 0)
        if rel_bias is not None:
            pitch = keys + P
            rows = logits[0:nq].rearrange("p b h k -> p (b h k)")
            ext, head_row = rows[:, 0:pitch], rows[:, pitch:pitch + REL_SIZE]
            skew = nc.dram_tensor(f"{tag}_skew", (nq, P * pitch), F32, kind="Internal").ap()
        block = ph.open_block()

        @block.sync
        def _(sp):
            if rel_bias is not None:
                sp.dma_start(head_row, rel_bias).then_inc(row_in, 16)
            for c in range(0, DCH, 2):
                at = 0
                for cols, n in zip(weights, (wq, wk, wv)):
                    sp.dma_start(w[:, c:c + 2, at:at + n],
                                 cols[c * P:(c + 2) * P].rearrange("(c p) n -> p c n", p=P)).then_inc(w_in_[c // 2], 16)
                    at += n
            for j in range(2):
                sp.dma_start(gain[:, j:j + 1], gains[j].rearrange("(p o) -> p o", o=1)).then_inc(small_in, 16)
            if sinks is not None:
                sp.dma_start(sink[:], sinks.partition_broadcast(P)).then_inc(small_in, 16)
            if rel_bias is not None:
                sp.wait_ge(made, 2)
                for i in range(nq):
                    sp.dma_start(skew[i:i + 1, :].rearrange("o (q m) -> o q m", q=P),
                                 ext[i:i + 1, :].unsqueeze(1).broadcast_to([1, P, pitch])).then_inc(skew_out, 16)
                sp.wait_ge(skew_out, 16 * nq)
                for i in range(nq):
                    rows = skew[i, P - 1:P - 1 + P * (pitch - 1)].rearrange("(q m) -> q m", q=P)
                    sp.dma_start(bias[:, i, :], rows[:, 0:keys]).then_inc(bias_in, 16)
                sp.wait_ge(bias_in, 16 * nq)

        @block.gpsimd
        def _(pool):
            if rel_bias is None:
                pool.iota(bias[:, 0, :], pattern=[[-1, keys]], base=window, channel_multiplier=1,
                          allow_small_or_imprecise_dtypes=True).then_inc(made, 1)

        @block.scalar
        def _(act):
            def root(t):
                act.wait_ge(sq_free, t + 3)
                part = rstd[:, t * nqk:(t + 1) * nqk]
                nc.scalar.activation(part, part, ACT.Sqrt, bias=core.eps[:, 0:1], scale=1.0 / HD).then_inc(rooted, 1)

            for t in range(TILES):
                act.wait_ge(proj_full, t + 1)
                src = ps[:, 2 * (t % 4):2 * (t % 4) + 2, :].rearrange("p k n -> p (k n)")
                nc.scalar.activation(qk[:, t, :], src[:, 0:nqk * HD], ACT.Copy).then_inc(proj_free, 1)
                act.wait_ge(sq_free, t + 1)
                nc.scalar.activation(sq[:, t % 2, :], src[:, 0:nqk * HD], ACT.Square).then_inc(sq_full, 1)
                if t:
                    root(t - 1)
            root(TILES - 1)
            act.wait_ge(small_in, 16 * n_small)
            def copy_turned(t):
                act.wait_ge(turned, t + 1)
                nc.scalar.activation(qT[:], ps[0:HD, bank_q:bank_q + t_banks, :].rearrange("p k n -> p (k n)")[:, 0:nq * P],
                                     ACT.Copy, scale=gain[:, 0:1]).then_inc(qT_full, 1)

            def exponentials(t, par, heads):
                for i in heads:
                    part = logits[:, par, i, 0:key_tiles(t) * P]
                    nc.scalar.activation(part, part, ACT.Exp, bias=negmax[:, i:i + 1],
                                         accum_out=rowsum[:, i:i + 1]).then_inc(p_full, 1)

            def step(t, par, normalise, scores):
                act.wait_ge(neg_ready, t * n_neg + n_neg)
                needed = [last_head(t, u) + 1 for u in range(units(t))] + [nq, nq]
                exponentials(t, par, range(needed[1]))
                if scores:
                    copy_turned(t + 1)
                if sinks is not None:
                    nc.scalar.activation(sinkexp[:], sinkexp[:], ACT.Exp).then_inc(sink_full, 1)
                for u in range(units(t)):
                    n = unit_parity(t, par, u)
                    act.wait_ge(pt_full, unit_no(t, u + 1))
                    act.wait_ge(pt_used, unit_no(t, u + 1))
                    nc.scalar.activation(pT[:, n].rearrange("p k n -> p (k n)"), ps[:, bank_p + n, :], ACT.Copy).then_inc(pt_copied, 1)
                    exponentials(t, par, range(needed[u + 1], needed[u + 2]))

            act.sem_inc(pt_copied, 2)
            pipeline(act, lambda: copy_turned(0), step, irregular=full)

        @block.vector
        def _(dve):
            dve.sem_inc(sq_free, 2)
            dve.sem_inc(s_free, 2)
            dve.sem_inc(o_free, 2)
            once = Chain(dve, bias_ready)

            def extend_rows():
                dve.wait_ge(row_in, 16)
                far = window + P - 1 - REL_PAST
                ext_rev = ext[:, far:far + REL_SIZE]
                nc.vector.tensor_copy(ext_rev, head_row[:, ::-1]).then_inc(made, 1)
                dve.wait_ge(made, 1)
                once.link(nc.vector.tensor_scalar(ext[:, 0:far], head_row[:, REL_SIZE - 1:REL_SIZE].broadcast_to([nq, far]),
                                                  1.0, None, ALU.mult))
                nc.vector.tensor_scalar(ext[:, far + REL_SIZE:], head_row[:, 0:1].broadcast_to([nq, pitch - far - REL_SIZE]),
                                        1.0, None, ALU.mult).then_inc(made, 1)

            def make_bias():
                if rel_bias is None:
                    dve.wait_ge(made, 1)
                    once.link(nc.vector.tensor_scalar(bias[:, 1, :], bias[:, 0, :], -1.0, None, ALU.mult))
                    once.link(nc.vector.tensor_tensor(bias[:, 0, :], bias[:, 0, :], bias[:, 1, :], ALU.max))
                    for i in reversed(range(nq)):
                        slope = float(np.float32(2.0 ** (-8.0 * (i + 1) / nq)))
                        once.link(nc.vector.tensor_scalar(bias[:, i, :], bias[:, 0, :], -slope / HD ** -0.5, None, ALU.mult))
                else:
                    dve.wait_ge(bias_in, 16 * nq)
                    flat = bias[:].rearrange("p h k -> p (h k)")
                    once.link(nc.vector.tensor_scalar(flat, flat, HD ** 0.5, None, ALU.mult))
                early, late = bias[0:CHUNK], bias[CHUNK:P]
                once.link(nc.vector.memset(early[:, :, keys - CHUNK:keys], NEG))
                if rel_bias is None:
                    once.link(nc.vector.memset(early[:, :, 0:CHUNK], NEG))
                    once.link(nc.vector.memset(late[:, :, 0:2 * CHUNK], NEG))
                else:
                    once.link(nc.vector.memset(late[:, :, 0:CHUNK], NEG))

            def invert(t):
                dve.wait_ge(rooted, t + 1)
                part = rstd[:, t * nqk:(t + 1) * nqk]
                nc.vector.reciprocal(part, part).then_inc(rstd_ready, 1)

            def normalise_qk(t):
                nc.vector.tensor_tensor(qkn[:].rearrange("p (h d) -> p h d", d=HD),
                                        qk[:, bass.ds(t, 1), :].rearrange("p o (h d) -> p (o h) d", d=HD),
                                        rstd[:, bass.ds(t * nqk, nqk)].unsqueeze(2).broadcast_to([P, nqk, HD]),
                                        ALU.mult).then_inc(qkn_full, 1)

            def copy_keys(t):
                dve.wait_ge(turned, t + 1)
                nc.vector.tensor_scalar(kT[:, :, bass.ds(t * P, P)],
                                        ps[0:HD, bank_k, 0:nkv * P].rearrange("p (k n) -> p k n", n=P),
                                        gain[0:HD, 1:2], None, ALU.mult).then_inc(kT_full, 1)

            def read_scores(t, par, middle=None):
                for i in range(nq):
                    dve.wait_ge(s_full, t * nq + (i + 1))
                    dve.sem_inc(held, 1)
                    b, n = bank_s[i % 2], key_tiles(t) * P
                    nc.vector.tensor_tensor_reduce(
                        out=logits[:, par, i, 0:n], in0=ps[:, b:b + s_banks, :].rearrange("p k n -> p (k n)")[:, 0:n],
                        in1=bias[:, i, keys - n:], scale=HD ** -0.5, scalar=sink[:, i:i + 1] if sinks is not None else NEG,
                        op0=ALU.add, op1=ALU.max, accum_out=rowmax[:, i:i + 1]).then_inc(s_free, 1)
                    if middle is not None and i == nq // 2:
                        middle()
                dve.wait_ge(s_free, t * nq + (nq + 2))
                nc.vector.tensor_scalar(negmax[:], rowmax[:], -1.0, None, ALU.mult).then_inc(neg_ready, 1)
                if sinks is not None:
                    dve.wait_ge(neg_ready, t * 2 + 1)
                    nc.vector.tensor_tensor(sinkexp[:], sink[:], negmax[:], ALU.add).then_inc(neg_ready, 1)

            def begin():
                if rel_bias is not None:
                    extend_rows()
                for t in range(TILES):
                    dve.wait_ge(sq_full, t + 1)
                    nc.vector.tensor_copy(v[:, t, :],
                                          ps[:, 2 * (t % 4):2 * (t % 4) + 2, :].rearrange("p k n -> p (k n)")[:, nqk * HD:width]).then_inc(v_full, 1)
                    nc.vector.tensor_reduce(rstd[:, t * nqk:(t + 1) * nqk], sq[:, t % 2, :].rearrange("p (h d) -> p h d", d=HD),
                                            axis=AX.X, op=ALU.add).then_inc(sq_free, 1)
                    if t:
                        invert(t - 1)
                    if t == 1:
                        dve.wait_ge(rstd_ready, 1)
                        normalise_qk(0)
                    if t == 4:
                        make_bias()
                invert(TILES - 1)
                dve.wait_ge(small_in, 16 * n_small)
                dve.wait_ge(rstd_ready, TILES)
                copy_keys(0)
                normalise_qk(1)
                read_scores(0, 0)

            def step(t, par, normalise, scores):
                def invert_sums():
                    dve.wait_ge(p_full, t * nq + nq)
                    dve.wait_ge(o_free, t + 2)
                    chain = Chain(dve, link, t * n_neg)
                    if sinks is not None:
                        dve.wait_ge(sink_full, t + 1)
                        chain.link(nc.vector.tensor_tensor(inv[:], rowsum[:], sinkexp[:], ALU.add))
                        chain.link(nc.vector.reciprocal(inv[:], inv[:]))
                    else:
                        chain.link(nc.vector.reciprocal(inv[:], rowsum[:]))

                if scores:
                    copy_keys(t + 1)
                if normalise:
                    normalise_qk(t + 2)
                if scores:
                    read_scores(t + 1, 1 - par, middle=invert_sums)
                else:
                    invert_sums()
                dve.wait_ge(o_full, t + 1)
                nc.vector.tensor_tensor(
                    y[:, bass.ds(t, 1), ycol:ycol + wq].rearrange("p o (h d) -> p (o h) d", d=HD),
                    ps[:, bank_k, 0:wq].rearrange("p (h d) -> p h d", d=HD),
                    inv[:].unsqueeze(2).broadcast_to([P, nq, HD]), ALU.mult).then_inc(o_free, 1)

            pipeline(dve, begin, step, irregular=full)

        @block.tensor
        def _(pe):
            for t in range(TILES):
                if t >= 4:
                    pe.wait_ge(sq_full, t - 3)
                    pe.wait_ge(proj_free, t - 3)
                    pe.wait_ge(v_full, t - 3)
                b = 2 * (t % 4)
                for lo in range(0, width, 512):
                    hi = min(lo + 512, width)
                    for c in range(DCH):
                        if t == 0 and lo == 0 and c % 2 == 0:
                            pe.wait_ge(w_in_[c // 2], 48)
                        last = nc.tensor.matmul(ps[:, b + lo // 512, 0:hi - lo], uT[:, c, t * P:(t + 1) * P],
                                                w[:, c, lo:hi], start=(c == 0), stop=(c == DCH - 1))
                last.then_inc(proj_full, 1)
            pe.wait_ge(sq_full, TILES)
            pe.wait_ge(proj_free, TILES)
            pe.wait_ge(v_full, TILES)

            def turn(t):
                pe.wait_ge(qkn_full, t + 1)
                pe.sem_inc(held, 1)
                for i in range(nqk):
                    if i == nq:
                        pe.wait_ge(o_free, t + 1)
                        pe.sem_inc(held, 1)
                    b, col = (bank_q + i * P // 512, i * P % 512) if i < nq else (bank_k, (i - nq) * P)
                    last = nc.tensor.transpose(ps[0:HD, b, col:col + P], qkn[:, i * HD:(i + 1) * HD], core.ident[:])
                last.then_inc(turned, 1)

            def score_heads(t, heads):
                for i in heads:
                    if i == 0:
                        pe.wait_ge(qT_full, t + 1)
                        pe.wait_ge(kT_full, t + 1)
                    pe.wait_ge(s_free, t * nq + (i + 1))
                    pe.sem_inc(held, 1)
                    n_keys = key_tiles(t) * P
                    for lo in range(0, n_keys, 512):
                        n = min(512, n_keys - lo)
                        last = nc.tensor.matmul(ps[:, bank_s[i % 2] + lo // 512, 0:n], qT[:, i * P:(i + 1) * P],
                                                kT[:, i * nkv // nq, bass.ds(t * P + (P + lo - n_keys), n)], start=True, stop=True)
                    last.then_inc(s_full, 1)

            def turn_unit(t, par, u):
                pe.wait_ge(p_full, t * nq + (last_head(t, u) + 1))
                pe.wait_ge(pt_copied, unit_no(t, u + 1))
                for j in range(4):
                    i, k = divmod(4 * u + j, key_tiles(t))
                    last = nc.tensor.transpose(ps[:, bank_p + unit_parity(t, par, u), j * P:(j + 1) * P],
                                               logits[:, par, i, k * P:(k + 1) * P], core.ident[:])
                last.then_inc(pt_full, 1)

            def multiply_unit(t, par, u):
                pe.wait_ge(pt_copied, unit_no(t, u + 3))
                for j in range(4):
                    i, k = divmod(4 * u + j, key_tiles(t))
                    kv = i * nkv // nq
                    last = nc.tensor.matmul(ps[:, bank_k, i * HD:(i + 1) * HD], pT[:, unit_parity(t, par, u), j, :],
                                            v[:, bass.ds(t + (1 + k - key_tiles(t)), 1), kv * HD:(kv + 1) * HD].rearrange("p o d -> p (o d)"),
                                            start=(k == 0), stop=(k == key_tiles(t) - 1))
                last.then_inc(pt_used, 1)
                if u == units(t) - 1:
                    pe.wait_ge(pt_used, unit_no(t, units(t) + 2))
                    pe.sem_inc(o_full, 1)

            def begin():
                turn(0)
                score_heads(0, range(nq))

            def step(t, par, normalise, scores):
                if scores:
                    turn(t + 1)
                for u in range(min(2, units(t))):
                    turn_unit(t, par, u)
                if not scores:
                    pe.wait_ge(o_free, t + 2)
                per_unit = -(-nq // units(t))
                for u in range(units(t)):
                    if scores:
                        score_heads(t + 1, range(u * per_unit, min(nq, (u + 1) * per_unit)))
                    multiply_unit(t, par, u)
                    if u + 2 < units(t):
                        turn_unit(t, par, u + 2)

            pe.sem_inc(pt_used, 2)
            pipeline(pe, begin, step, irregular=full)


def project_out(nc, core, tag, y, nch, gain, w_rows, stream=None, w_query=None):
    with ExitStack() as ctx:
        ph = Phase(nc, ctx, tag)
        w = ph.sb("w", [P, nch, D])
        scratch = ph.sb("scratch", [P, nch * P])
        yn = ph.sb("yn", [P, 2, nch * P])
        yT = ph.sb("yT", [P, 2, nch * P])
        gT = ph.sb("gT", [P, nch])
        rstd = ph.sb("rstd", [P, TILES])
        w_in_ = [ph.sem(f"w{c}_in") for c in range(0, nch, 2)]
        stored, held, small_in, squares, rooted, rstd_ready, yn_full, t_full, yT_full, out_full, out_free = ph.sems(
            "stored held small_in squares rooted rstd_ready yn_full t_full yT_full out_full out_free")
        block = ph.open_block()
        h, ps = core.h, core.ps

        @block.sync
        def _(sp):
            sp.dma_start(gT[:], gain.rearrange("(c p) -> p c", p=P), allow_slow_non_contiguous=True).then_inc(small_in, 16)
            for c in range(0, nch, 2):
                sp.dma_start(w[:, c:c + 2, :], w_rows[c * P:(c + 2) * P].rearrange("(c p) n -> p c n", p=P)).then_inc(w_in_[c // 2], 16)
            if stream is not None:
                sp.dma_start(core.wq[:, 0], w_query[:, 0:PH // 2 * PKD].rearrange("(c p) n -> p c n", p=P)).then_inc(core.wq0_in, 16)
                for t in range(TILES):
                    sp.wait_ge(out_free, t + 3)
                    sp.dma_start(stream[t * P:(t + 1) * P, :], h[:, t, :]).then_inc(stored, 16)
                sp.wait_ge(stored, 16 * TILES)

        @block.scalar
        def _(act):
            with act.Fori(0, TILES // 2) as i:
                for b in range(2):
                    root = rstd[:, bass.ds(i * 2 + b, 1)]
                    nc.scalar.activation(scratch[:], y[:, bass.ds(i * 2 + b, 1), :].rearrange("p o d -> p (o d)"), ACT.Square,
                                         accum_out=root).then_inc(squares, 1)
                    act.wait_ge(squares, i * 2 + (b + 1))
                    act.sem_inc(held, 1)
                    nc.scalar.activation(root, root, ACT.Sqrt, bias=core.eps[:, 0:1], scale=1.0 / (nch * P)).then_inc(rooted, 1)

        @block.vector
        def _(dve):
            def normalise(t, b):
                dve.wait_ge(rooted, t + 1)
                nc.vector.reciprocal(rstd[:, bass.ds(t, 1)], rstd[:, bass.ds(t, 1)]).then_inc(rstd_ready, 1)
                dve.wait_ge(rstd_ready, t + 1)
                nc.vector.tensor_scalar(yn[:, b, :], y[:, bass.ds(t, 1), :].rearrange("p o d -> p (o d)"),
                                        rstd[:, bass.ds(t, 1)], None, ALU.mult).then_inc(yn_full, 1)

            def scale(t, b):
                dve.wait_ge(t_full, t + 1)
                nc.vector.tensor_tensor(
                    yT[:, b, :].rearrange("p (c n) -> p c n", n=P),
                    ps[:, 2 * b:2 * b + 2, :].rearrange("p k (c n) -> p (k c) n", n=P)[:, 0:nch, :],
                    gT[:].unsqueeze(2).broadcast_to([P, nch, P]), ALU.mult).then_inc(yT_full, 1)

            def add(t, b):
                dve.wait_ge(out_full, t + 1)
                row = h[:, bass.ds(t, 1), :].rearrange("p o d -> p (o d)")
                nc.vector.tensor_tensor(row, ps[:, 4 + 2 * b:6 + 2 * b, :].rearrange("p k n -> p (k n)"), row,
                                        ALU.add).then_inc(out_free, 1)

            dve.sem_inc(out_free, 2)
            dve.wait_ge(small_in, 16)
            normalise(0, 0)
            normalise(1, 1)
            scale(0, 0)
            with dve.Fori(0, TILES // 2 - 1) as i:
                for b in range(2):
                    scale(i * 2 + (b + 1), 1 - b)
                    normalise(i * 2 + (b + 2), b)
                    add(i * 2 + b, b)
            scale(TILES - 1, 1)
            add(TILES - 2, 0)
            add(TILES - 1, 1)

        @block.tensor
        def _(pe):
            def turn(t, b):
                pe.wait_ge(yn_full, t + 1)
                for c in range(nch):
                    last = nc.tensor.transpose(ps[:, 2 * b + c // 4, c % 4 * P:(c % 4 + 1) * P],
                                               yn[:, b, c * P:(c + 1) * P], core.ident[:])
                last.then_inc(t_full, 1)

            def multiply(t, b, weights_in=False):
                pe.wait_ge(yT_full, t + 1)
                pe.wait_ge(out_free, t + 1)
                for half in range(2):
                    for c in range(nch):
                        if weights_in and half == 0 and c % 2 == 0:
                            pe.wait_ge(w_in_[c // 2], 16)
                        last = nc.tensor.matmul(ps[:, 4 + 2 * b + half, :], yT[:, b, c * P:(c + 1) * P],
                                                w[:, c, half * 512:(half + 1) * 512], start=(c == 0), stop=(c == nch - 1))
                last.then_inc(out_full, 1)

            turn(0, 0)
            turn(1, 1)
            multiply(0, 0, weights_in=True)
            with pe.Fori(0, TILES // 2 - 1) as i:
                for b in range(2):
                    turn(i * 2 + (b + 2), b)
                    multiply(i * 2 + (b + 1), 1 - b)
            multiply(TILES - 1, 1)


def mixer_a(nc, core, uT, y, spare, io):
    w = io["w_in"][0]
    kcol, vcol = A_WIDTH, A_WIDTH + A_KV * HD
    attention(nc, core, uT, y, spare, 0, "a", [w[:, 0:kcol], w[:, kcol:vcol], w[:, vcol:A_QKV]], A_HEADS, A_KV, 2,
              [io["a_q_norm"][0], io["a_k_norm"][0]], io["a_sinks"][0], None)
    project_out(nc, core, "aout", y, A_WIDTH // P, io["a_out_norm"][0], io["w_out"][0, 0:A_WIDTH, :])


def mixer_c(nc, core, uT, y, spare, io):
    w = io["w_in"][0]
    for part in range(C_HEADS // C_PASS):
        n = C_PASS * HD
        at = A_QKV + B_IN + part * n
        attention(nc, core, uT, y, spare, part * n, f"c{part}", [w[:, at + j * C_WIDTH:at + j * C_WIDTH + n] for j in range(3)],
                  C_PASS, C_PASS, 5, [io["c_q_norm"][0], io["c_k_norm"][0]], None,
                  io["c_rel_bias"][0, part * C_PASS:(part + 1) * C_PASS, :])
    project_out(nc, core, "cout", y, C_WIDTH // P, io["c_out_norm"][0], io["w_out"][0, A_WIDTH + B_WIDTH:, :])


class ScanTables:

    def __init__(self, nc, ctx):
        sb = lambda name, shape: ctx.enter_context(nc.sbuf_tensor(f"b_{name}", shape, F32))
        HB = TILES * B_HEADS
        self.rows = sb("rows", [P, 3, B_HEADS])
        self.dt = sb("dt", [P, HB])
        self.cs = sb("cs", [P, HB])
        self.from_start = sb("from_start", [P, HB])
        self.to_end = sb("to_end", [P, HB])
        self.whole = sb("whole", [P, HB])
        self.tri = sb("tri", [P, P])
        self.cs_rows = nc.dram_tensor("b_cs_rows", (HB, P), F32, kind="Internal").ap()


def mixer_b_project(nc, core, uT, z, xbc, tab, io):
    HB = TILES * B_HEADS
    zcol = A_QKV
    xcol = zcol + B_WIDTH
    dcol = xcol + B_XBC
    XCH = B_XBC // P
    w_in = io["w_in"][0]
    slabs = [zcol, zcol + 512, xcol, xcol + 512, xcol + 1024]
    with ExitStack() as ctx:
        ph = Phase(nc, ctx, "bp")
        w = ph.sb("w", [P, 2, DCH, 512])
        wdt = ph.sb("wdt", [P, DCH, B_HEADS])
        taps = ph.sb("taps", [P, XCH, B_CONV])
        cbias = ph.sb("cbias", [P, XCH])
        acc = ph.sb("acc", [P, 2, SEQ])
        ones = ph.sb("ones", [P, P])
        soft = ph.sb("soft", [P, 3, HB])
        dtA = ph.sb("dtA", [P, HB])
        csT = ph.sb("csT", [HB, P])
        first_in = [ph.sem(f"first{c}_in") for c in range(0, DCH, 2)]
        slab_in = [ph.sem(f"slab{j}_in") for j in range(len(slabs))]
        (small_in, rows_in, history, unit_full, unit_copied, conv_full, silu_full, link,
         consts, dt_full, pre, exped, sums, csT_full, spilled, tables) = ph.sems(
            "small_in rows_in history unit_full unit_copied conv_full silu_full link "
            "consts dt_full pre exped sums csT_full spilled tables")
        block = ph.open_block()
        ps = core.ps
        dt_ps, cs_ps, csT_ps, total_ps = (ps[:, 7, j * P:(j + 1) * P] for j in range(4))
        n_z = 2 * TILES
        n_units = n_z + 2 * XCH

        @block.sync
        def _(sp):
            for j, col in enumerate(slabs):
                if j >= 2:
                    sp.wait_ge(unit_full, 8 * (j - 1))
                if j:
                    sp.dma_start(w[:, j % 2], w_in[:, col:col + 512].rearrange("(c p) n -> p c n", p=P)).then_inc(slab_in[j], 16)
                else:
                    for c in range(0, DCH, 2):
                        sp.dma_start(w[:, 0, c:c + 2], w_in[c * P:(c + 2) * P, col:col + 512].rearrange(
                            "(c p) n -> p c n", p=P)).then_inc(first_in[c // 2], 16)
                    sp.dma_start(wdt[:], w_in[:, dcol:dcol + B_HEADS].rearrange("(c p) n -> p c n", p=P)).then_inc(small_in, 16)
                    sp.dma_start(cbias[:], io["b_conv_b"][0].rearrange("(c p) -> p c", p=P),
                                 allow_slow_non_contiguous=True).then_inc(small_in, 16)
                    for k in range(B_CONV):
                        sp.dma_start(taps[:, :, k], io["b_conv_w"][0, k].rearrange("(c p) -> p c", p=P),
                                     allow_slow_non_contiguous=True).then_inc(small_in, 16)
                    for k, name in enumerate(["b_dt_bias", "b_a_log", "b_d"]):
                        sp.dma_start(tab.rows[:, k, :], io[name][0].partition_broadcast(P)).then_inc(rows_in, 16)
            sp.wait_ge(csT_full, 1)
            sp.dma_start(tab.cs_rows, csT[:]).then_inc(spilled, 16)
            sp.wait_ge(spilled, 16)

        @block.gpsimd
        def _(pool):
            nc.gpsimd.memset(xbc[:, :, 0:B_CONV - 1], 0.0).then_inc(history, 1)
            fill = Chain(pool, consts)
            fill.link(nc.gpsimd.memset(tab.tri[:], 1.0))
            fill.link(nc.gpsimd.affine_select(out=tab.tri[:], in_=tab.tri[:], compare_op=ALU.is_ge, fill=0.0, base=0,
                                              pattern=[[1, P]], channel_multiplier=-1))
            fill.link(nc.gpsimd.memset(ones[:], 1.0))

        @block.scalar
        def _(act):
            for u in range(n_z):
                act.wait_ge(unit_full, u + 1)
                s, t = divmod(u, TILES)
                nc.scalar.activation(z[:, t, s * 512:(s + 1) * 512], ps[:, u % 7, :], ACT.Silu).then_inc(unit_copied, 1)
                if u == TILES + 1:
                    act.wait_ge(pre, 3)
                    nc.scalar.activation(soft[:, 1, :], soft[:, 1, :], ACT.Exp, scale=-1.0).then_inc(exped, 1)
                    nc.scalar.activation(tab.rows[:, 1, :], tab.rows[:, 1, :], ACT.Exp).then_inc(exped, 1)
                    act.wait_ge(exped, 2)
                    nc.scalar.activation(soft[:, 1, :], soft[:, 1, :], ACT.Ln, bias=1.0).then_inc(exped, 1)
            act.wait_ge(sums, 1)
            nc.scalar.activation(tab.cs[:], cs_ps, ACT.Copy).then_inc(exped, 1)
            nc.scalar.activation(csT[:], csT_ps, ACT.Copy).then_inc(csT_full, 1)
            nc.scalar.activation(tab.from_start[:], cs_ps, ACT.Exp).then_inc(tables, 1)
            nc.scalar.activation(tab.whole[:], total_ps, ACT.Exp).then_inc(tables, 1)
            act.wait_ge(pre, 6)
            nc.scalar.activation(tab.to_end[:], tab.to_end[:], ACT.Exp).then_inc(tables, 1)
            for j in range(XCH + 1):
                if j < XCH:
                    for half in range(2):
                        u = n_z + 2 * j + half
                        act.wait_ge(unit_full, u + 1)
                        nc.scalar.activation(xbc[:, j, 3 + half * 512:3 + (half + 1) * 512], ps[:, u % 7, :],
                                             ACT.Copy).then_inc(unit_copied, 1)
                if j:
                    act.wait_ge(conv_full, j)
                    nc.scalar.activation(xbc[:, j - 1, 3:], acc[:, (j - 1) % 2, :], ACT.Silu).then_inc(silu_full, 1)

        @block.vector
        def _(dve):
            dve.wait_ge(rows_in, 48)
            dve.wait_ge(dt_full, 1)
            first = Chain(dve, pre)
            by_tile = lambda ap: ap.rearrange("p (t h) -> p t h", h=B_HEADS)
            first.link(nc.vector.tensor_tensor(by_tile(soft[:, 0, :]), by_tile(dt_ps),
                                               tab.rows[:, 0:1, :].broadcast_to([P, TILES, B_HEADS]), ALU.add))
            first.link(nc.vector.tensor_scalar(soft[:, 2, :], soft[:, 0, :], 0.0, None, ALU.max))
            first.link(nc.vector.scalar_tensor_tensor(soft[:, 1, :], soft[:, 2, :], 2.0, soft[:, 0, :], ALU.mult, ALU.subtract))
            dve.wait_ge(exped, 3)
            first.link(nc.vector.tensor_tensor(tab.dt[:], soft[:, 1, :], soft[:, 2, :], ALU.add))
            first.link(nc.vector.scalar_tensor_tensor(by_tile(dtA[:]), by_tile(tab.dt[:]), -1.0,
                                                      tab.rows[:, 1:2, :].broadcast_to([P, TILES, B_HEADS]), ALU.mult, ALU.mult))
            dve.wait_ge(sums, 1)
            dve.wait_ge(exped, 4)
            dve.wait_ge(tables, 2)
            first.link(nc.vector.tensor_tensor(tab.to_end[:], total_ps, tab.cs[:], ALU.subtract))
            dve.wait_ge(small_in, 16 * (2 + B_CONV))
            dve.wait_ge(history, 1)
            chain = Chain(dve, link)
            for j in range(XCH):
                dve.wait_ge(unit_copied, n_z + 2 * j + 2)
                if j >= 2:
                    dve.wait_ge(silu_full, j - 1)
                a = acc[:, j % 2, :]
                chain.link(nc.vector.tensor_scalar(a, xbc[:, j, 3:], taps[:, j, 3:4], cbias[:, j:j + 1], ALU.mult, ALU.add))
                for k in range(B_CONV - 1):
                    ins = nc.vector.scalar_tensor_tensor(a, xbc[:, j, k:k + SEQ], taps[:, j, k:k + 1], a, ALU.mult, ALU.add)
                    if k < B_CONV - 2:
                        chain.link(ins)
                ins.then_inc(conv_full, 1)

        @block.tensor
        def _(pe):
            u = 0
            for j in range(len(slabs)):
                if j:
                    pe.wait_ge(slab_in[j], 16)
                for part in range(8):
                    if u >= 7:
                        pe.wait_ge(unit_copied, u - 6)
                    for c in range(DCH):
                        if u == 0 and c % 2 == 0:
                            pe.wait_ge(first_in[c // 2], 16)
                        if j < 2:
                            lhsT, rhs = uT[:, c, part * P:(part + 1) * P], w[:, j % 2, c, :]
                        else:
                            lhsT = w[:, j % 2, c, part // 2 * P:(part // 2 + 1) * P]
                            rhs = uT[:, c, part % 2 * 512:(part % 2 + 1) * 512]
                        last = nc.tensor.matmul(ps[:, u % 7, :], lhsT, rhs, start=(c == 0), stop=(c == DCH - 1))
                    last.then_inc(unit_full, 1)
                    u += 1
                if j == 0:
                    pe.wait_ge(small_in, 16 * (2 + B_CONV))
                    for t in range(TILES):
                        for c in range(DCH):
                            last = nc.tensor.matmul(dt_ps[:, t * B_HEADS:(t + 1) * B_HEADS], uT[:, c, t * P:(t + 1) * P], wdt[:, c, :],
                                                    start=(c == 0), stop=(c == DCH - 1))
                    last.then_inc(dt_full, 1)
                if j == 1:
                    pe.wait_ge(consts, 3)
                    pe.wait_ge(pre, 5)
                    nc.tensor.matmul(cs_ps, tab.tri[:], dtA[:], start=True, stop=True)
                    nc.tensor.matmul(csT_ps, dtA[:], tab.tri[:], start=True, stop=True)
                    nc.tensor.matmul(total_ps, ones[:], dtA[:], start=True, stop=True).then_inc(sums, 1)


def mixer_b_scan(nc, core, uT, z, xbc, tab, io):
    XH = B_WIDTH // P
    GH = B_HEADS // B_GROUPS
    with ExitStack() as ctx:
        ph = Phase(nc, ctx, "bs")
        xs = ph.sb("xs", [P, 2, XH + 2 * B_GROUPS, P])
        bcs = uT[:, 0:4, :].rearrange("p (b k) n -> p b (k n)", b=2)
        seg = uT[:, 4:8, :].rearrange("p (b k) (h l) -> p b (k h) l", b=2, l=P)
        xdt = ph.sb("xdt", [P, 2, B_WIDTH])
        xend = ph.sb("xend", [P, 2, B_WIDTH])
        skip = ph.sb("skip", [P, B_WIDTH])
        yo = ph.sb("yo", [P, B_WIDTH])
        yx = ph.sb("yx", [P, 2, B_WIDTH])
        bnat = ph.sb("bnat", [P, 2, B_GROUPS * P])
        cb = ph.sb("cb", [P, B_GROUPS * P])
        state = ph.sb("state", [P, B_WIDTH])
        (zeroed, xs_full, bcs0_in, bcs1_in, seg_full, decay, turned, b_full, cb_full, xdt_full, x_free, xend_full,
         off_full, yo_full, ysum_full, m_full, diag_full, state_add, faded, state_full, y_full, gated, held) = ph.sems(
            "zeroed xs_full bcs0_in bcs1_in seg_full decay turned b_full cb_full xdt_full x_free xend_full "
            "off_full yo_full ysum_full m_full diag_full state_add faded state_full y_full gated held")
        arrived = [bcs0_in, bcs1_in]
        block = ph.open_block()
        ps = core.ps
        x_ps = ps[:, 0:2, :].rearrange("p k n -> p (k n)")
        diag_ps = ps[:, 3:5, :].rearrange("p k n -> p (k n)")
        off_ps = ps[:, 5:7, :].rearrange("p k n -> p (k n)")
        b_ps = [ps[:, k, 0:B_GROUPS * P] for k in (2, 7)]
        cb_ps = [ps[:, k, B_GROUPS * P:2 * B_GROUPS * P] for k in (2, 7)]
        heads = lambda ap: ap.rearrange("p (h d) -> p h d", d=HD)
        per_head = lambda ap: ap.unsqueeze(2).broadcast_to([P, B_HEADS, HD])
        of_tile = lambda table, t: table[:, bass.ds(t * B_HEADS, B_HEADS)]

        @block.sync
        def _(sp):
            with sp.Fori(0, TILES // 2) as i:
                for b in range(2):
                    sp.wait_ge(seg_full, i * 2 + (b + 1))
                    src = tab.cs_rows[bass.ds((i * 2 + b) * B_HEADS, B_HEADS), :].rearrange("h l -> (h l)")
                    sp.dma_start(bcs[:, b, :], src.partition_broadcast(P)).then_inc(arrived[b], 16)

        @block.gpsimd
        def _(pool):
            def decay_to_end(t, par):
                pool.wait_ge(xdt_full, t + 1)
                nc.gpsimd.tensor_tensor(heads(xend[:, par, :]), heads(xdt[:, par, :]), per_head(of_tile(tab.to_end, t)),
                                        ALU.mult).then_inc(xend_full, 1)

            def begin():
                nc.gpsimd.memset(state[:], 0.0).then_inc(zeroed, 1)
                pool.wait_ge(zeroed, 1)
                pool.sem_inc(state_full, 1)
                decay_to_end(0, 0)

            def apply_gate(t, par):
                pool.wait_ge(y_full, t + 2)
                row = z[:, bass.ds(t, 1), :].rearrange("p o d -> p (o d)")
                nc.gpsimd.tensor_tensor(row, yx[:, par, :], row, ALU.mult).then_inc(gated, 1)

            def step(t, par, ahead, front):
                pool.wait_ge(off_full, t + 1)
                pool.wait_ge(state_full, t + 1)
                nc.gpsimd.tensor_tensor(heads(state[:]), heads(state[:]), per_head(of_tile(tab.whole, t)), ALU.mult).then_inc(faded, 1)
                if front:
                    decay_to_end(t + 1, 1 - par)
                if not isinstance(t, int) or t:
                    apply_gate(t - 1, 1 - par)
                if not front:
                    apply_gate(t, par)

            pipeline(pool, begin, step, irregular=1)

        @block.scalar
        def _(act):
            def copy_tile(t, par):
                nc.scalar.activation(xs[:, par], xbc[:, :, bass.ds(t * P + 3, P)], ACT.Copy).then_inc(xs_full, 1)

            def decays(t, par):
                act.wait_ge(arrived[par], t * 8 + (8 if par else 16))
                act.wait_ge(diag_full, t + 1)
                act.sem_inc(held, 1)
                for hd in range(B_HEADS):
                    last = nc.scalar.activation(seg[:, par, hd, :], bcs[:, par, hd * P:(hd + 1) * P], ACT.Relu,
                                                bias=tab.cs[:, bass.ds(t * B_HEADS + hd, 1)], scale=-1.0)
                last.then_inc(seg_full, 1)
                act.wait_ge(seg_full, t + 3)
                nc.scalar.activation(seg[:, par], seg[:, par], ACT.Exp, scale=-1.0).then_inc(decay, 1)

            def copy_b(t, par):
                act.wait_ge(turned, t + 1)
                act.wait_ge(state_add, t + 1)
                nc.scalar.activation(bnat[:, par, :], b_ps[par], ACT.Copy).then_inc(b_full, 1)

            def begin():
                act.sem_inc(seg_full, 2)
                act.sem_inc(diag_full, 2)
                act.sem_inc(state_add, 2)
                copy_tile(0, 0)
                copy_tile(1, 1)
                decays(0, 0)
                copy_b(0, 0)

            def step(t, par, ahead, front):
                if front:
                    decays(t + 1, 1 - par)
                    copy_b(t + 1, 1 - par)
                if ahead:
                    act.wait_ge(off_full, t + 1)
                    act.sem_inc(held, 1)
                    copy_tile(t + 2, par)

            pipeline(act, begin, step, irregular=1)

        @block.vector
        def _(dve):
            def read_x(t, par):
                dve.wait_ge(turned, t + 1)
                nc.vector.tensor_tensor(heads(xdt[:, par, :]), heads(x_ps), per_head(of_tile(tab.dt, t)), ALU.mult).then_inc(xdt_full, 1)
                nc.vector.tensor_tensor(heads(skip[:]), heads(x_ps), per_head(tab.rows[:, 2, :]), ALU.mult).then_inc(x_free, 1)

            def begin():
                dve.sem_inc(x_free, 1)
                dve.sem_inc(y_full, 1)
                dve.sem_inc(gated, 2)
                read_x(0, 0)

            def step(t, par, ahead, front):
                dve.wait_ge(off_full, t + 1)
                nc.vector.tensor_tensor(heads(yo[:]), heads(off_ps), per_head(of_tile(tab.from_start, t)), ALU.mult).then_inc(yo_full, 1)
                dve.wait_ge(b_full, t + 1)
                nc.vector.tensor_tensor(cb[:].rearrange("p (g l) -> p g l", l=P), cb_ps[par].rearrange("p (g l) -> p g l", l=P),
                                        tab.tri[:].unsqueeze(1).broadcast_to([P, B_GROUPS, P]), ALU.mult).then_inc(cb_full, 1)
                dve.wait_ge(decay, t + 1)
                dve.wait_ge(cb_full, t + 1)
                by_group = seg[:, par].rearrange("p (g h) l -> p g h l", g=B_GROUPS)
                nc.vector.tensor_tensor(by_group, by_group,
                                        cb[:].rearrange("p (g l) -> p g l", l=P).unsqueeze(2).broadcast_to([P, B_GROUPS, GH, P]),
                                        ALU.mult).then_inc(m_full, 1)
                dve.wait_ge(yo_full, t + 1)
                dve.wait_ge(x_free, t + 2)
                nc.vector.tensor_tensor(yo[:], skip[:], yo[:], ALU.add).then_inc(ysum_full, 1)
                if front:
                    dve.wait_ge(ysum_full, t + 1)
                    read_x(t + 1, 1 - par)
                dve.wait_ge(state_add, t + 3)
                dve.wait_ge(faded, t + 1)
                nc.vector.tensor_tensor(state[:], off_ps, state[:], ALU.add).then_inc(state_full, 1)
                dve.wait_ge(diag_full, t + 3)
                dve.wait_ge(ysum_full, t + 1)
                dve.wait_ge(gated, t + 1)
                nc.vector.tensor_tensor(yx[:, par, :], diag_ps, yo[:], ALU.add).then_inc(y_full, 1)
                dve.wait_ge(y_full, t + 2)
                dve.wait_ge(m_full, t + 1)

            pipeline(dve, begin, step, irregular=1)

        @block.tensor
        def _(pe):
            def turn(t, par):
                pe.wait_ge(xs_full, t + 1)
                pe.wait_ge(x_free, t + 1)
                for c in range(XH + B_GROUPS):
                    out = x_ps[:, c * P:(c + 1) * P] if c < XH else b_ps[par][:, (c - XH) * P:(c - XH + 1) * P]
                    nc.tensor.transpose(out, xs[:, par, c, :], core.ident[:])
                for g in range(B_GROUPS):
                    last = nc.tensor.matmul(cb_ps[par][:, g * P:(g + 1) * P], xs[:, par, XH + g, :],
                                            xs[:, par, XH + B_GROUPS + g, :], start=True, stop=True)
                last.then_inc(turned, 1)

            def begin():
                turn(0, 0)

            def step(t, par, ahead, front):
                pe.wait_ge(state_full, t + 1)
                for g in range(B_GROUPS):
                    last = nc.tensor.matmul(off_ps[:, g * 512:(g + 1) * 512], xs[:, par, XH + B_GROUPS + g, :],
                                            state[:, g * 512:(g + 1) * 512], start=True, stop=True)
                last.then_inc(off_full, 1)
                if front:
                    turn(t + 1, 1 - par)
                pe.wait_ge(xend_full, t + 1)
                pe.wait_ge(yo_full, t + 1)
                pe.wait_ge(b_full, t + 1)
                for g in range(B_GROUPS):
                    last = nc.tensor.matmul(off_ps[:, g * 512:(g + 1) * 512], bnat[:, par, g * P:(g + 1) * P],
                                            xend[:, par, g * 512:(g + 1) * 512], start=True, stop=True)
                last.then_inc(state_add, 1)
                pe.wait_ge(m_full, t + 1)
                pe.wait_ge(xdt_full, t + 1)
                pe.wait_ge(y_full, t + 1)
                for hd in range(B_HEADS):
                    last = nc.tensor.matmul(diag_ps[:, hd * HD:(hd + 1) * HD], seg[:, par, hd, :], xdt[:, par, hd * HD:(hd + 1) * HD],
                                            start=True, stop=True)
                last.then_inc(diag_full, 1)

            pipeline(pe, begin, step, irregular=1)


def mixer_b(nc, core, uT, z, stream, io):
    with ExitStack() as ctx:
        tab = ScanTables(nc, ctx)
        xbc = ctx.enter_context(nc.sbuf_tensor("b_xbc", [P, B_XBC // P, SEQ + B_CONV - 1], F32))
        mixer_b_project(nc, core, uT, z, xbc, tab, io)
        mixer_b_scan(nc, core, uT, z, xbc, tab, io)
    project_out(nc, core, "bout", z, B_WIDTH // P, io["b_out_norm"][0], io["w_out"][0, A_WIDTH:A_WIDTH + B_WIDTH, :],
                stream=stream, w_query=io["peer_w_query"][0])


def peer_and_gate(nc, core, hd, out, io):
    AHEAD = 5
    FIRST = 2
    RING = 4
    KK = PH * TOPK
    with ExitStack() as ctx:
        ph = Phase(nc, ctx, "peer")
        wg = ph.sb("wg", [P, DCH, D])
        wp = ph.sb("wp", [P, PLE // P, D])
        gain_row = ph.sb("gain_row", [P, D])
        gT = ph.sb("gT", [P, DCH])
        u_ring = ph.sb("u_ring", [P, RING, D])
        v_ring = ph.sb("v_ring", [P, RING, D])
        h_next = ph.sb("h_next", [P, D])
        h_sum = ph.sb("h_sum", [P, D])
        h_out = ph.sb("h_out", [P, D])
        un = ph.sb("un", [P, D])
        norm = ph.sb("norm", [P, D])
        uT = ph.sb("uT", [P, DCH, P])
        fT = ph.sb("fT", [P, DCH, P])
        gate = ph.sb("gate", [P, 512])
        ptok = ph.sb("ptok", [P, PLE])
        pT = ph.sb("pT", [P, PLE // P, P])
        q = ph.sb("q", [P, PKD])
        qT = ph.sb("qT", [P, PKD])
        top = ph.sb("top", [P, 2, TOPK])
        top_i = ph.sb("top_i", [P, 2, TOPK], U32)
        top_f = ph.sb("top_f", [P, 2, TOPK])
        rest = ph.sb("rest", [P, 2, PK])
        cand = ph.sb("cand", [P, TOPK, TOPK])
        cand2 = ph.sb("cand2", [P, TOPK * TOPK])
        best = ph.sb("best", [P, TOPK])
        best_i = ph.sb("best_i", [P, TOPK], U32)
        pair_i = ph.sb("pair_i", [P, 2, TOPK], U32)
        pair_f = ph.sb("pair_f", [P, 2 * TOPK])
        hot = ph.sb("hot", [P, 2 * TOPK, TOPK])
        halves = ph.sb("halves", [P, 2, TOPK])
        row_f = ph.sb("row_f", [P, TOPK])
        steps16 = ph.sb("steps16", [P, TOPK])
        idx_all = ph.sb("idx_all", [P, KK], U32)
        gates_all = ph.sb("gates_all", [P, KK])
        idx_u = ph.sb("idx_u", [P, 2, TOPK], U32)
        idx_v = ph.sb("idx_v", [P, 2, TOPK], U32)
        negbest = ph.sb("negbest", [P, 1])
        gexp = ph.sb("gexp", [P, TOPK])
        gsum = ph.sb("gsum", [P, 1])
        dots = ph.sb("dots", [P, 2, TOPK])
        weights = ph.sb("weights", [P, 2, TOPK])
        diag = ph.sb("diag", [P, RING, P])
        stat = ph.sb("stat", [P, 2])
        (held, small_in, wq1_in, wg_in, h_in, p_in,
         pre_sq, pre_root, pre_link, norm_full, pre_turned, uT_full,
         q_full, q_copied, qT_full, qT_copied, score_full, topk_link, idx_full, best_full, gexp_full, gates_full, gate_link, un_taken,
         u_free, v_free, iu_full, iv_full, gelu_full, weights_full, diag_full, sum_read,
         fin_sum, fin_sq, fin_root, fin_link, fin_turned, fin_copied, p_turned, p_copied,
         gate_full, gate_copied, ple_full, fin_mul, fin_done, stored, iota_done) = ph.sems(
            "held small_in wq1_in wg_in h_in p_in "
            "pre_sq pre_root pre_link norm_full pre_turned uT_full "
            "q_full q_copied qT_full qT_copied score_full topk_link idx_full best_full gexp_full gates_full gate_link un_taken "
            "u_free v_free iu_full iv_full gelu_full weights_full diag_full sum_read "
            "fin_sum fin_sq fin_root fin_link fin_turned fin_copied p_turned p_copied "
            "gate_full gate_copied ple_full fin_mul fin_done stored iota_done")
        u_in = [ph.sem(f"u{j}_in") for j in range(RING)]
        v_in = [ph.sem(f"v{j}_in") for j in range(RING)]
        ps, wq, skT = core.ps, core.wq, core.skT
        sum_ps = [ps[:, 2 * b:2 * b + 2, :].rearrange("p k n -> p (k n)") for b in range(2)]
        q_ps, qT_ps, score_ps, misc_ps = (ps[:, b, :] for b in range(4, 8))
        TK = 24
        block = ph.open_block()

        def schedule(eng, begin, group, finish_tail):
            def tile(t, first, last):
                g = t * PH
                two = lambda h: (FIRST + 2 * h, FIRST + 2 * h + 1) if first else None
                group(g, t, 0, v=not first, add=not first, topk=not first, two=two(0))
                group(g + 1, t, 1, v=True, add=not first, topk=not first, finish=not first, two=two(1))
                group(g + 2, t, 2, v=True, topk=not first, finish2=not first, prepare=not last, final_topk=last, two=two(2))
                with eng.Fori(0, 2) as k:
                    for b in range(2):
                        group(g + k * 2 + (3 + b), t, k * 2 + (3 + b), v=True, topk=not last, odd=1 - b)
                group(g + 7, t, 7, v=True, topk=not last, ple_first=last)
            begin()
            tile(0, True, False)
            with eng.Fori(1, TILES - 1) as t:
                tile(t, False, False)
            tile(TILES - 1, False, True)
            finish_tail(TILES * PH)

        @block.sync
        def _(sp):
            def load_tile(t):
                sp.dma_start(h_next[:], hd[bass.ds(t * P, P), :]).then_inc(h_in, 16)

            sp.dma_start(h_next[:], hd[0:P, :]).then_inc(h_in, 16)
            sp.dma_start(gain_row[:], io["ffn_norm"][0].partition_broadcast(P)).then_inc(small_in, 16)
            sp.dma_start(gT[:], io["ple_norm"][0].rearrange("(c p) -> p c", p=P), allow_slow_non_contiguous=True).then_inc(small_in, 16)
            sp.dma_start(wq[:, 1], io["peer_w_query"][0][:, PH // 2 * PKD:].rearrange("(c p) n -> p c n", p=P)).then_inc(wq1_in, 16)
            sp.dma_start(wg[:], io["ple_w_gate"][0].rearrange("(c p) n -> p c n", p=P)).then_inc(wg_in, 16)
            sp.dma_start(wp[:], io["ple_w_proj"][0].rearrange("(c p) n -> p c n", p=P)).then_inc(wg_in, 16)

            def fetch(t):
                sp.wait_ge(sum_read, t * PH + 3)
                sp.sem_inc(held, 1)
                sp.dma_start(h_next[:], hd[bass.ds((t + 1) * P, P), :]).then_inc(h_in, 16)

            def fetch_p(t):
                sp.wait_ge(p_copied, t + 1)
                sp.sem_inc(held, 1)
                sp.dma_start(ptok[:], io["p"][0, 0, bass.ds(t * P, P), :]).then_inc(p_in, 16)

            def store(t):
                sp.wait_ge(fin_done, t * 2 + 2)
                sp.sem_inc(held, 1)
                sp.dma_start(out[bass.ds(t * P, P), :], h_out[:]).then_inc(stored, 16)

            fetch(0)
            fetch_p(0)
            with sp.Fori(1, TILES - 1) as t:
                fetch(t)
                store(t - 1)
                fetch_p(t)
            store(TILES - 2)
            fetch_p(TILES - 1)
            for half in range(2):
                sp.wait_ge(fin_done, TILES * 2 - 1 + half)
                cols = slice(half * 512, (half + 1) * 512)
                sp.dma_start(out[(TILES - 1) * P:, cols], h_out[:, cols]).then_inc(stored, 16)
            sp.wait_ge(stored, 16 * (TILES + 1))

        @block.gpsimd
        def _(pool):
            def begin():
                pool.iota(steps16[:], pattern=[[1, TOPK]], base=0, channel_multiplier=0,
                          allow_small_or_imprecise_dtypes=True).then_inc(iota_done, 1)

            def gather(ring, s, table, idx, arrived):
                nc.gpsimd.indirect_dma_start(ring[:, s % RING, :], None, table,
                                             bass.IndirectOffsetOnAxis(ap=idx[:, s:s + 1], axis=0)).then_inc(arrived[s % RING], 16)

            def values(g, s, odd):
                if s == 0:
                    pool.wait_ge(iv_full, g + 1)
                pool.wait_ge(v_free, g * TOPK + (s + 1))
                pool.sem_inc(held, 1)
                gather(v_ring, s, io["peer_v"][0], idx_v[:, odd, :], v_in)

            def group(g, t, h, v=False, add=True, topk=False, finish=False, finish2=False, prepare=False, odd=None,
                      final_topk=False, two=None, ple_first=False):
                odd = h % 2 if odd is None else odd
                pool.wait_ge(iu_full, g + 1)
                for s in range(TOPK):
                    pool.wait_ge(u_free, g * TOPK + (s + 1))
                    pool.sem_inc(held, 1)
                    gather(u_ring, s, io["peer_u"][0], idx_u[:, odd, :], u_in)
                    if v:
                        values(g - 1, s, 1 - odd)

            def tail(g):
                for s in range(TOPK):
                    values(g - 1, s, 1)

            schedule(pool, begin, group, tail)

        @block.scalar
        def _(act):
            def square_and_root(src, at, squared, rooted, n):
                nc.scalar.activation(norm[:], src, ACT.Square, accum_out=stat[:, at:at + 1]).then_inc(squared, 1)
                act.wait_ge(squared, n + 1)
                nc.scalar.activation(stat[:, at:at + 1], stat[:, at:at + 1], ACT.Sqrt, bias=core.eps[:, 0:1],
                                     scale=1.0 / D).then_inc(rooted, 1)

            def prepare_root(t, begins=False):
                act.wait_ge(h_in, t * 16 + 16)
                if not begins:
                    act.wait_ge(fin_sq, t - 1)
                square_and_root(h_next[:], 0, pre_sq, pre_root, t)

            def prepare_copy(t):
                for half in range(2):
                    act.wait_ge(pre_turned, t * 2 + (half + 1))
                    nc.scalar.activation(uT[:, half * 4:half * 4 + 4, :], misc_ps.rearrange("p (c n) -> p c n", n=P),
                                         ACT.Copy).then_inc(uT_full, 1)

            def q_copy(k):
                act.wait_ge(q_full, k + 1)
                nc.scalar.activation(q[:], q_ps[:, 0:PKD], ACT.Copy).then_inc(q_copied, 1)

            def qT_copy(k):
                act.wait_ge(qT_full, k + 1)
                nc.scalar.activation(qT[:], qT_ps[:, 0:PKD], ACT.Copy).then_inc(qT_copied, 1)

            def gate_exp(k):
                act.wait_ge(best_full, k + 1)
                act.wait_ge(gates_full, k)
                nc.scalar.activation(gexp[:], best[:], ACT.Exp, bias=negbest[:, 0:1], accum_out=gsum[:, 0:1]).then_inc(gexp_full, 1)

            def begin():
                act.sem_inc(p_copied, 1)
                prepare_root(0, begins=True)
                prepare_copy(0)
                for k in range(FIRST):
                    q_copy(k)
                    qT_copy(k)
                    gate_exp(k)

            def diagonal(g, s, odd):
                if s == 0:
                    act.wait_ge(weights_full, g + 1)
                act.wait_ge(v_free, g * TOPK + (s + 1))
                nc.scalar.activation(diag[:, s % RING, :], core.ident[:], ACT.Copy,
                                     scale=weights[:, odd, s:s + 1]).then_inc(diag_full, 1)

            def p_copy(t):
                act.wait_ge(p_turned, t + 1)
                nc.scalar.activation(pT[:], misc_ps[:, 0:PLE].rearrange("p (c n) -> p c n", n=P), ACT.Copy).then_inc(p_copied, 1)

            def finish_root(t):
                act.wait_ge(fin_sum, t + 1)
                square_and_root(h_out[:], 1, fin_sq, fin_root, t)

            def gate_half(t, half, tail=False):
                act.wait_ge(gate_full, t * 2 + (half + 1))
                act.wait_ge(fin_link, t + 1)
                if half:
                    act.wait_ge(fin_done, t * 2 + half)
                nc.scalar.activation(gate[:], score_ps if tail and half else misc_ps, ACT.Sigmoid,
                                     scale=stat[:, 1:2]).then_inc(gate_copied, 1)

            def group(g, t, h, v=False, add=True, topk=False, finish=False, finish2=False, prepare=False, odd=None,
                      final_topk=False, two=None, ple_first=False):
                odd = h % 2 if odd is None else odd
                for s in range(TOPK):
                    if v:
                        diagonal(g - 1, s, 1 - odd)
                    if topk and s == 3:
                        q_copy(g + AHEAD)
                    if topk and s == 5:
                        qT_copy(g + AHEAD)
                    if two and s in (3, 8):
                        q_copy(two[s // 8])
                    if two and s in (5, 10):
                        qT_copy(two[s // 10])
                    if two and s == 11:
                        gate_exp(two[0])
                    if finish and s == 2:
                        p_copy(t - 1)
                        finish_root(t - 1)
                    if ple_first and s == 4:
                        p_copy(TILES - 1)
                    if (finish and s == 9) or (finish2 and s == 3):
                        gate_half(t - 1, 1 if finish2 else 0)
                    if prepare and s == 6:
                        prepare_root(t + 1)
                    if prepare and s == 13:
                        prepare_copy(t + 1)
                if topk:
                    gate_exp(g + AHEAD)
                if two:
                    gate_exp(two[1])
                act.wait_ge(u_free, g * TOPK + (TOPK + RING))
                nc.scalar.activation(dots[:, odd, :], dots[:, odd, :], ACT.Gelu).then_inc(gelu_full, 1)

            def tail(g):
                for s in range(TOPK):
                    diagonal(g - 1, s, 1)
                finish_root(TILES - 1)
                for half in range(2):
                    gate_half(TILES - 1, half, tail=True)

            schedule(act, begin, group, tail)

        @block.vector
        def _(dve):
            def retrieval(k, slot):
                chain = Chain(dve, topk_link, k * TK)

                def link(ins):
                    chain.link(ins)
                    dve.sem_inc(held, 1)

                def sixteen_best(vals, idx, src, scratch):
                    link(nc.vector.max(vals[:, 0:8], src))
                    link(nc.vector.max_index(idx[:, 0:8], vals[:, 0:8], src))
                    link(nc.vector.match_replace(scratch, vals[:, 0:8], src, -3e38))
                    link(nc.vector.max(vals[:, 8:16], scratch))
                    link(nc.vector.max_index(idx[:, 8:16], vals[:, 8:16], scratch))

                def keys(side):
                    def step():
                        if side == 0:
                            dve.wait_ge(score_full, k + 1)
                            dve.sem_inc(held, 1)
                        sixteen_best(top[:, side, :], top_i[:, side, :], score_ps[:, side * PK:(side + 1) * PK], rest[:, side, :])
                    return step

                def pairs():
                    chain.link(nc.vector.tensor_copy(top_f[:], top_i[:]))
                    chain.link(nc.vector.tensor_tensor(cand[:], top[:, 0, :].unsqueeze(2).broadcast_to([P, TOPK, TOPK]),
                                                       top[:, 1:2, :].broadcast_to([P, TOPK, TOPK]), ALU.add))

                def best_pairs():
                    dve.wait_ge(gexp_full, k)
                    dve.sem_inc(held, 1)
                    sixteen_best(best[:], best_i[:], cand[:].rearrange("p a b -> p (a b)"), cand2[:])

                def unpair():
                    chain.link(nc.vector.tensor_scalar(pair_i[:, 0, :], best_i[:], 4, None, ALU.logical_shift_right))
                    chain.link(nc.vector.tensor_scalar(pair_i[:, 1, :], best_i[:], 15, None, ALU.bitwise_and))
                    chain.link(nc.vector.tensor_copy(pair_f[:], pair_i[:].rearrange("p a b -> p (a b)")))
                    chain.link(nc.vector.tensor_tensor(hot[:], pair_f[:].unsqueeze(2).broadcast_to([P, 2 * TOPK, TOPK]),
                                                       steps16[:].unsqueeze(1).broadcast_to([P, 2 * TOPK, TOPK]), ALU.is_equal))
                    by_side = hot[:].rearrange("p (a s) b -> p a s b", a=2)
                    chain.link(nc.vector.tensor_tensor(by_side, by_side, top_f[:].unsqueeze(2).broadcast_to([P, 2, TOPK, TOPK]), ALU.mult))
                    chain.link(nc.vector.tensor_reduce(halves[:], by_side, axis=AX.X, op=ALU.add))

                def rows():
                    chain.link(nc.vector.scalar_tensor_tensor(row_f[:], halves[:, 0, :], float(PK), halves[:, 1, :], ALU.mult, ALU.add))
                    nc.vector.tensor_copy(idx_all[:, bass.ds(slot * TOPK, TOPK)], row_f[:]).then_inc(idx_full, 1)
                    assert chain.n == TK, chain.n
                    nc.vector.tensor_scalar(negbest[:], best[:, 0:1], -1.0, None, ALU.mult).then_inc(best_full, 1)

                return keys(0), keys(1), pairs, best_pairs, unpair, rows

            def gates(k, slot):
                dve.wait_ge(gexp_full, k + 1)
                nc.vector.reciprocal(gsum[:], gsum[:]).then_inc(gate_link, 1)
                dve.wait_ge(gate_link, k + 1)
                nc.vector.tensor_scalar(gates_all[:, bass.ds(slot * TOPK, TOPK)], gexp[:], gsum[:, 0:1], None,
                                        ALU.mult).then_inc(gates_full, 1)

            def rstd_of(at, rooted, link, n):
                dve.wait_ge(rooted, n + 1)
                nc.vector.reciprocal(stat[:, at:at + 1], stat[:, at:at + 1]).then_inc(link, 1)
                dve.wait_ge(link, n + 1)

            def prepare(t):
                rstd_of(0, pre_root, pre_link, t)
                nc.vector.scalar_tensor_tensor(norm[:], h_next[:], stat[:, 0:1], gain_row[:], ALU.mult, ALU.mult).then_inc(norm_full, 1)

            def copy_rows(dst, b, slot, full):
                nc.vector.tensor_copy(dst[:, b, :], idx_all[:, bass.ds(slot * TOPK, TOPK)]).then_inc(full, 1)

            def begin():
                dve.sem_inc(u_free, RING)
                dve.sem_inc(sum_read, 2)
                dve.wait_ge(small_in, 32)
                dve.wait_ge(iota_done, 1)
                prepare(0)
                for k in range(FIRST):
                    for step in retrieval(k, k):
                        step()
                    if k == 0:
                        dve.wait_ge(idx_full, 1)
                        copy_rows(idx_u, 0, 0, iu_full)
                        gates(0, 1)

            def weigh(g, slot, odd):
                dve.wait_ge(gelu_full, g + 1)
                dve.wait_ge(gates_full, g + 1)
                nc.vector.tensor_tensor(weights[:, odd, :], dots[:, odd, :], gates_all[:, bass.ds(slot * TOPK, TOPK)],
                                        ALU.mult).then_inc(weights_full, 1)

            def add_sum(g, h, odd):
                dve.wait_ge(v_free, g * TOPK + (TOPK + RING))
                dve.wait_ge(sum_read, g + 2)
                src, dst = (h_next, h_sum) if h == 2 else (h_sum, h_out) if h == 1 else (h_sum, h_sum)
                return nc.vector.tensor_tensor(dst[:], sum_ps[odd], src[:], ALU.add)

            def finish_sum(t, g, odd):
                dve.wait_ge(stored, t * 16)
                add_sum(g, 1, odd).then_inc(fin_sum, 1)
                dve.wait_ge(fin_sum, t + 1)
                dve.sem_inc(sum_read, 1)

            def finish_copy(t, half, tail=False):
                dve.wait_ge(fin_turned, t * 2 + (half + 1))
                src = score_ps if tail and half else misc_ps
                nc.vector.tensor_tensor(fT[:, half * 4:half * 4 + 4, :], src.rearrange("p (c n) -> p c n", n=P),
                                        gT[:, half * 4:half * 4 + 4].unsqueeze(2).broadcast_to([P, 4, P]), ALU.mult).then_inc(fin_copied, 1)

            def finish_half(t, half, tail=False):
                dve.wait_ge(ple_full, t * 2 + (half + 1))
                dve.wait_ge(gate_copied, t * 2 + (half + 1))
                src = misc_ps if not tail else qT_ps if half else q_ps
                nc.vector.tensor_tensor(gate[:], src, gate[:], ALU.mult).then_inc(fin_mul, 1)
                dve.wait_ge(fin_mul, t * 2 + (half + 1))
                part = h_out[:, half * 512:(half + 1) * 512]
                nc.vector.tensor_tensor(part, part, gate[:], ALU.add).then_inc(fin_done, 1)

            def group(g, t, h, v=False, add=True, topk=False, finish=False, finish2=False, prepare=False, odd=None,
                      final_topk=False, two=None, ple_first=False):
                runtime = odd is not None
                odd = h % 2 if odd is None else odd
                if topk:
                    ks = retrieval(g + AHEAD, (h + AHEAD) % PH if not runtime else h - 3)
                if not runtime and h == 0:
                    dve.wait_ge(u_free, g * TOPK + RING)
                    nc.vector.scalar_tensor_tensor(un[:], h_next[:], stat[:, 0:1], gain_row[:], ALU.mult, ALU.mult).then_inc(un_taken, 1)
                    dve.wait_ge(un_taken, t + 1)
                if two:
                    ks2 = [step for k in two for step in retrieval(k, k)]
                    at = [6, 7, 8, 9, 9, 10, 13, 13, 14, 14, 15, 15]
                for s in range(TOPK):
                    dve.wait_ge(u_in[s % RING], g * 64 + 16 * (s // RING + 1))
                    row = u_ring[:, s % RING, :]
                    nc.vector.tensor_tensor_reduce(out=row, in0=row, in1=un[:], scale=1.0, scalar=0.0, op0=ALU.mult, op1=ALU.add,
                                                   accum_out=dots[:, odd, s:s + 1]).then_inc(u_free, 1)
                    if s == 0 and v:
                        weigh(g - 1, h, 1 - odd)
                    if s == 1 and add:
                        if finish:
                            finish_sum(t - 1, g - 2, odd)
                        else:
                            add_sum(g - 2, h if not runtime else 3, odd).then_inc(sum_read, 1)
                    if s == 3:
                        copy_rows(idx_v, odd, h, iv_full)
                    if two and s == 5:
                        gates(two[0] - 1, two[0])
                    if two and s == 12:
                        gates(two[0], two[1])
                    if two:
                        for step, when in zip(ks2, at):
                            if when == s:
                                step()
                    if s == 4 and (topk or runtime or h < 7):
                        dve.wait_ge(idx_full, g + 2)
                        copy_rows(idx_u, 1 - odd, (h + 1) % PH if not runtime else h + 1, iu_full)
                    if topk and 7 <= s <= 12:
                        ks[s - 7]()
                    if topk and s == 5:
                        gates(g + AHEAD - 1, h - 3 if runtime else (h + AHEAD) % PH)
                    if final_topk and s == 15:
                        gates(g + AHEAD, (h + AHEAD + 1) % PH)
                    if finish and s == 4:
                        rstd_of(1, fin_root, fin_link, t - 1)
                    if finish and s in (6, 7):
                        finish_copy(t - 1, s - 6)
                    if (finish and s == 11) or (finish2 and s == 5):
                        finish_half(t - 1, 1 if finish2 else 0)
                    if prepare and s == 10:
                        prepare_dve(t + 1)

            def tail(g):
                weigh(g - 1, 0, 1)
                add_sum(g - 2, 0, 0).then_inc(sum_read, 1)
                finish_sum(TILES - 1, g - 1, 1)
                for half in range(2):
                    finish_copy(TILES - 1, half, tail=True)
                rstd_of(1, fin_root, fin_link, TILES - 1)
                for half in range(2):
                    finish_half(TILES - 1, half, tail=True)

            prepare_dve = prepare
            schedule(dve, begin, group, tail)

        @block.tensor
        def _(pe):
            def prepare(t, begins=False):
                if not begins:
                    pe.wait_ge(fin_mul, (t - 1) * 2)
                for half in range(2):
                    pe.wait_ge(norm_full, t + 1)
                    if half:
                        pe.wait_ge(uT_full, t * 2 + 1)
                    for c in range(4):
                        last = nc.tensor.transpose(misc_ps[:, c * P:(c + 1) * P], norm[:, (half * 4 + c) * P:(half * 4 + c + 1) * P],
                                                   core.ident[:])
                    last.then_inc(pre_turned, 1)

            def query(k, slot, t):
                pe.wait_ge(uT_full, t * 2 + 2)
                pe.wait_ge(q_copied, k)
                half, at = 0, slot
                if isinstance(slot, int):
                    half, at = divmod(slot, PH // 2)
                if half:
                    pe.wait_ge(wq1_in, 16)
                for c in range(DCH):
                    last = nc.tensor.matmul(q_ps[:, 0:PKD], uT[:, c, :], wq[:, half, c, bass.ds(at * PKD, PKD)],
                                            start=(c == 0), stop=(c == DCH - 1))
                last.then_inc(q_full, 1)

            def turn_query(k):
                pe.wait_ge(q_copied, k + 1)
                for side in range(2):
                    last = nc.tensor.transpose(qT_ps[:, side * P:(side + 1) * P], q[:, side * P:(side + 1) * P], core.ident[:])
                last.then_inc(qT_full, 1)

            def scores(k, slot):
                pe.wait_ge(qT_copied, k + 1)
                pe.wait_ge(idx_full, k)
                for side in range(2):
                    last = nc.tensor.matmul(score_ps[:, side * PK:(side + 1) * PK], qT[:, side * P:(side + 1) * P],
                                            skT[:, bass.ds(slot * 2 + side, 1), :].rearrange("p o k -> p (o k)"), start=True, stop=True)
                last.then_inc(score_full, 1)

            def begin():
                pe.sem_inc(v_free, RING)
                prepare(0, begins=True)
                pe.wait_ge(core.wq0_in, 16)
                for k in range(FIRST):
                    query(k, k, 0)
                    turn_query(k)
                    scores(k, k)

            def values(g, s, odd):
                if s == 0:
                    pe.wait_ge(sum_read, g + 1)
                pe.wait_ge(diag_full, g * TOPK + (s + 1))
                pe.wait_ge(v_in[s % RING], g * 64 + 16 * (s // RING + 1))
                for half in range(2):
                    last = nc.tensor.matmul(sum_ps[odd][:, half * 512:(half + 1) * 512], diag[:, s % RING, :],
                                            v_ring[:, s % RING, half * 512:(half + 1) * 512], start=(s == 0), stop=(s == TOPK - 1))
                last.then_inc(v_free, 1)

            def turn_p(t):
                pe.wait_ge(p_in, t * 16 + 16)
                pe.wait_ge(fin_mul, t * 2)
                for c in range(PLE // P):
                    last = nc.tensor.transpose(misc_ps[:, c * P:(c + 1) * P], ptok[:, c * P:(c + 1) * P], core.ident[:])
                last.then_inc(p_turned, 1)

            def finish_turn(t, half, tail=False):
                pe.wait_ge(fin_sum, t + 1)
                if not half:
                    pe.wait_ge(p_copied, t + 2)
                elif not tail:
                    pe.wait_ge(fin_copied, t * 2 + 1)
                dst = score_ps if tail and half else misc_ps
                for c in range(4):
                    last = nc.tensor.transpose(dst[:, c * P:(c + 1) * P], h_out[:, (half * 4 + c) * P:(half * 4 + c + 1) * P],
                                               core.ident[:])
                last.then_inc(fin_turned, 1)

            def gate_half(t, half, tail=False):
                pe.wait_ge(wg_in, 32)
                pe.wait_ge(fin_copied, t * 2 + 2)
                if half and not tail:
                    pe.wait_ge(fin_mul, t * 2 + 1)
                dst = score_ps if tail and half else misc_ps
                for c in range(DCH):
                    last = nc.tensor.matmul(dst, fT[:, c, :], wg[:, c, half * 512:(half + 1) * 512], start=(c == 0), stop=(c == DCH - 1))
                last.then_inc(gate_full, 1)

            def ple_half(t, half, tail=False):
                dst = misc_ps if not tail else qT_ps if half else q_ps
                if tail:
                    pe.wait_ge(p_copied, t + 2)
                else:
                    pe.wait_ge(gate_copied, t * 2 + (half + 1))
                for c in range(PLE // P):
                    last = nc.tensor.matmul(dst, pT[:, c, :], wp[:, c, half * 512:(half + 1) * 512], start=(c == 0), stop=(c == PLE // P - 1))
                last.then_inc(ple_full, 1)

            prepare_pe = prepare

            def group(g, t, h, v=False, add=True, topk=False, finish=False, finish2=False, prepare=False, odd=None,
                      final_topk=False, two=None, ple_first=False):
                runtime = odd is not None
                odd = h % 2 if odd is None else odd
                slot = (h + AHEAD) % PH if not runtime else h - 3
                late = runtime or h + AHEAD >= PH
                for s in range(TOPK):
                    if v:
                        values(g - 1, s, 1 - odd)
                    if two and s in (1, 6):
                        query(two[s // 6], two[s // 6], 0)
                    if two and s in (3, 8):
                        turn_query(two[s // 8])
                    if two and s in (5, 12):
                        scores(two[s // 12], two[s // 12])
                    if topk and s == 1:
                        query(g + AHEAD, slot, t + 1 if late else t)
                    if topk and s == 3:
                        turn_query(g + AHEAD)
                    if topk and s == 5:
                        scores(g + AHEAD, slot)
                    if finish and s == 0:
                        turn_p(t - 1)
                    if ple_first and s == 1:
                        turn_p(TILES - 1)
                    if ple_first and s in (7, 10):
                        ple_half(TILES - 1, s // 10, tail=True)
                    if finish and s in (5, 6):
                        finish_turn(t - 1, s - 5)
                    if (finish and s == 8) or (finish2 and s == 2):
                        gate_half(t - 1, 1 if finish2 else 0)
                    if (finish and s == 9) or (finish2 and s == 3):
                        ple_half(t - 1, 1 if finish2 else 0)
                    if prepare and s == 12:
                        prepare_pe(t + 1)

            def tail(g):
                for s in range(TOPK):
                    values(g - 1, s, 1)
                for half in range(2):
                    finish_turn(TILES - 1, half, tail=True)
                for half in range(2):
                    gate_half(TILES - 1, half, tail=True)

            schedule(pe, begin, group, tail)


def build(nc, io, out):
    stream = nc.dram_tensor("stream", (SEQ, D), F32, kind="Internal").ap()
    with ExitStack() as ctx:
        core = Core(nc, ctx)
        with ExitStack() as mixers:
            core.h = mixers.enter_context(nc.sbuf_tensor("h", [P, TILES, D], F32))
            uT = core.wq[:, 0]
            outputs = core.wq[:, 1].rearrange("p c n -> p (c n)")
            z = core.wq[:, 1]
            y = outputs[:, 0:TILES * A_WIDTH].rearrange("p (t n) -> p t n", t=TILES)
            spare = outputs[:, TILES * A_WIDTH:]
            normalise_input(nc, core, uT, io["x"][0], io["mix_norm"][0], io["peer_sub_keys"][0])
            mixer_a(nc, core, uT, y, spare, io)
            mixer_c(nc, core, uT, y, spare, io)
            mixer_b(nc, core, uT, z, stream, io)
        peer_and_gate(nc, core, stream, out[0], io)


_INS = ["x", "p", "mix_norm", "w_in", "a_q_norm", "a_k_norm", "a_sinks", "a_out_norm", "b_conv_w", "b_conv_b", "b_dt_bias",
        "b_a_log", "b_d", "b_out_norm", "c_q_norm", "c_k_norm", "c_rel_bias", "c_out_norm", "w_out", "ffn_norm",
        "peer_w_query", "peer_sub_keys", "peer_u", "peer_v", "ple_norm", "ple_w_gate", "ple_w_proj"]


def kernel(**inputs):
    import concourse.bacc as bacc
    from concourse.bass_utils import run_bass_kernel_spmd

    nc = bacc.Bacc("TRN2", target_bir_lowering=False, num_devices=1)
    arrays = {name: np.ascontiguousarray(inputs[name]) for name in _INS}
    io = {name: nc.dram_tensor(name, a.shape, mybir.dt.from_np(a.dtype), kind="ExternalInput").ap() for name, a in arrays.items()}
    out = nc.dram_tensor("out", (1, SEQ, D), F32, kind="ExternalOutput").ap()
    build(nc, io, out)
    r = run_bass_kernel_spmd(nc, [arrays], core_ids=[0])
    return r.results[0]["out"]
```
